# Optimizing a Trainium2 kernel written in Bass

```python
import math
import jax, jax.numpy as jnp
from jax import lax
import numpy as np

D_MODEL = 1024
BATCH = 1
SEQ = 512
DEPTH = 1

MEM_LEN = 256
ROPE_THETA = 500000.0
EPS = 1e-6
NEG = -1e30
Q_BLOCK = 128
N_BRANCH = 3
BRANCH_WIDTH = 512
A_HEADS = 8
A_HEAD_DIM = 64
A_ROT = A_HEAD_DIM // 4
IDX_HEADS = 8
IDX_DIM = 64
IDX_ROT = IDX_DIM // 4
TOPK_MAX = 256
B_HEADS = 8
B_NOPE = 64
B_ROPE = 32
B_VDIM = 64
B_QK = B_NOPE + B_ROPE
B_Q_RANK = 384
B_KV_RANK = 256
M_HEADS = 4
M_HEAD_DIM = 128

SPLITS = (
    A_HEADS * A_HEAD_DIM,
    A_HEADS * A_HEAD_DIM,
    A_HEADS * A_HEAD_DIM,
    IDX_HEADS * IDX_DIM,
    IDX_DIM,
    IDX_HEADS,
    BRANCH_WIDTH,
    B_Q_RANK,
    B_KV_RANK,
    B_ROPE,
    BRANCH_WIDTH,
    M_HEADS * M_HEAD_DIM,
    BRANCH_WIDTH,
    N_BRANCH * D_MODEL,
)
D_IN = (4 * A_HEADS * A_HEAD_DIM + IDX_DIM + IDX_HEADS + BRANCH_WIDTH
        + B_Q_RANK + B_KV_RANK + B_ROPE + BRANCH_WIDTH
        + M_HEADS * M_HEAD_DIM + BRANCH_WIDTH + N_BRANCH * D_MODEL)


def rms_norm(x, g):
    xf = x.astype(jnp.float32)
    y = xf * lax.rsqrt(jnp.mean(xf * xf, axis=-1, keepdims=True) + EPS)
    return (y * g.astype(jnp.float32)).astype(x.dtype)

def rope_tables(positions, rot_dim):
    inv_freq = ROPE_THETA ** (-(jnp.arange(0, rot_dim, 2, dtype=jnp.float32) / rot_dim))
    ang = positions.astype(jnp.float32)[..., None] * inv_freq
    return jnp.cos(ang), jnp.sin(ang)

def rotate(x, cos, sin):
    half = x.shape[-1] // 2
    x1 = x[..., :half].astype(jnp.float32)
    x2 = x[..., half:].astype(jnp.float32)
    return jnp.concatenate([x1 * cos - x2 * sin, x2 * cos + x1 * sin], axis=-1).astype(x.dtype)

def partial_rope(x, cos, sin):
    rd = 2 * cos.shape[-1]
    return jnp.concatenate([rotate(x[..., :rd], cos, sin), x[..., rd:]], axis=-1)

def to_blocks(t, nb):
    b = t.shape[0]
    return jnp.moveaxis(t.reshape((b, nb, Q_BLOCK) + t.shape[2:]), 1, 0)

def from_blocks(t):
    t = jnp.moveaxis(t, 0, 1)
    return t.reshape((t.shape[0], t.shape[1] * t.shape[2]) + t.shape[3:])

def dsa_attention(q, k, v, qi, ki, wi):
    b, s, h, d = q.shape
    nb = s // Q_BLOCK
    topk = min(TOPK_MAX, s // 4)
    key_pos = jnp.arange(s)
    ki_f = ki.astype(jnp.float32)
    scale = d ** -0.5

    def one_block(args):
        qb, qib, wib, start = args
        q_pos = start + jnp.arange(Q_BLOCK)
        causal = key_pos[None, :] <= q_pos[:, None]
        dots = jnp.einsum('bqhc,bsc->bhqs', qib.astype(jnp.float32), ki_f) * (IDX_DIM ** -0.5)
        index = jnp.einsum('bhqs,bqh->bqs', jax.nn.relu(dots),
                           wib.astype(jnp.float32) * (IDX_HEADS ** -0.5))
        index = jnp.where(causal[None], index, NEG)
        _, idx = lax.top_k(index, topk)
        valid = idx <= q_pos[None, :, None]
        k_sel = jax.vmap(lambda kb, ib: kb[ib])(k, idx)
        v_sel = jax.vmap(lambda vb, ib: vb[ib])(v, idx)
        sc = jnp.einsum('bqhd,bqkhd->bhqk', qb, k_sel).astype(jnp.float32) * scale
        sc = jnp.where(valid[:, None], sc, NEG)
        p = jax.nn.softmax(sc, axis=-1).astype(v.dtype)
        return jnp.einsum('bhqk,bqkhd->bqhd', p, v_sel)

    starts = jnp.arange(nb) * Q_BLOCK
    out = lax.map(one_block, (to_blocks(q, nb), to_blocks(qi, nb), to_blocks(wi, nb), starts))
    return from_blocks(out)

def causal_attention(q, k, v):
    b, s, h, dq = q.shape
    nb = s // Q_BLOCK
    key_pos = jnp.arange(s)
    scale = dq ** -0.5

    def one_block(args):
        qb, start = args
        q_pos = start + jnp.arange(Q_BLOCK)
        sc = jnp.einsum('bqhd,bkhd->bhqk', qb, k).astype(jnp.float32) * scale
        sc = jnp.where((key_pos[None, :] <= q_pos[:, None])[None, None], sc, NEG)
        p = jax.nn.softmax(sc, axis=-1).astype(v.dtype)
        return jnp.einsum('bhqk,bkhd->bqhd', p, v)

    starts = jnp.arange(nb) * Q_BLOCK
    return from_blocks(lax.map(one_block, (to_blocks(q, nb), starts)))

def first_inputs(seed: int = 0) -> dict:
    key = jax.random.key(seed)
    ks = jax.random.split(key, 24)
    f32 = jnp.float32

    def w(k, shape, fan_in):
        return jax.random.normal(k, shape, f32) * (fan_in ** -0.5)

    def gain(k, shape):
        return 1.0 + 0.02 * jax.random.normal(k, shape, f32)

    x = jax.random.normal(ks[0], (BATCH, SEQ, D_MODEL), f32)
    mem = jax.random.normal(ks[1], (BATCH, MEM_LEN, D_MODEL), f32)
    offsets = jax.random.randint(ks[2], (BATCH, 1), 0, 4096, dtype=jnp.int32)
    positions = offsets + jnp.arange(SEQ, dtype=jnp.int32)[None, :]
    return {
        "x": x,
        "mem": mem,
        "positions": positions,
        "g_norm": gain(ks[3], (DEPTH, D_MODEL)),
        "w_in": w(ks[4], (DEPTH, D_MODEL, D_IN), D_MODEL),
        "g_qn_a": gain(ks[5], (DEPTH, A_HEAD_DIM)),
        "g_kn_a": gain(ks[6], (DEPTH, A_HEAD_DIM)),
        "g_cq": gain(ks[7], (DEPTH, B_Q_RANK)),
        "g_ckv": gain(ks[8], (DEPTH, B_KV_RANK)),
        "w_uq": w(ks[9], (DEPTH, B_Q_RANK, B_HEADS * B_QK), B_Q_RANK),
        "w_ukv": w(ks[10], (DEPTH, B_KV_RANK, B_HEADS * (B_NOPE + B_VDIM)), B_KV_RANK),
        "g_qn_b": gain(ks[11], (DEPTH, B_QK)),
        "g_kn_b": gain(ks[12], (DEPTH, B_QK)),
        "g_mem": gain(ks[13], (DEPTH, D_MODEL)),
        "w_mem_kv": w(ks[14], (DEPTH, D_MODEL, 2 * M_HEADS * M_HEAD_DIM), D_MODEL),
        "g_qn_m": gain(ks[15], (DEPTH, M_HEAD_DIM)),
        "g_kn_m": gain(ks[16], (DEPTH, M_HEAD_DIM)),
        "w_branch": w(ks[17], (DEPTH, N_BRANCH, BRANCH_WIDTH, D_MODEL), BRANCH_WIDTH),
        "w_out": w(ks[18], (DEPTH, D_MODEL, D_MODEL), D_MODEL),
    }

def first_block(x, mem, positions, g_norm, w_in, g_qn_a, g_kn_a, g_cq, g_ckv, w_uq, w_ukv,
              g_qn_b, g_kn_b, g_mem, w_mem_kv, g_qn_m, g_kn_m, w_branch, w_out):
    b, s, _ = x.shape
    m_len = mem.shape[1]
    cos_a, sin_a = rope_tables(positions, A_ROT)
    cos_b, sin_b = rope_tables(positions, B_ROPE)
    split_at = [int(o) for o in np.cumsum(SPLITS)[:-1]]

    for layer in range(DEPTH):
        h = rms_norm(x, g_norm[layer])
        proj = h @ w_in[layer]
        (q_a, k_a, v_a, q_i, k_i, w_i, z_a, c_q, c_kv, k_rope, z_b, q_m, z_m,
         gate_logits) = jnp.split(proj, split_at, axis=-1)

        q_a = partial_rope(rms_norm(q_a.reshape(b, s, A_HEADS, A_HEAD_DIM), g_qn_a[layer]),
                           cos_a[:, :, None], sin_a[:, :, None])
        k_a = partial_rope(rms_norm(k_a.reshape(b, s, A_HEADS, A_HEAD_DIM), g_kn_a[layer]),
                           cos_a[:, :, None], sin_a[:, :, None])
        v_a = v_a.reshape(b, s, A_HEADS, A_HEAD_DIM)
        q_i = partial_rope(q_i.reshape(b, s, IDX_HEADS, IDX_DIM), cos_a[:, :, None], sin_a[:, :, None])
        k_i = partial_rope(k_i, cos_a, sin_a)
        o_a = dsa_attention(q_a, k_a, v_a, q_i, k_i, w_i)

        q_b = (rms_norm(c_q, g_cq[layer]) @ w_uq[layer]).reshape(b, s, B_HEADS, B_QK)
        kv_b = (rms_norm(c_kv, g_ckv[layer]) @ w_ukv[layer]).reshape(b, s, B_HEADS, B_NOPE + B_VDIM)
        k_nope, v_b = kv_b[..., :B_NOPE], kv_b[..., B_NOPE:]
        k_b = jnp.concatenate(
            [k_nope, jnp.broadcast_to(k_rope[:, :, None, :], (b, s, B_HEADS, B_ROPE))], axis=-1)
        q_b = rms_norm(q_b, g_qn_b[layer])
        k_b = rms_norm(k_b, g_kn_b[layer])
        q_b = jnp.concatenate(
            [q_b[..., :B_NOPE], rotate(q_b[..., B_NOPE:], cos_b[:, :, None], sin_b[:, :, None])], axis=-1)
        k_b = jnp.concatenate(
            [k_b[..., :B_NOPE], rotate(k_b[..., B_NOPE:], cos_b[:, :, None], sin_b[:, :, None])], axis=-1)
        o_b = causal_attention(q_b, k_b, v_b)

        kv_m = (rms_norm(mem, g_mem[layer]) @ w_mem_kv[layer]).reshape(b, m_len, 2, M_HEADS, M_HEAD_DIM)
        k_m = rms_norm(kv_m[:, :, 0], g_kn_m[layer])
        v_m = kv_m[:, :, 1]
        q_m = rms_norm(q_m.reshape(b, s, M_HEADS, M_HEAD_DIM), g_qn_m[layer])
        sc_m = jnp.einsum('bqhd,bmhd->bhqm', q_m, k_m).astype(jnp.float32) * (M_HEAD_DIM ** -0.5)
        p_m = jax.nn.softmax(sc_m, axis=-1).astype(v_m.dtype)
        o_m = jnp.einsum('bhqm,bmhd->bqhd', p_m, v_m)

        ys = jnp.stack([
            o_a.reshape(b, s, BRANCH_WIDTH) * jax.nn.silu(z_a),
            o_b.reshape(b, s, BRANCH_WIDTH) * jax.nn.silu(z_b),
            o_m.reshape(b, s, BRANCH_WIDTH) * jax.nn.silu(z_m),
        ], axis=0)
        branch = jnp.einsum('nbsw,nwd->nbsd', ys, w_branch[layer])
        gates = jax.nn.sigmoid(
            gate_logits.reshape(b, s, N_BRANCH, D_MODEL).astype(jnp.float32)).astype(x.dtype)
        merged = jnp.einsum('bsnd,nbsd->bsd', gates, branch)
        x = x + merged @ w_out[layer]
    return x


POOL_WINDOWS = (2, 4, 8, 16)
POOL_GROUPS = len(POOL_WINDOWS)
POOL_WIDTH = D_MODEL // 2
POOL_GW = POOL_WIDTH // POOL_GROUPS
N_HEADS = 16
HEAD_DIM = 64
N_KV_GROUPS = 2
HPG = N_HEADS // N_KV_GROUPS
NSA_WIDTH = N_HEADS * HEAD_DIM
KV_WIDTH = N_KV_GROUPS * HEAD_DIM
CMP_LEN = 32
CMP_STRIDE = 16
CMP_HIDDEN = 256
SEL_BLOCK = 64
N_SEL = 16
WINDOW = 512
Q_BLOCK_2 = 64
SEL_BONUS = 1e4
NEG_INF = -1e30
ROPE_THETA_2 = 10000.0
D_FF = 4 * D_MODEL
RMS_EPS = 1e-6
IN_SIZES = (POOL_WIDTH, NSA_WIDTH, KV_WIDTH, KV_WIDTH, KV_WIDTH, KV_WIDTH, KV_WIDTH, KV_WIDTH, 3 * N_HEADS, 2 * D_MODEL)
N_IN = sum(IN_SIZES)
IN_SPLITS = tuple(int(v) for v in np.cumsum(IN_SIZES)[:-1])


def rms_norm_2(x, g):
    xf = x.astype(jnp.float32)
    y = xf * lax.rsqrt(jnp.mean(xf * xf, axis=-1, keepdims=True) + RMS_EPS)
    return (y * g.astype(jnp.float32)).astype(x.dtype)

def rope_tables_2(pos):
    inv = ROPE_THETA_2 ** (-jnp.arange(0, HEAD_DIM, 2, dtype=jnp.float32) / HEAD_DIM)
    ang = pos.astype(jnp.float32)[:, None] * inv[None, :]
    ang = jnp.concatenate([ang, ang], axis=-1)
    return jnp.cos(ang), jnp.sin(ang)

def apply_rope(x, cos, sin):
    x1, x2 = jnp.split(x, 2, axis=-1)
    rot = jnp.concatenate([-x2, x1], axis=-1)
    y = x.astype(jnp.float32) * cos[:, None, :] + rot.astype(jnp.float32) * sin[:, None, :]
    return y.astype(x.dtype)

def masked_softmax(s, mask):
    s = jnp.where(mask, s.astype(jnp.float32), NEG_INF)
    return jnp.where(mask, jax.nn.softmax(s, axis=-1), 0.0)

def pool_mixer(u, w_pool, pool_scale):
    B, S, _ = u.shape
    uf = u.astype(jnp.float32)
    csum = jnp.pad(jnp.cumsum(uf, axis=1), ((0, 0), (1, 0), (0, 0)))
    t = jnp.arange(S)
    diffs = []
    for g, w in enumerate(POOL_WINDOWS):
        c = csum[:, :, g * POOL_GW:(g + 1) * POOL_GW]
        upper = c[:, 1:]
        lower = jnp.pad(c, ((0, 0), (w - 1, 0), (0, 0)))[:, :S]
        count = jnp.minimum(t + 1, w).astype(jnp.float32)[None, :, None]
        diffs.append((upper - lower) / count - uf[:, :, g * POOL_GW:(g + 1) * POOL_GW])
    d = jnp.stack(diffs, axis=2)
    y = jnp.einsum('bsgc,gcd->bsgd', d, w_pool.astype(jnp.float32)).reshape(B, S, POOL_WIDTH)
    return (y * pool_scale.astype(jnp.float32)).astype(u.dtype)

def compress(k, pe, w1, w2):
    B, S, G, dh = k.shape
    r = CMP_LEN // CMP_STRIDE
    n_chunks = S // CMP_STRIDE
    n_cmp = n_chunks - r + 1
    ch = k.reshape(B, n_chunks, CMP_STRIDE, G, dh)
    blocks = jnp.concatenate([ch[:, j:j + n_cmp] for j in range(r)], axis=2)
    blocks = blocks + pe[None, None, :, None, :]
    flat = blocks.transpose(0, 1, 3, 2, 4).reshape(B, n_cmp, G, CMP_LEN * dh)
    return jax.nn.gelu(flat @ w1) @ w2

def nsa_mixer(q, kc, vc, ks, vs, kw, vw, g_nsa, pe_k, pe_v, w_ck1, w_ck2, w_cv1, w_cv2):
    B, S = q.shape[:2]
    G, dh = N_KV_GROUPS, HEAD_DIM
    cos, sin = rope_tables_2(jnp.arange(S))
    q = apply_rope(q.reshape(B, S, N_HEADS, dh), cos, sin).reshape(B, S, G, HPG, dh)
    ks = apply_rope(ks.reshape(B, S, G, dh), cos, sin)
    kw = apply_rope(kw.reshape(B, S, G, dh), cos, sin)
    vs = vs.reshape(B, S, G, dh)
    vw = vw.reshape(B, S, G, dh)
    k_cmp = compress(kc.reshape(B, S, G, dh), pe_k, w_ck1, w_ck2)
    v_cmp = compress(vc.reshape(B, S, G, dh), pe_v, w_cv1, w_cv2)
    n_cmp = k_cmp.shape[1]
    cmp_start = jnp.arange(n_cmp) * CMP_STRIDE
    cmp_end = cmp_start + CMP_LEN - 1
    ccos, csin = rope_tables_2(cmp_end)
    k_cmp = apply_rope(k_cmp, ccos, csin)
    n_slc = S // SEL_BLOCK
    k_blk = ks.reshape(B, n_slc, SEL_BLOCK, G, dh).transpose(0, 3, 1, 2, 4)
    v_blk = vs.reshape(B, n_slc, SEL_BLOCK, G, dh).transpose(0, 3, 1, 2, 4)
    slc_start = jnp.arange(n_slc) * SEL_BLOCK
    slc_idx = jnp.arange(n_slc)
    overlap = ((cmp_start[:, None] <= slc_start[None, :] + SEL_BLOCK - 1)
               & (cmp_end[:, None] >= slc_start[None, :])).astype(jnp.float32)
    n_pick = min(N_SEL, n_slc)
    gather_blocks = jax.vmap(jax.vmap(lambda kb, i: kb[i]))
    win_len = Q_BLOCK_2 + WINDOW - 1
    kw_pad = jnp.pad(kw, ((0, 0), (WINDOW - 1, 0), (0, 0), (0, 0)))
    vw_pad = jnp.pad(vw, ((0, 0), (WINDOW - 1, 0), (0, 0), (0, 0)))
    scale = HEAD_DIM ** -0.5
    gates = jax.nn.sigmoid(g_nsa.astype(jnp.float32)).reshape(B, S, G, HPG, 3)

    def block(s0):
        t = s0 + jnp.arange(Q_BLOCK_2)
        qb = lax.dynamic_slice_in_dim(q, s0, Q_BLOCK_2, axis=1)
        gb = lax.dynamic_slice_in_dim(gates, s0, Q_BLOCK_2, axis=1)
        s_c = jnp.einsum('bqghd,bngd->bghqn', qb, k_cmp) * scale
        p_c = masked_softmax(s_c, cmp_end[None, :] <= t[:, None])
        o_c = jnp.einsum('bghqn,bngd->bqghd', p_c, v_cmp)
        imp = jnp.einsum('bghqn,nj->bgqj', p_c, overlap)
        causal = slc_start[None, :] <= t[:, None]
        cur = t // SEL_BLOCK
        forced = causal & ((slc_idx[None, :] == 0) | (slc_idx[None, :] >= cur[:, None] - 1))
        score = jnp.where(forced, SEL_BONUS, jnp.where(causal, imp, NEG_INF))
        top_v, idx = lax.top_k(score, n_pick)
        sel_ok = top_v > 0.5 * NEG_INF
        idx_flat = idx.reshape(B, G, Q_BLOCK_2 * n_pick)
        k_sel = gather_blocks(k_blk, idx_flat).reshape(B, G, Q_BLOCK_2, n_pick * SEL_BLOCK, dh)
        v_sel = gather_blocks(v_blk, idx_flat).reshape(B, G, Q_BLOCK_2, n_pick * SEL_BLOCK, dh)
        key_pos = idx[..., None] * SEL_BLOCK + jnp.arange(SEL_BLOCK)
        ok = (sel_ok[..., None] & (key_pos <= t[:, None, None])).reshape(B, G, Q_BLOCK_2, n_pick * SEL_BLOCK)
        s_s = jnp.einsum('bqghd,bgqkd->bghqk', qb, k_sel) * scale
        p_s = masked_softmax(s_s, ok[:, :, None])
        o_s = jnp.einsum('bghqk,bgqkd->bqghd', p_s, v_sel)
        kwb = lax.dynamic_slice_in_dim(kw_pad, s0, win_len, axis=1)
        vwb = lax.dynamic_slice_in_dim(vw_pad, s0, win_len, axis=1)
        kpos = s0 - (WINDOW - 1) + jnp.arange(win_len)
        wmask = (kpos[None, :] <= t[:, None]) & (kpos[None, :] > t[:, None] - WINDOW) & (kpos[None, :] >= 0)
        s_w = jnp.einsum('bqghd,bkgd->bghqk', qb, kwb) * scale
        p_w = masked_softmax(s_w, wmask)
        o_w = jnp.einsum('bghqk,bkgd->bqghd', p_w, vwb)
        o = gb[..., 0:1] * o_c + gb[..., 1:2] * o_s + gb[..., 2:3] * o_w
        return o.reshape(B, Q_BLOCK_2, NSA_WIDTH)

    out = lax.map(block, jnp.arange(S // Q_BLOCK_2) * Q_BLOCK_2)
    return out.transpose(1, 0, 2, 3).reshape(B, S, NSA_WIDTH)

def second_inputs(seed: int = 0) -> dict:
    key = jax.random.key(seed)
    ks = jax.random.split(key, 20)
    f32 = jnp.float32

    def nrm(k, shape, fan_in):
        return jax.random.normal(k, shape, f32) * (fan_in ** -0.5)

    return {
        'x': jax.random.normal(ks[0], (BATCH, SEQ, D_MODEL), f32),
        'norm_mix': 1.0 + 0.05 * jax.random.normal(ks[1], (DEPTH, D_MODEL), f32),
        'w_in': nrm(ks[2], (DEPTH, D_MODEL, N_IN), D_MODEL),
        'w_pool': nrm(ks[3], (DEPTH, POOL_GROUPS, POOL_GW, POOL_GW), POOL_GW),
        'pool_scale': 1.0 + 0.1 * jax.random.normal(ks[4], (DEPTH, POOL_WIDTH), f32),
        'pe_k': 0.1 * jax.random.normal(ks[5], (DEPTH, CMP_LEN, HEAD_DIM), f32),
        'pe_v': 0.1 * jax.random.normal(ks[6], (DEPTH, CMP_LEN, HEAD_DIM), f32),
        'w_ck1': nrm(ks[7], (DEPTH, CMP_LEN * HEAD_DIM, CMP_HIDDEN), CMP_LEN * HEAD_DIM),
        'w_ck2': nrm(ks[8], (DEPTH, CMP_HIDDEN, HEAD_DIM), CMP_HIDDEN),
        'w_cv1': nrm(ks[9], (DEPTH, CMP_LEN * HEAD_DIM, CMP_HIDDEN), CMP_LEN * HEAD_DIM),
        'w_cv2': nrm(ks[10], (DEPTH, CMP_HIDDEN, HEAD_DIM), CMP_HIDDEN),
        'w_proj_pool': nrm(ks[11], (DEPTH, POOL_WIDTH, D_MODEL), POOL_WIDTH),
        'w_proj_nsa': nrm(ks[12], (DEPTH, NSA_WIDTH, D_MODEL), NSA_WIDTH),
        'w_out': nrm(ks[13], (DEPTH, D_MODEL, D_MODEL), D_MODEL),
        'norm_mlp': 1.0 + 0.05 * jax.random.normal(ks[14], (DEPTH, D_MODEL), f32),
        'w_ff1': nrm(ks[15], (DEPTH, D_MODEL, D_FF), D_MODEL),
        'w_ff2': nrm(ks[16], (DEPTH, D_FF, D_MODEL), D_FF),
        'norm_final': 1.0 + 0.05 * jax.random.normal(ks[17], (D_MODEL,), f32),
    }

def second_block(x, norm_mix, w_in, w_pool, pool_scale, pe_k, pe_v, w_ck1, w_ck2, w_cv1, w_cv2,
              w_proj_pool, w_proj_nsa, w_out, norm_mlp, w_ff1, w_ff2, norm_final):
    for l in range(DEPTH):
        h = rms_norm_2(x, norm_mix[l])
        proj = h @ w_in[l]
        u, q, kc, vc, ksl, vsl, kwn, vwn, g_nsa, g_merge = jnp.split(proj, IN_SPLITS, axis=-1)
        y_pool = pool_mixer(u, w_pool[l], pool_scale[l])
        y_nsa = nsa_mixer(q, kc, vc, ksl, vsl, kwn, vwn, g_nsa, pe_k[l], pe_v[l],
                          w_ck1[l], w_ck2[l], w_cv1[l], w_cv2[l]).astype(x.dtype)
        g_a, g_b = jnp.split(jax.nn.sigmoid(g_merge.astype(jnp.float32)).astype(x.dtype), 2, axis=-1)
        merged = g_a * (y_pool @ w_proj_pool[l]) + g_b * (y_nsa @ w_proj_nsa[l])
        x = x + merged @ w_out[l]
        h = rms_norm_2(x, norm_mlp[l])
        x = x + jnp.square(jax.nn.relu(h @ w_ff1[l])) @ w_ff2[l]
    return rms_norm_2(x, norm_final)


def setup_inputs(seed=0):
    out = dict(first_inputs(seed))
    for name, value in second_inputs(seed + 1).items():
        if name != "x":
            out[name + "_2"] = value
    return out


def reference(
    x, mem, positions, g_norm, w_in, g_qn_a, g_kn_a, g_cq, g_ckv, w_uq, w_ukv, g_qn_b, g_kn_b,
    g_mem, w_mem_kv, g_qn_m, g_kn_m, w_branch, w_out, norm_mix_2, w_in_2, w_pool_2,
    pool_scale_2, pe_k_2, pe_v_2, w_ck1_2, w_ck2_2, w_cv1_2, w_cv2_2, w_proj_pool_2,
    w_proj_nsa_2, w_out_2, norm_mlp_2, w_ff1_2, w_ff2_2, norm_final_2,
):
    x = first_block(
        x, mem, positions, g_norm, w_in, g_qn_a, g_kn_a, g_cq, g_ckv, w_uq, w_ukv, g_qn_b,
        g_kn_b, g_mem, w_mem_kv, g_qn_m, g_kn_m, w_branch, w_out,
    )
    return second_block(
        x, norm_mix_2, w_in_2, w_pool_2, pool_scale_2, pe_k_2, pe_v_2, w_ck1_2, w_ck2_2,
        w_cv1_2, w_cv2_2, w_proj_pool_2, w_proj_nsa_2, w_out_2, norm_mlp_2, w_ff1_2, w_ff2_2,
        norm_final_2,
    )


_drawn_inputs = setup_inputs


def setup_inputs(seed=0):
    import zlib

    import numpy as np

    out = dict(_drawn_inputs(seed))
    spreads = {}
    factors = {'g_norm': 8.0,
     'g_qn_a': 8.0,
     'g_kn_a': 8.0,
     'g_cq': 8.0,
     'g_ckv': 8.0,
     'g_qn_b': 8.0,
     'g_kn_b': 8.0,
     'g_mem': 8.0,
     'g_qn_m': 8.0,
     'g_kn_m': 8.0,
     'pe_k_2': 64.0,
     'pe_v_2': 30.28,
     'norm_mix_2': 8.0,
     'w_in_2': 5.917,
     'w_pool_2': 6.052,
     'pool_scale_2': 8.0,
     'w_ck1_2': 8.0,
     'w_ck2_2': 8.0,
     'w_cv1_2': 8.0,
     'w_cv2_2': 8.0,
     'w_proj_pool_2': 6.054,
     'w_proj_nsa_2': 8.0,
     'w_out_2': 5.795,
     'norm_mlp_2': 64.0,
     'w_ff1_2': 8.0,
     'w_ff2_2': 8.0}
    for name, (base, spread) in spreads.items():
        noise = np.random.default_rng([zlib.crc32(name.encode()), seed]).standard_normal(out[name].shape)
        drawn = base * np.exp(spread * noise) if base else spread * noise
        out[name] = __import__('jax').numpy.asarray(drawn.astype(out[name].dtype))
    for name, factor in factors.items():
        out[name] = (out[name] * factor).astype(out[name].dtype)
    return out
```

```python
from contextlib import ExitStack

import numpy as np

import concourse.bass as bass
from concourse import mybir

ALU = mybir.AluOpType
ACT = mybir.ActivationFunctionType
AX = mybir.AxisListType
F32 = mybir.dt.float32
F32R = mybir.dt.float32r
I32 = mybir.dt.int32

P = 128
S = 512
TT = S // P
D = 1024
KT = D // P
NEG = -1e30
TAKEN = -3e38
BIG = 3e38
EPS = 1e-6
TOPK = 128
TWO_PI = 2 * np.pi
ROUND = 1.5 * 2.0 ** 23
PI_LOW = 3.1415925

QA, KA, VA, QI, KI, WI, ZA, CQ, CKV, KR, ZB, QM, ZM, GATES = (
    0, 512, 1024, 1536, 2048, 2112, 2120, 2632, 3016, 3272, 3304, 3816, 4328, 4840)
IN1_W = GATES // 10
KVB, QB, KB, YTA, YTB, YTM = 0, 1024, 1792, 2760, 0, 4328
GATED, MERGED, XRES = 512, 1536, 3816
U2, Q2, KC2, VC2, KS2, VS2, KW2, VW2, GN2, GATES2 = (
    0, 512, 1536, 1664, 1792, 1920, 2048, 2176, 2304, 2352)
IN2_W = GATES2 // 6
W1C = 2352
YS2, GATED2, MERGED2 = 512, 1536, 2560
NCMP = 31
HEADS = 8
WINDOWS = (2, 4, 8, 16)

PAIR_IN1, PAIR_MEM, PAIR_UQ, PAIR_UKV, PAIR_MERGE, PAIR_OUT1, PAIR_IN2, PAIR_M2, PAIR_OUT2, PAIR_FF = (
    0, 40, 48, 52, 54, 90, 98, 122, 150, 158)
RING = 4

STRIP_IN1, STRIP_MEM, STRIP_UQ, STRIP_UKV, STRIP_MERGE, STRIP_OUT1, STRIP_IN2, STRIP_M2, STRIP_OUT2, STRIP_FF = (
    0, 10, 12, 14, 16, 28, 30, 36, 44, 46)
STRIPS = ("A" * 10 + "AA" + "AA" + "AA" + "AADD" * 3 + "DD" + "A" * 6 + "AADDAADD" + "DD"
          + "A" + "ADD" * 7 + "DD")

PAIRS_OF = [4] * 12 + [2, 2, 1, 1] + [4, 4, 2, 2] * 3 + [4] * 8 + [4, 4, 2, 2, 4, 4, 4, 4] + [4, 4] + [4] + [4, 2, 2] * 7 + [2, 2]

GROUPS = {}
GROUP_OF = []
for _name, _n, _who in (
        ("vec", 1, "A"), ("x", 8, "AD"), ("mem", 4, "AD"), ("iq", 4, "A"), ("ik", 1, "A"),
        ("aq", 4, "A"), ("ak", 4, "D"), ("cq", 3, "AD"), ("ckv", 2, "AD"), ("ya", 4, "A"),
        ("b0", 8, "A"), ("b1", 8, "A"), ("yb", 4, "A"), ("mq", 4, "A"), ("mk", 2, "A"), ("ym", 4, "A"),
        ("x2", 8, "AD"), ("ck", 1, "D"), ("ckh", 1, "D"), ("cv", 1, "D"), ("cvh", 1, "D"),
        ("ckt", 1, "A"), ("cvt", 1, "A"), ("kcmp", 1, "D"), ("vcmp", 1, "D"), ("kct", 1, "A"),
        ("pd", 4, "A"), ("py", 4, "A"),
        ("n0", 6, "A"), ("n1", 6, "A"), ("yn", 8, "AD"), ("x3", 8, "AD")):
    GROUPS[_name] = len(GROUP_OF)
    GROUP_OF += [_who] * _n


def groups_emptied(who, through):
    return sum(who in g for g in GROUP_OF[:through + 1])


def strip_end(s):
    return sum(PAIRS_OF[:s + 1])


def strips_emptied(who, through):
    return sum(who == g for g in STRIPS[:through + 1])


def at(i, count):
    if isinstance(i, int):
        return count(i)
    step = count(2) - count(1)
    return i * step + (count(1) - step)


def wait(eng, sem, value):
    if not isinstance(value, int) or value > 0:
        eng.wait_ge(sem, value)


def constants():
    p = np.arange(P)
    out = {"ident": np.eye(P)}
    causal = np.zeros((P, S))
    causal[:, S - P:] = np.where(p[None, :] <= p[:, None], 0.0, NEG)
    out["causal"] = causal
    pos = (np.arange(TT)[None, :] * P + p[:, None]).astype(np.float64)
    inv2 = 10000.0 ** (-np.arange(0, 64, 2) / 64)
    ang = (pos[:, :, None].astype(np.float32) * inv2.astype(np.float32)).astype(np.float64)
    out["cos2"], out["sin2"] = np.cos(ang).reshape(P, -1), np.sin(ang).reshape(P, -1)
    end = p * 16 + 31
    angc = (end[:, None].astype(np.float32) * inv2.astype(np.float32)).astype(np.float64)
    out["cosc"], out["sinc"] = np.cos(angc), np.sin(angc)
    end = np.arange(NCMP) * 16 + 31
    out["cmask"] = np.where(end[None, None, :] <= pos[:, :, None], 0.0, NEG).reshape(P, -1)
    out["anyc"] = (pos >= 31).astype(np.float64)
    inva = 500000.0 ** (-np.arange(0, 16, 2) / 16)
    invb = 500000.0 ** (-np.arange(0, 32, 2) / 32)
    out["inv"] = np.tile(np.concatenate([inva, invb])[None], (P, 1))
    first, rest, halo = (np.zeros((P, 4, n)) for n in (P, P, 16))
    for g, w in enumerate(WINDOWS):
        for t in range(P):
            lo = max(0, t - w + 1)
            first[lo:t + 1, g, t] += 1.0 / min(t + 1, w)
            rest[lo:t + 1, g, t] += 1.0 / w
            first[t, g, t] -= 1.0
            rest[t, g, t] -= 1.0
            if t < w - 1:
                halo[P + t - w + 1:, g, t] = 1.0 / w
    out["pool0"], out["pool1"], out["poolh"] = (a.reshape(P, -1) for a in (first, rest, halo))
    return {k: v.astype(np.float32) for k, v in out.items()}


POOLS = ("pool0", "pool1", "poolh")


def two_block_kernel(
        nc, x, mem, positions, g_norm, w_in, g_qn_a, g_kn_a, g_cq, g_ckv, w_uq, w_ukv, g_qn_b, g_kn_b,
        g_mem, w_mem_kv, g_qn_m, g_kn_m, w_branch, w_out, norm_mix_2, w_in_2, w_pool_2,
        pool_scale_2, pe_k_2, pe_v_2, w_ck1_2, w_ck2_2, w_cv1_2, w_cv2_2, w_proj_pool_2,
        w_proj_nsa_2, w_out_2, norm_mlp_2, w_ff1_2, w_ff2_2, norm_final_2, out):
    with ExitStack() as ctx:
        SIZE = 53100
        arena = ctx.enter_context(nc.sbuf_tensor("arena", [P, SIZE], F32))
        base = nc.sbuf_base - SIZE * 4
        top = [0]

        def place(name, shape, dt=F32, where=None):
            n = int(np.prod(shape[1:]))
            if where is None:
                where = top[0]
                top[0] += -(-n // 8) * 8
                assert top[0] <= SIZE, (name, top[0])
            return nc.alloc_sbuf_tensor_at(name, shape, dt, offset=base + 4 * where)

        proj = place("proj", [P, TT, GATES])
        projr = place("projr", [P, TT, GATES], F32R, where=0)
        xt_hi = place("xt_hi", [P, KT, S], F32R)
        xt_lo = place("xt_lo", [P, KT, S], F32R)
        raw = place("raw", [P, RING, 2, S])
        w_hi = place("w_hi", [P, RING, 2, S], F32R)
        w_lo = place("w_lo", [P, RING, 2, S], F32R)
        E = top[0]
        top[0] += 9216
        mt_hi = place("mt_hi", [P, KT, 256], F32R, where=E)
        mt_lo = place("mt_lo", [P, KT, 256], F32R, where=E + 2048)
        kvm = place("kvm", [P, 2, D], where=E + 4096)
        q_t = place("q_t", [P, 4, S], where=E)
        k_t = place("k_t", [P, 4, S], where=E + 2048)
        z_tanh = [place(f"z_tanh{b}", [P, TT, S], where=E + 2048 * b) for b in range(2)]
        cq_hi = place("cq_hi", [P, 3, S], F32R, where=E)
        cq_lo = place("cq_lo", [P, 3, S], F32R, where=E + 1536)
        ckv_hi = place("ckv_hi", [P, 2, S], F32R, where=E + 6144)
        ckv_lo = place("ckv_lo", [P, 2, S], F32R, where=E + 7168)
        junk = place("junk", [P, 3072], where=E + 6144)
        sc = place("sc", [P, 2, S], where=E + 6144)
        prob = place("prob", [P, 2, S], where=E + 7168)
        prob_t = place("prob_t", [P, 2, S], where=E + 8192)
        ys = [[place(f"ys_{part}{b}", [P, 4, S], F32R, where=E + 4096 * b + 2048 * k)
               for k, part in enumerate(("hi", "lo"))] for b in range(2)]
        junk2 = place("junk2", [P, S], where=E + 4096)
        kd_t = place("kd_t", [P, 2, S], where=E + 2048)
        flat = place("flat", [P, 16, 2, NCMP], where=E + 3072)
        rot_q = place("rot_q", [P, 4, 512], where=E)
        rot_c = place("rot_c", [32, 4, 64], where=E + 4096)
        hid = place("hid", [64, 4, 256], where=E + 5120)
        hid_t = place("hid_t", [P, 2, 2, 62], where=E + 6144)
        pools = place("pools", [P, 1088], where=E + 6144)
        d_t = place("d_t", [P, 4, S], where=E)
        wpool = place("wpool", [P, 4, P], where=E + 2048)
        yn_hi = place("yn_hi", [P, KT, S], F32R, where=E)
        yn_lo = place("yn_lo", [P, KT, S], F32R, where=E + 4096)
        gfin = place("gfin", [P, D], where=E + 8192)

        consts = constants()
        cw = sum(v.shape[1] for k, v in consts.items() if k not in POOLS)
        cst = place("cst", [P, cw])
        col, o = {}, 0
        for k, v in consts.items():
            if k not in POOLS:
                col[k] = cst[:, o:o + v.shape[1]]
                o += v.shape[1]
        ident = col["ident"]
        causal = col["causal"]
        cst_d = nc.inline_tensor(np.concatenate([v for k, v in consts.items() if k not in POOLS], 1), "cst_d").ap()
        pool_d = nc.inline_tensor(np.concatenate([consts[k] for k in POOLS], 1), "pool_d").ap()

        vec_rows = place("vec_rows", [73, P], where=E + 8192)
        vec = place("vec", [P, 73])
        rows = {}
        for name, src, n in (("qa", g_qn_a, 64), ("ka", g_kn_a, 64), ("qb", g_qn_b, 96), ("kb", g_kn_b, 96),
                             ("qm", g_qn_m, P), ("km", g_kn_m, P)):
            rows[name] = (place("row_" + name, [P, n]), src)
        A = top[0]
        allow = place("allow", [P, 1280 - P])
        kcv = place("kcv", [32, 2, 2, 64], where=A)
        kc_t = place("kc_t", [P, 2, 32], where=A + 256)
        wc2 = place("wc2", [P, 2, 2, 64], where=A + 320)
        pos_i = place("pos_i", [P, TT], I32)
        pos_f = place("pos_f", [P, TT])
        ang = place("ang", [P, 4, TT, 24])
        cos1 = place("cos1", [P, TT, 24])
        sin1 = place("sin1", [P, TT, 24])
        stat = place("stat", [P, 64])
        rstd = place("rstd", [P, 64])
        half = place("half", [P, 64])
        m8 = place("m8", [P, 8])
        wi8 = place("wi8", [P, TT, HEADS])
        negmax = place("negmax", [P, 4])
        sums = place("sums", [P, 2, 8])
        rsum = place("rsum", [P, 2, 8])
        gsig = place("gsig", [P, TT, 48])

        bank = [ctx.enter_context(nc.psum_tensor(f"bank{i}", [P, 512], F32)) for i in range(8)]

        VEC = dict(norm=0, mem=8, mix=16, mlp=24, pool=32, cq=36, ckv=39, pek=41, pev=57)

        names = (
            "x_in", "mem_in", "cst_in", "vec_in", "pos_in", "row_in", "xres_in", "w1_in", "wc2_in", "w1v_in",
            "pool_in", "wpool_in", "fin_in", "stored",
            "hi_made", "lo_made", "pair_used", "emptied_a", "emptied_d",
            "group_done", "group_a", "group_d",
            "squares", "xs_ready", "stat_ready", "pow_done", "dve_step", "act_step", "sin_in", "sin_out", "half_set",
            "prep", "ready_for_t", "ix_scores", "ix_relu", "ix_acc", "allowed", "z_ready", "z_tanh",
            "scores", "masked", "exps", "probs_t", "copied_a", "copied_d", "applied", "o_emptied",
            "y_ready", "yt_in", "ys_hi", "ys_lo", "gated", "merged_in", "mhi", "mlo", "x2_ready",
            "tanh_in", "tanh_out", "hid_in", "w1_used", "relu_out", "sq_out", "h_hi", "h_lo",
            "x_out")
        sem = {n: ctx.enter_context(nc.semaphore(n)) for n in names}
        landed = [ctx.enter_context(nc.semaphore(f"landed{i}")) for i in range(RING)]

        UNITS, PASSES = [], []
        STAGE_UNITS, STAGE_PASSES = {}, {}

        def add_pass(stage, units, width, empty):
            STAGE_UNITS.setdefault(stage, [len(UNITS), 0])
            STAGE_PASSES.setdefault(stage, [len(PASSES), 0])
            for j, u in enumerate(units):
                UNITS.append(dict(u, j=j, pas=len(PASSES), first=j == 0, last=j == len(units) - 1, width=width))
            PASSES.append(dict(n=len(units), width=width, last=len(UNITS) - 1, **empty))
            STAGE_UNITS[stage][1] = len(UNITS)
            STAGE_PASSES[stage][1] = len(PASSES)

        def causal_mask(i):
            return causal[:, (TT - 1 - i) * P:S]

        def allow_mask(i):
            o = 0 if i == 1 else 256 if i == 2 else 640
            return causal_mask(0) if i == 0 else allow[:, o:o + (i + 1) * P]

        def half_rows(h):
            return slice(64 * (h % 2), 64 * (h % 2) + 64)

        for i in range(TT):
            add_pass("a", [dict(q=q_t[half_rows(h), h // 2, i * P:(i + 1) * P],
                                k=k_t[half_rows(h), h // 2, 0:(i + 1) * P], mask=allow_mask(i), n=(i + 1) * P,
                                v=[proj[:, t, VA + 64 * h:VA + 64 * h + 64] for t in range(i + 1)], scale=64 ** -0.5)
                           for h in range(HEADS)], 64, dict(kind="z", y=proj[:, i, QA:QA + 512],
                                                            z=proj[:, i, ZA:ZA + 512]))
        for r in range(2):
            for i in range(TT):
                add_pass(f"b{r}", [dict(q=q_t[0:96, h, i * P:(i + 1) * P], k=k_t[0:96, h, 0:(i + 1) * P],
                                        mask=causal_mask(i), n=(i + 1) * P, scale=96 ** -0.5,
                                        v=[proj[:, t, KVB + 128 * (4 * r + h) + 64:KVB + 128 * (4 * r + h) + 128]
                                           for t in range(i + 1)]) for h in range(4)], 64,
                         dict(kind="z", y=proj[:, i, QB + 256 * r:QB + 256 * r + 256],
                              z=proj[:, i, ZB + 256 * r:ZB + 256 * r + 256]))
        for i in range(TT):
            add_pass("m", [dict(q=q_t[:, h, i * P:(i + 1) * P], k=k_t[:, h, 0:256], mask=causal[:, 0:256], n=256,
                                v=[kvm[:, t, 512 + P * h:512 + P * h + P] for t in range(2)], scale=P ** -0.5)
                           for h in range(4)], P, dict(kind="z", y=proj[:, i, QM:QM + 512], z=proj[:, i, ZM:ZM + 512]))
        for g in range(2):
            for i in range(TT):
                for kind in range(3):
                    units = []
                    for h in range(HEADS):
                        hr = half_rows(h)
                        u = dict(q=q_t[hr, h // 2, i * P:(i + 1) * P], scale=64 ** -0.5)
                        if kind == 0:
                            u.update(k=kc_t[hr, g, 0:NCMP], n=NCMP, mask=col["cmask"][:, NCMP * i:NCMP * (i + 1)],
                                     v=[kcv[0:NCMP, 1, g, :]])
                        else:
                            vc = (VS2, VW2)[kind - 1] + 64 * g
                            u.update(k=kd_t[hr, kind - 1, 0:(i + 1) * P], n=(i + 1) * P, mask=causal_mask(i),
                                     v=[proj[:, t, vc:vc + 64] for t in range(i + 1)])
                        units.append(u)
                    add_pass(f"n{g}", units, 64, dict(
                        kind="g", y=proj[:, i, Q2 + 512 * g:Q2 + 512 * g + 512], first=kind == 0,
                        gate=gsig[:, i, 24 * g + kind:24 * g + 24:3]))

        def copier(u):
            return "D" if u % 2 == 0 else "A"

        def copies(who, through):
            return sum(copier(u) == who for u in range(through + 1))

        def wait_copied(eng, u):
            if u >= 0:
                eng.wait_ge(sem["copied_d" if copier(u) == "D" else "copied_a"], copies(copier(u), u))

        block = ctx.enter_context(nc.Block())

        def pairs_of(w, c0, n):
            return w.rearrange("(q two p) c -> q p two c", two=2, p=P)

        @block.sync
        def _(sp):
            sp.dma_start(cst[:], cst_d).then_inc(sem["cst_in"], 16)
            sp.dma_start(proj[:, 0:TT, XRES:XRES + D], x[0].rearrange("(t p) d -> p t d", p=P)).then_inc(sem["x_in"], 16)

            def load(p, slot, src, halves, width):
                if not isinstance(p, int) or p >= RING:
                    sp.wait_ge(sem["hi_made"], p - (RING - 1))
                    sp.wait_ge(sem["lo_made"], p - (RING - 1))
                sp.dma_start(raw[:, slot, 0:halves, 0:width], src).then_inc(landed[slot], 16)

            def stream(p0, w, col0, width, strips, looped=True):
                v = pairs_of(w, 0, 0)
                for q in range(4):
                    load(p0 + q, (p0 + q) % RING, v[q][:, :, col0:col0 + width], 2, width)
                if strips > 1:
                    with sp.Fori(1, strips) as i:
                        for q in range(4):
                            load(i * 4 + (p0 + q), (p0 + q) % RING,
                                 v[q][:, :, bass.ds(i * width + col0, width)], 2, width)

            stream(PAIR_IN1, w_in[0], 0, IN1_W, 10)
            stream(PAIR_MEM, w_mem_kv[0], 0, S, 2)
            for s in range(2):
                for q, halves in enumerate((2, 1)):
                    p = PAIR_UQ + 2 * s + q
                    src = w_uq[0, 256 * q:256 * q + 128 * halves, 384 * s:384 * s + 384]
                    load(p, p % RING, src.rearrange("(two p) c -> p two c", p=P), halves, 384)
            for s in range(2):
                p = PAIR_UKV + s
                load(p, p % RING, w_ukv[0, :, S * s:S * s + S].rearrange("(two p) c -> p two c", p=P), 2, S)

            def merge_weights(n):
                for s in range(2):
                    for q in range(4):
                        p = n * 12 + (PAIR_MERGE + 4 * s + q)
                        load(p, (PAIR_MERGE + q) % RING,
                             pairs_of(w_in[0], 0, 0)[q][:, :, bass.ds(n * D + (GATES + S * s), S)], 2, S)
                for s in range(2):
                    for q in range(2):
                        p = n * 12 + (PAIR_MERGE + 8 + 2 * s + q)
                        src = w_branch[0].rearrange("n (q two p) c -> (n q) p two c", two=2, p=P)
                        load(p, (PAIR_MERGE + 2 * s + q) % RING, src[n * 2 + q][:, :, S * s:S * s + S], 2, S)

            merge_weights(0)
            with sp.Fori(1, 3) as n:
                merge_weights(n)
            stream(PAIR_OUT1, w_out[0], 0, S, 2)
            sp.wait_ge(sem["pair_used"], strip_end(STRIP_OUT1 - 1))
            sp.dma_start(proj[:, 0:TT, XRES:XRES + D], x[0].rearrange("(t p) d -> p t d", p=P)).then_inc(sem["xres_in"], 16)
            stream(PAIR_IN2, w_in_2[0], 0, IN2_W, 6)
            def w1_load(w, name):
                for t in range(TT):
                    sp.dma_start(proj[:, t, W1C:W1C + D].rearrange("p (l c) -> p l c", l=4),
                                 w[S * t:S * t + S, :].rearrange("(l p) c -> p l c", p=P)).then_inc(sem[name], 16)
            sp.wait_ge(sem["pair_used"], strip_end(STRIP_OUT1 + 2 - 1))
            w1_load(w_ck1_2[0], "w1_in")
            for k, w in enumerate((w_ck2_2, w_cv2_2)):
                sp.dma_start(wc2[:, k], w[0].rearrange("(j p) c -> p j c", p=P)).then_inc(sem["wc2_in"], 16)
            sp.wait_ge(sem["group_done"], GROUPS["ckh"] + 1)
            w1_load(w_cv1_2[0], "w1v_in")
            sp.wait_ge(sem["group_done"], GROUPS["kct"] + 1)
            sp.dma_start(pools[:], pool_d).then_inc(sem["pool_in"], 16)
            sp.dma_start(wpool[:], w_pool_2[0].rearrange("g c d -> c g d")).then_inc(sem["wpool_in"], 16)
            stream(PAIR_M2, w_in_2[0], GATES2, S, 2)
            sp.wait_ge(sem["group_done"], GROUPS["yn"] + 8)
            sp.dma_start(gfin[:], norm_final_2.rearrange("(o d) -> o d", o=1).to_broadcast([P, D])).then_inc(sem["fin_in"], 16)
            for s in range(2):
                for q in range(2):
                    p = PAIR_M2 + 8 + 2 * s + q
                    load(p, p % RING, pairs_of(w_proj_pool_2[0], 0, 0)[q][:, :, S * s:S * s + S], 2, S)
            stream(PAIR_M2 + 12, w_in_2[0], GATES2 + D, S, 2)
            stream(PAIR_M2 + 20, w_proj_nsa_2[0], 0, S, 2)
            stream(PAIR_OUT2, w_out_2[0], 0, S, 2)

            def ff1_weights(f, p0):
                for q in range(4):
                    load(p0 + q, (PAIR_FF + q) % RING, pairs_of(w_ff1_2[0], 0, 0)[q][:, :, bass.ds(f * S, S)], 2, S)

            def ff2_weights(f, p0):
                for s in range(2):
                    for q in range(2):
                        src = pairs_of(w_ff2_2[0], 0, 0)[f * 2 + q]
                        load(p0 + 2 * s + q, (PAIR_FF + 2 * s + q) % RING, src[:, :, S * s:S * s + S], 2, S)

            ff1_weights(0, PAIR_FF)
            with sp.Fori(1, 8) as f:
                ff1_weights(f, f * 8 + (PAIR_FF - 4))
                ff2_weights(f - 1, f * 8 + PAIR_FF)
            ff2_weights(7, PAIR_FF + 60)
            sp.wait_ge(sem["x_out"], TT)
            sp.dma_start(out[0].rearrange("(t p) d -> p t d", p=P), proj[:, 0:TT, 0:D]).then_inc(sem["stored"], 16)
            sp.wait_ge(sem["stored"], 16)

        @block.gpsimd
        def _(pool):
            pool.memset(half[:], -0.5).then_inc(sem["half_set"], 1)
            pool.wait_ge(sem["half_set"], 1)
            pows = [0]

            def inv_sqrt(n):
                pool.wait_ge(sem["stat_ready"], pows[0] + 1)
                pool.tensor_tensor(rstd[:, 0:n], stat[:, 0:n], half[:, 0:n], ALU.pow).then_inc(sem["pow_done"], 1)
                pows[0] += 1

            def split(p, slot, halves, width):
                pool.wait_ge(sem["hi_made"], p + 1)
                if not isinstance(p, int) or p >= RING:
                    pool.wait_ge(sem["pair_used"], p - (RING - 1))
                pool.tensor_tensor(w_lo[:, slot, 0:halves, 0:width], raw[:, slot, 0:halves, 0:width],
                                   w_hi[:, slot, 0:halves, 0:width].bitcast(F32), ALU.subtract).then_inc(sem["lo_made"], 1)

            def split_run(p0, p1, width):
                if p0 == 0:
                    for q in range(RING):
                        split(q, q, 2, width)
                    p0 = RING
                with pool.Fori(0, (p1 - p0) // RING) as i:
                    for q in range(RING):
                        split(i * RING + (p0 + q), (p0 + q) % RING, 2, width)

            inv_sqrt(6)
            split_run(PAIR_IN1, 16, IN1_W)
            inv_sqrt(32)
            split_run(16, 20, IN1_W)
            inv_sqrt(32)
            split_run(20, PAIR_MEM, IN1_W)
            inv_sqrt(8)
            inv_sqrt(16)
            split_run(PAIR_MEM, PAIR_UQ, S)
            inv_sqrt(8)
            for p in range(PAIR_UQ, PAIR_UKV):
                split(p, p % RING, 2 - p % 2, 384)
            for p in range(PAIR_UKV, PAIR_MERGE):
                split(p, p % RING, 2, S)
            inv_sqrt(32)
            inv_sqrt(32)
            split_run(PAIR_MERGE, PAIR_IN2, S)
            inv_sqrt(4)
            split_run(PAIR_IN2, PAIR_M2, IN2_W)
            split_run(PAIR_M2, PAIR_FF, S)
            inv_sqrt(4)
            split_run(PAIR_FF, PAIR_FF + 64, S)
            inv_sqrt(4)

        @block.tensor
        def _(pe):
            def group(name, n, work):
                t = GROUPS[name] + n
                if t >= 2:
                    for who, s in (("A", "group_a"), ("D", "group_d")):
                        if who in GROUP_OF[t - 2]:
                            pe.wait_ge(sem[s], groups_emptied(who, t - 2))
                work(bank[6 + t % 2]).then_inc(sem["group_done"], 1)

            def enter_banks(strips):
                for who, s in (("A", "emptied_a"), ("D", "emptied_d")):
                    wait(pe, sem[s], strips_emptied(who, strips - 1))

            def enter_strips(name, passes):
                t = GROUPS[name] - 1
                pe.wait_ge(sem["group_a"], groups_emptied("A", t))
                pe.wait_ge(sem["group_d"], groups_emptied("D", t))
                wait(pe, sem["o_emptied"], passes)

            def transposes(pieces):
                def work(b):
                    o = 0
                    for src, k, m in pieces:
                        ins = pe.transpose(b[0:m, o:o + k], src, ident[0:k, 0:k])
                        o += k
                    return ins
                return work

            def columns(c, n=P):
                return transposes([(proj[:, t, c:c + n], P, n) for t in range(TT)])

            def wait_pair(p):
                pe.wait_ge(sem["hi_made"], p + 1)
                pe.wait_ge(sem["lo_made"], p + 1)

            def free_banks(i, strip):
                s0 = strip(i if isinstance(i, int) else 1) - 2
                if s0 >= 0:
                    who = STRIPS[s0]
                    pe.wait_ge(sem["emptied_a" if who == "A" else "emptied_d"],
                               at(i, lambda j: strips_emptied(who, strip(j) - 2)))

            def strip_products(s, p0, tiles, halves, kt0, x_parts, width, feature_major, first=True, last=True,
                               tok=TT):
                x_hi, x_lo = x_parts
                for q in range(tiles):
                    p = p0[q]
                    wait_pair(p[0])
                    slot = p[1]
                    n_half = halves[q]
                    for kk in range(n_half):
                        kt = kt0 + 2 * q + kk
                        st, en = first and q == 0 and kk == 0, last and q == tiles - 1 and kk == n_half - 1
                        wh, wl = w_hi[:, slot, kk, 0:width], w_lo[:, slot, kk, 0:width]
                        for b in range(tok):
                            dst = bank[4 * (s % 2) + b]
                            if feature_major:
                                c = slice(b * P, b * P + P)
                                terms = [(w_hi[:, slot, kk, c], x_hi[:, kt, :]), (w_hi[:, slot, kk, c], x_lo[:, kt, :]),
                                         (w_lo[:, slot, kk, c], x_hi[:, kt, :])]
                                o = dst[:, 0:S]
                            else:
                                c = slice(b * P, b * P + P)
                                terms = [(x_hi[:, kt, c], wh), (x_hi[:, kt, c], wl), (x_lo[:, kt, c], wh)]
                                o = dst[:, 0:width]
                            for j, (lhs, rhs) in enumerate(terms):
                                ins = pe.matmul(o, lhs, rhs, start=st and j == 0, stop=en and j == 2)
                    ins.then_inc(sem["pair_used"], 1)

            def slots(i, p0, n):
                return [(at(i, lambda j, q=q: p0(j) + q), (p0(i if isinstance(i, int) else 1) + q) % RING)
                        for q in range(n)]

            def strip(i, s, p0, n, x_parts, width, feature_major, halves=None, kt0=0, tok=TT):
                free_banks(i, s)
                sx = s(i if isinstance(i, int) else 1)
                strip_products(sx, slots(i, p0, n), n, halves or [2] * n, kt0, x_parts, width, feature_major, tok=tok)

            pe.wait_ge(sem["cst_in"], 16)
            pe.wait_ge(sem["vec_in"], 16 * 9)
            group("vec", 0, transposes([(vec_rows[:, :], 73, P)]))
            pe.wait_ge(sem["xs_ready"], 4)
            for k in range(KT):
                group("x", k, columns(XRES + P * k))
            pe.wait_ge(sem["xs_ready"], 6)
            for k in range(4):
                group("mem", k, transposes([(proj[:, t, 2792 + P * (2 * k + j):2792 + P * (2 * k + j) + P], P, P)
                                            for j in range(2) for t in range(2)]))
            enter_strips("iq", 0)

            xt = (xt_hi, xt_lo)

            def in1(i):
                for b in range(2):
                    strip(i, lambda j: STRIP_IN1 + 2 * j + b, lambda j: PAIR_IN1 + 8 * j + 4 * b, 4, xt, IN1_W, False)
            in1(0)
            with pe.Fori(1, 5) as i:
                in1(i)
            for b in range(2):
                strip(0, lambda j: STRIP_MEM + b, lambda j: PAIR_MEM + 4 * b, 4, (mt_hi, mt_lo), S, False, tok=2)

            enter_banks(STRIP_UQ)
            pe.wait_ge(sem["ready_for_t"], 1)
            for k in range(4):
                group("iq", k, columns(QI + P * k))
            group("ik", 0, transposes([(proj[:, t, KI:KI + 64], P, 64) for t in range(TT)]))
            pe.wait_ge(sem["group_a"], groups_emptied("A", GROUPS["ik"]))
            for n, (i, h) in enumerate((i, h) for i in range(1, TT) for h in range(HEADS)):
                if n >= 2:
                    pe.wait_ge(sem["ix_relu"], n - 1)
                pe.matmul(bank[n % 2][:, 0:(i + 1) * P], q_t[half_rows(h), h // 2, i * P:(i + 1) * P],
                          k_t[half_rows(h), 0, 0:(i + 1) * P], start=True, stop=True).then_inc(sem["ix_scores"], 1)
            pe.wait_ge(sem["ix_relu"], 24)

            def attention(stage):
                u0, u1 = STAGE_UNITS[stage]
                for step in range(u0, u1 + 3):
                    u = step
                    if u < u1:
                        w = UNITS[u]
                        if u >= 2:
                            pe.wait_ge(sem["masked"], u - 1)
                        pe.matmul(bank[u % 2][:, 0:w["n"]], w["q"], w["k"], start=True, stop=True)\
                          .then_inc(sem["scores"], 1)
                    u = step - 2
                    if u0 <= u < u1:
                        w = UNITS[u]
                        pe.wait_ge(sem["exps"], u + 1)
                        wait_copied(pe, u - 2)
                        for t in range(-(-w["n"] // P)):
                            n = min(P, w["n"] - t * P)
                            ins = pe.transpose(bank[2 + u % 2][0:n, t * P:(t + 1) * P],
                                               prob[:, u % 2, t * P:t * P + n], ident)
                        ins.then_inc(sem["probs_t"], 1)
                    u = step - 3
                    if u0 <= u < u1:
                        w = UNITS[u]
                        wait_copied(pe, u)
                        if w["first"] and w["pas"] >= 2:
                            pe.wait_ge(sem["o_emptied"], w["pas"] - 1)
                        wd = w["width"]
                        nt = len(w["v"])
                        for t in range(nt):
                            n = min(P, w["n"] - t * P)
                            ins = pe.matmul(bank[4 + w["pas"] % 2][:, w["j"] * wd:(w["j"] + 1) * wd],
                                            prob_t[0:n, u % 2, t * P:(t + 1) * P], w["v"][t],
                                            start=t == 0, stop=t == nt - 1)
                        ins.then_inc(sem["applied"], 1)

            for k in range(4):
                group("aq", k, columns(QA + P * k))
            for k in range(4):
                group("ak", k, columns(KA + P * k))
            pe.wait_ge(sem["group_a"], groups_emptied("A", GROUPS["ak"] + 3))
            pe.wait_ge(sem["group_d"], groups_emptied("D", GROUPS["ak"] + 3))
            attention("a")

            pe.wait_ge(sem["ready_for_t"], 2)
            for k in range(3):
                group("cq", k, columns(CQ + P * k))
            for k in range(2):
                group("ckv", k, columns(CKV + P * k))
            pe.wait_ge(sem["y_ready"], 1)
            for k in range(4):
                group("ya", k, columns(QA + P * k))
            enter_strips("b0", STAGE_PASSES["a"][1])
            for b in range(2):
                strip(0, lambda j: STRIP_UQ + b, lambda j: PAIR_UQ + 2 * b, 2, (cq_hi, cq_lo), 384, False, halves=[2, 1])
            for b in range(2):
                strip(0, lambda j: STRIP_UKV + b, lambda j: PAIR_UKV + b, 1, (ckv_hi, ckv_lo), S, False)
            enter_banks(STRIP_MERGE)
            pe.wait_ge(sem["ready_for_t"], 3)
            for r in range(2):
                for h in range(4):
                    group(f"b{r}", h, columns(QB + 96 * (4 * r + h), 96))
                for h in range(4):
                    group(f"b{r}", 4 + h, columns(KB + 96 * (4 * r + h), 96))
                pe.wait_ge(sem["group_a"], groups_emptied("A", GROUPS[f"b{r}"] + 7))
                attention(f"b{r}")
            pe.wait_ge(sem["y_ready"], 2)
            for k in range(4):
                group("yb", k, columns(QB + P * k))
            for k in range(4):
                group("mq", k, columns(QM + P * k))
            for k in range(2):
                group("mk", k, transposes([(kvm[:, t, P * (2 * k + j):P * (2 * k + j) + P], P, P)
                                           for j in range(2) for t in range(2)]))
            pe.wait_ge(sem["group_a"], groups_emptied("A", GROUPS["mk"] + 1))
            attention("m")
            pe.wait_ge(sem["y_ready"], 3)
            for k in range(4):
                group("ym", k, columns(QM + P * k))

            enter_strips("x2", STAGE_PASSES["m"][1])

            def merge(n, buf):
                for b in range(2):
                    strip(n, lambda j: STRIP_MERGE + 4 * j + b, lambda j: PAIR_MERGE + 12 * j + 4 * b, 4, xt, S, True)
                pe.wait_ge(sem["ys_hi"], at(n, lambda j: j + 1))
                pe.wait_ge(sem["ys_lo"], at(n, lambda j: j + 1))
                for b in range(2):
                    strip(n, lambda j: STRIP_MERGE + 4 * j + 2 + b, lambda j: PAIR_MERGE + 12 * j + 8 + 2 * b, 2,
                          buf, S, True)
            for n in range(3):
                merge(n, ys[n % 2])
            pe.wait_ge(sem["mhi"], 4)
            pe.wait_ge(sem["mlo"], 4)
            for b in range(2):
                strip(0, lambda j: STRIP_OUT1 + b, lambda j: PAIR_OUT1 + 4 * b, 4, xt, S, False)

            enter_banks(STRIP_IN2)
            pe.wait_ge(sem["xs_ready"], 10)
            for k in range(KT):
                group("x2", k, columns(P * k))
            enter_strips("ck", STAGE_PASSES["m"][1])

            def in2(i):
                for b in range(2):
                    strip(i, lambda j: STRIP_IN2 + 2 * j + b, lambda j: PAIR_IN2 + 8 * j + 4 * b, 4, xt, IN2_W, False)
            in2(0)
            with pe.Fori(1, 3) as i:
                in2(i)

            enter_banks(STRIP_M2)
            pe.wait_ge(sem["ready_for_t"], 4)
            for k, (name, w_in_sem) in enumerate((("ck", "w1_in"), ("cv", "w1v_in"))):
                group(name, 0, columns((KC2, VC2)[k]))
                pe.wait_ge(sem["group_d"], groups_emptied("D", GROUPS[name]))
                pe.wait_ge(sem[w_in_sem], 64)

                def hidden(b):
                    for lp in range(16):
                        c = W1C + 256 * (lp % 4)
                        ins = pe.matmul(b[0:62, 0:256], flat[:, lp].rearrange("p g n -> p (g n)"),
                                        proj[:, lp // 4, c:c + 256], start=lp == 0, stop=lp == 15)
                    return ins
                group(name + "h", 0, hidden)
            for k, name in enumerate(("ckt", "cvt")):
                pe.wait_ge(sem["hid_in"], k + 1)
                group(name, 0, transposes([(hid[0:62, 3, j * P:j * P + P] if k else hid[0:62, 2, j * P:j * P + P], 62, P)
                                           for j in range(2)]))
            pe.wait_ge(sem["wc2_in"], 32)
            for k, name in enumerate(("kcmp", "vcmp")):
                pe.wait_ge(sem["group_a"], groups_emptied("A", GROUPS["ckt"] + k))

                def second(b):
                    for g in range(2):
                        for j in range(2):
                            ins = pe.matmul(b[0:NCMP, 64 * g:64 * g + 64], hid_t[:, k, j, NCMP * g:NCMP * g + NCMP],
                                            wc2[:, k, j, :], start=j == 0, stop=j == 1)
                    return ins
                group(name, 0, second)
            pe.wait_ge(sem["ready_for_t"], 5)

            group("kct", 0, transposes([(kcv[0:NCMP, 0].rearrange("p g d -> p (g d)"), NCMP, P)]))

            pe.wait_ge(sem["pool_in"], 16)
            for g in range(4):
                def means(b):
                    c = slice(U2 + P * g, U2 + P * g + P)
                    for t in range(TT):
                        w = pools[:, (512 if t else 0) + P * g:(512 if t else 0) + P * g + P]
                        pe.matmul(b[:, t * P:t * P + P], proj[:, t, c], w, start=t == 0, stop=False,
                                  skip_group_check=True)
                    for t in range(1, TT):
                        ins = pe.matmul(b[:, t * P:t * P + 16], proj[:, t - 1, c],
                                        pools[:, 1024 + 16 * g:1040 + 16 * g], start=False, stop=t == TT - 1,
                                        skip_group_check=True)
                    return ins
                group("pd", g, means)
            pe.wait_ge(sem["wpool_in"], 16)
            pe.wait_ge(sem["group_a"], groups_emptied("A", GROUPS["pd"] + 3))
            for g in range(4):
                group("py", g, lambda b: pe.matmul(b[:, 0:S], wpool[:, g, :], d_t[:, g, :], start=True, stop=True))

            for g in range(2):
                for k in range(4):
                    group(f"n{g}", k, columns(Q2 + 512 * g + P * k))
                for k, c in enumerate((KS2, KW2)):
                    group(f"n{g}", 4 + k, columns(c))
                pe.wait_ge(sem["group_a"], groups_emptied("A", GROUPS[f"n{g}"] + 5))
                attention(f"n{g}")
            pe.wait_ge(sem["y_ready"], 4)
            for k in range(KT):
                group("yn", k, columns(Q2 + P * k))

            enter_strips("x3", STAGE_PASSES["n1"][1])
            m2 = PAIR_M2
            pool_parts = (projr[:, :, YS2:YS2 + S], projr[:, :, YS2 + S:YS2 + 2 * S])
            for b in range(2):
                strip(0, lambda j: STRIP_M2 + b, lambda j: m2 + 4 * b, 4, xt, S, True)
            pe.wait_ge(sem["ys_hi"], 4)
            pe.wait_ge(sem["ys_lo"], 4)
            for b in range(2):
                strip(0, lambda j: STRIP_M2 + 2 + b, lambda j: m2 + 8 + 2 * b, 2, pool_parts, S, True)
            for b in range(2):
                strip(0, lambda j: STRIP_M2 + 4 + b, lambda j: m2 + 12 + 4 * b, 4, xt, S, True)
            for b in range(2):
                strip(0, lambda j: STRIP_M2 + 6 + b, lambda j: m2 + 20 + 4 * b, 4, (yn_hi, yn_lo), S, True)
            pe.wait_ge(sem["mhi"], 8)
            pe.wait_ge(sem["mlo"], 8)
            for b in range(2):
                strip(0, lambda j: STRIP_OUT2 + b, lambda j: PAIR_OUT2 + 4 * b, 4, xt, S, False)

            enter_banks(STRIP_FF)
            pe.wait_ge(sem["xs_ready"], 14)
            for k in range(KT):
                group("x3", k, columns(P * k))
            pe.wait_ge(sem["group_a"], groups_emptied("A", GROUPS["x3"] + 7))
            pe.wait_ge(sem["group_d"], groups_emptied("D", GROUPS["x3"] + 7))

            def ff_up(f, s, p):
                strip(f, s, p, 4, xt, S, True)

            def ff_down(f, buf, s, p):
                pe.wait_ge(sem["h_hi"], at(f, lambda j: j))
                pe.wait_ge(sem["h_lo"], at(f, lambda j: j))
                for b in range(2):
                    strip(f, lambda j: s(j) + b, lambda j: p(j) + 2 * b, 2, ys[buf], S, False)

            def ff_step(i, parity, t):
                ff_up(i, lambda j: STRIP_FF + 1 + 3 * t(j), lambda j: PAIR_FF + 4 + 8 * t(j))
                pe.wait_ge(sem["h_hi"], at(i, lambda j: t(j) + 1))
                pe.wait_ge(sem["h_lo"], at(i, lambda j: t(j) + 1))
                for b in range(2):
                    strip(i, lambda j: STRIP_FF + 2 + b + 3 * t(j), lambda j: PAIR_FF + 8 + 2 * b + 8 * t(j), 2,
                          ys[parity], S, False)
            ff_up(0, lambda j: STRIP_FF, lambda j: PAIR_FF)
            ff_step(0, 0, lambda j: 0)
            with pe.Fori(1, 4) as i:
                ff_step(i, 1, lambda j: 2 * j - 1)
                ff_step(i, 0, lambda j: 2 * j)
            ff_down(8, 1, lambda j: STRIP_FF + 22, lambda j: PAIR_FF + 60)

        @block.scalar
        def _(act):
            act.dma_start(pos_i[:], positions[0].rearrange("(t p) -> p t", p=P), allow_slow_non_contiguous=True)\
               .then_inc(sem["pos_in"], 16)
            act.dma_start(proj[:, 0:2, 2792:2792 + D], mem[0].rearrange("(t p) d -> p t d", p=P)).then_inc(sem["mem_in"], 16)
            r = 0
            for src in (g_norm[0].rearrange("(r c) -> r c", c=P), g_mem[0].rearrange("(r c) -> r c", c=P),
                        norm_mix_2[0].rearrange("(r c) -> r c", c=P), norm_mlp_2[0].rearrange("(r c) -> r c", c=P),
                        pool_scale_2[0].rearrange("(r c) -> r c", c=P), g_cq[0].rearrange("(r c) -> r c", c=P),
                        g_ckv[0].rearrange("(r c) -> r c", c=P), pe_k_2[0].rearrange("(r two) c -> r (two c)", two=2),
                        pe_v_2[0].rearrange("(r two) c -> r (two c)", two=2)):
                act.dma_start(vec_rows[r:r + src.shape[0], :], src).then_inc(sem["vec_in"], 16)
                r += src.shape[0]
            for dst, src in rows.values():
                act.dma_start(dst[:], src.to_broadcast(dst.shape)).then_inc(sem["row_in"], 16)

            def part_hi(p, slot, halves, width):
                act.wait_ge(landed[slot], p // RING * 16 + 16 if isinstance(p, int) else (p + (RING - slot)) * 4)
                if not isinstance(p, int) or p >= RING:
                    act.wait_ge(sem["pair_used"], p - (RING - 1))
                act.activation(w_hi[:, slot, 0:halves, 0:width], raw[:, slot, 0:halves, 0:width], ACT.Copy)\
                   .then_inc(sem["hi_made"], 1)

            def his(i, p0, n=RING, width=S):
                for q in range(n):
                    slot = (p0(i if isinstance(i, int) else 1) + q) % RING
                    part_hi(at(i, lambda j: p0(j) + q), slot, 2, width)

            def group_wait(name, n):
                act.wait_ge(sem["group_done"], GROUPS[name] + n + 1)
                return bank[6 + (GROUPS[name] + n) % 2]

            def strip_wait(i, s):
                act.wait_ge(sem["pair_used"], at(i, lambda j: strip_end(s(j))))
                sx = s(i if isinstance(i, int) else 1)
                return bank[4 * (sx % 2):4 * (sx % 2) + 4]

            act.wait_ge(sem["sin_in"], 1)
            act.activation(sin1[:], ang[:, 1], ACT.Sin).then_inc(sem["sin_out"], 1)
            act.activation(cos1[:], ang[:, 1], ACT.Sin, scale=0.5).then_inc(sem["sin_out"], 1)
            act.preload_act_table(ACT.Exp)
            act.wait_ge(sem["x_in"], 16)
            for t in (1, 3):
                act.activation(junk[:, D:2 * D], proj[:, t, XRES:XRES + D], ACT.Square, accum_out=stat[:, t:t + 1])\
                   .then_inc(sem["squares"], 1)
                act.wait_ge(sem["squares"], t // 2 + 1)
            act.wait_ge(sem["mem_in"], 16)
            act.activation(junk[:, D:2 * D], proj[:, 1, 2792:2792 + D], ACT.Square, accum_out=stat[:, 5:6])\
               .then_inc(sem["squares"], 1)
            b = group_wait("vec", 0)
            act.activation(vec[:], b[:, 0:73], ACT.Copy).then_inc(sem["group_a"], 1)
            act.wait_ge(sem["group_a"], 1)
            for k in range(KT):
                b = group_wait("x", k)
                act.mul(xt_hi[:, k, :], b[:], vec[:, k:k + 1]).then_inc(sem["group_a"], 1)
            for k in range(4):
                b = group_wait("mem", k)
                act.mul(mt_hi[:, 2 * k, :], b[:, 0:256], vec[:, 8 + 2 * k:9 + 2 * k])
                act.mul(mt_hi[:, 2 * k + 1, :], b[:, 256:512], vec[:, 9 + 2 * k:10 + 2 * k]).then_inc(sem["group_a"], 1)

            def empty_in1(i, b):
                banks = strip_wait(i, lambda j: STRIP_IN1 + 2 * j + b)
                for t in range(TT):
                    c = at(i, lambda j: (2 * j + b) * IN1_W)
                    ins = act.activation(proj[:, t, bass.ds(c, IN1_W)], banks[t][:, 0:IN1_W], ACT.Copy)
                ins.then_inc(sem["emptied_a"], 1)
            his(0, lambda j: 0, width=IN1_W)

            def in1(i, last=False):
                his(i, lambda j: 8 * j + 4, width=IN1_W)
                empty_in1(i, 0)
                if not last:
                    his(i, lambda j: 8 * j + 8, width=IN1_W)
                    empty_in1(i, 1)
            in1(0)
            with act.Fori(1, 4) as i:
                in1(i)
            in1(4, last=True)
            his(0, lambda j: PAIR_MEM)
            empty_in1(4, 1)
            his(0, lambda j: PAIR_MEM + 4)
            for b in range(2):
                banks = strip_wait(0, lambda j: STRIP_MEM + b)
                for t in range(2):
                    ins = act.activation(kvm[:, t, S * b:S * b + S], banks[t][:], ACT.Copy)
                ins.then_inc(sem["emptied_a"], 1)
                for q in range(2):
                    p = PAIR_UQ + 2 * b + q
                    part_hi(p, p % RING, 2 - q, 384)

            act.activation(z_tanh[0][:], proj[:, :, ZA:ZA + S], ACT.Tanh, scale=0.5).then_inc(sem["z_tanh"], 1)
            act.activation(z_tanh[1][:], proj[:, :, ZB:ZB + S], ACT.Tanh, scale=0.5).then_inc(sem["z_tanh"], 1)
            act.wait_ge(sem["z_ready"], 1)
            act.activation(z_tanh[0][:], proj[:, :, ZM:ZM + S], ACT.Tanh, scale=0.5).then_inc(sem["z_tanh"], 1)

            for k in range(4):
                b = group_wait("iq", k)
                act.activation(q_t[:, k, :], b[:], ACT.Copy).then_inc(sem["group_a"], 1)
            b = group_wait("ik", 0)
            act.activation(k_t[0:64, 0, :], b[0:64, :], ACT.Copy)
            act.activation(k_t[64:128, 0, :], b[0:64, :], ACT.Copy).then_inc(sem["group_a"], 1)
            for n, i in enumerate(i for i in range(1, TT) for h in range(HEADS)):
                act.wait_ge(sem["ix_scores"], n + 1)
                if n >= 2:
                    act.wait_ge(sem["ix_acc"], n - 1)
                elif n == 0:
                    act.wait_ge(sem["ready_for_t"], 1)
                act.activation(sc[:, n % 2, 0:(i + 1) * P], bank[n % 2][:, 0:(i + 1) * P], ACT.Relu,
                               scale=64 ** -0.5).then_inc(sem["ix_relu"], 1)
            def attention(stage):
                u0, u1 = STAGE_UNITS[stage]
                for step in range(u0, u1 + 2):
                    u = step
                    if u < u1:
                        w = UNITS[u]
                        act.wait_ge(sem["masked"], u + 1)
                        if u >= 2:
                            act.wait_ge(sem["probs_t"], u - 1)
                        act.activation(prob[:, u % 2, 0:w["n"]], sc[:, u % 2, 0:w["n"]], ACT.Exp, scale=-1.0,
                                       bias=negmax[:, u % 4:u % 4 + 1],
                                       accum_out=sums[:, w["pas"] % 2, w["j"]:w["j"] + 1]).then_inc(sem["exps"], 1)
                    u = step - 2
                    if u0 <= u < u1 and copier(u) == "A":
                        w = UNITS[u]
                        act.wait_ge(sem["probs_t"], u + 1)
                        if u >= 2:
                            act.wait_ge(sem["applied"], u - 1)
                        n, r = (w["n"], P) if w["n"] >= P else (P, w["n"])
                        act.activation(prob_t[0:r, u % 2, 0:n], bank[2 + u % 2][0:r, 0:n], ACT.Copy)\
                           .then_inc(sem["copied_a"], 1)

            for k in range(4):
                b = group_wait("aq", k)
                act.activation(q_t[:, k, :], b[:], ACT.Copy).then_inc(sem["group_a"], 1)
            attention("a")

            def transposed_y(name, c):
                for k in range(4):
                    b = group_wait(name, k)
                    if k == 0:
                        act.wait_ge(sem["group_done"], GROUPS[name] + 2)
                    act.mul(yt[name][:, k, :], b[:], 0.5).then_inc(sem["group_a"], 1)

            yt = {"ya": proj[:, :, YTA:YTA + S], "yb": proj[:, :, YTB:YTB + S], "ym": proj[:, :, YTM:YTM + S]}

            for k in range(3):
                b = group_wait("cq", k)
                act.mul(cq_hi[:, k, :], b[:], vec[:, VEC["cq"] + k:VEC["cq"] + k + 1]).then_inc(sem["group_a"], 1)
            for k in range(2):
                b = group_wait("ckv", k)
                act.mul(ckv_hi[:, k, :], b[:], vec[:, VEC["ckv"] + k:VEC["ckv"] + k + 1]).then_inc(sem["group_a"], 1)
            transposed_y("ya", QA)
            for p in range(PAIR_UKV, PAIR_MERGE):
                part_hi(p, p % RING, 2, S)
            for b in range(2):
                banks = strip_wait(0, lambda j: STRIP_UQ + b)
                for t in range(TT):
                    ins = act.activation(proj[:, t, QB + 384 * b:QB + 384 * b + 384], banks[t][:, 0:384], ACT.Copy)
                ins.then_inc(sem["emptied_a"], 1)
            for b in range(2):
                banks = strip_wait(0, lambda j: STRIP_UKV + b)
                for t in range(TT):
                    ins = act.activation(proj[:, t, KVB + S * b:KVB + S * b + S], banks[t][:], ACT.Copy)
                ins.then_inc(sem["emptied_a"], 1)
            for r in range(2):
                for h in range(8):
                    b = group_wait(f"b{r}", h)
                    dst = q_t if h < 4 else k_t
                    act.activation(dst[0:96, h % 4, :], b[0:96, :], ACT.Copy).then_inc(sem["group_a"], 1)
                attention(f"b{r}")
            transposed_y("yb", QB)
            for k in range(4):
                b = group_wait("mq", k)
                act.activation(q_t[:, k, :], b[:], ACT.Copy).then_inc(sem["group_a"], 1)
            for k in range(2):
                b = group_wait("mk", k)
                act.activation(k_t[:, 2 * k:2 * k + 2, 0:256], b[:].rearrange("p (a n) -> p a n", a=2), ACT.Copy)\
                   .then_inc(sem["group_a"], 1)
            attention("m")
            transposed_y("ym", QM)

            def merge_act(n, nxt=None):
                for b in range(2):
                    his(n, lambda j: PAIR_MERGE + 12 * j + 4 * b)
                    if b == 1:
                        empty_gate(n, 0)
                his(n, lambda j: PAIR_MERGE + 12 * j + 8)
                empty_gate(n, 1)

            def empty_gate(n, b, s0=STRIP_MERGE, per=4, dst=GATED):
                banks = strip_wait(n, lambda j: s0 + per * j + b)
                if b == 0:
                    wait(act, sem["gated"], at(n, lambda j: 2 * j))
                for m in range(4):
                    mt = 4 * b + m
                    ins = act.activation(proj[:, mt // 2, dst + S * (mt % 2):dst + S * (mt % 2) + S],
                                         banks[m][:], ACT.Tanh, scale=0.5)
                ins.then_inc(sem["emptied_a"], 1)

            for n, name in enumerate(("ya", "yb", "ym")):
                if n == 2:
                    act.wait_ge(sem["pair_used"], strip_end(STRIP_MERGE + 4 - 1))
                act.activation(ys[n % 2][0][:], yt[name], ACT.Copy).then_inc(sem["ys_hi"], 1)
                merge_act(n)
            his(0, lambda j: PAIR_OUT1)
            act.wait_ge(sem["merged_in"], 1)
            act.wait_ge(sem["pair_used"], strip_end(STRIP_OUT1 - 1))
            for t in range(TT):
                act.mul(xt_hi[:, 2 * t:2 * t + 2, :], proj[:, t, MERGED:MERGED + D].rearrange("p (a n) -> p a n", a=2),
                        0.5).then_inc(sem["mhi"], 1)
            his(0, lambda j: PAIR_OUT1 + 4)

            def normed(name, v):
                for k in range(KT):
                    b = group_wait(name, k)
                    if k == 0:
                        act.wait_ge(sem["pair_used"], strip_end((STRIP_IN2 if name == "x2" else STRIP_FF) - 1))
                    act.mul(xt_hi[:, k, :], b[:], vec[:, v + k:v + k + 1]).then_inc(sem["group_a"], 1)

            act.wait_ge(sem["emptied_d"], strips_emptied("D", STRIP_IN2 - 1))
            his(0, lambda j: PAIR_IN2, width=IN2_W)
            for t in (1, 3):
                act.activation(junk[:, D:2 * D], proj[:, t, XRES:XRES + D], ACT.Square, accum_out=stat[:, t:t + 1])\
                   .then_inc(sem["squares"], 1)
                act.wait_ge(sem["squares"], 3 + t // 2 + 1)
            normed("x2", VEC["mix"])

            def empty_in2(i, b):
                banks = strip_wait(i, lambda j: STRIP_IN2 + 2 * j + b)
                for t in range(TT):
                    c = at(i, lambda j: (2 * j + b) * IN2_W)
                    ins = act.activation(proj[:, t, bass.ds(c, IN2_W)], banks[t][:, 0:IN2_W], ACT.Copy)
                ins.then_inc(sem["emptied_a"], 1)

            def in2(i, last=False):
                his(i, lambda j: PAIR_IN2 + 8 * j + 4, width=IN2_W)
                empty_in2(i, 0)
                if not last:
                    his(i, lambda j: PAIR_IN2 + 8 * j + 8, width=IN2_W)
                empty_in2(i, 1)
            in2(0)
            with act.Fori(1, 2) as i:
                in2(i)
            in2(2, last=True)

            act.wait_ge(sem["emptied_a"], strips_emptied("A", STRIP_M2 - 1))
            act.activation(gsig[:], proj[:, :, GN2:GN2 + 48], ACT.Tanh, scale=0.5).then_inc(sem["tanh_out"], 1)
            for k in range(2):
                act.wait_ge(sem["tanh_in"], k + 1)
                act.activation(hid[0:62, 1, :], hid[0:62, 1, :], ACT.Tanh, scale=(2 / np.pi) ** 0.5)\
                   .then_inc(sem["tanh_out"], 1)
            for k, name in enumerate(("ckt", "cvt")):
                b = group_wait(name, 0)
                act.mul(hid_t[:, k], b[:, 0:124].rearrange("p (j n) -> p j n", j=2), 0.5).then_inc(sem["group_a"], 1)
            b = group_wait("kct", 0)
            for g in range(2):
                for r in (slice(0, 64), slice(64, 128)):
                    ins = act.activation(kc_t[r, g, 0:NCMP], b[64 * g:64 * g + 64, 0:NCMP], ACT.Copy)
            ins.then_inc(sem["group_a"], 1)
            for g in range(4):
                b = group_wait("pd", g)
                act.activation(d_t[:, g, :], b[:], ACT.Copy).then_inc(sem["group_a"], 1)
            for g in range(4):
                b = group_wait("py", g)
                act.mul(proj[:, g, U2:U2 + S], b[:], vec[:, VEC["pool"] + g:VEC["pool"] + g + 1]).then_inc(sem["group_a"], 1)
            for g in range(2):
                for k in range(4):
                    b = group_wait(f"n{g}", k)
                    act.activation(q_t[:, k, :], b[:], ACT.Copy).then_inc(sem["group_a"], 1)
                for k in range(2):
                    b = group_wait(f"n{g}", 4 + k)
                    act.activation(kd_t[0:64, k, :], b[64 * g:64 * g + 64, :], ACT.Copy)
                    act.activation(kd_t[64:128, k, :], b[64 * g:64 * g + 64, :], ACT.Copy).then_inc(sem["group_a"], 1)
                attention(f"n{g}")
            for k in range(KT):
                b = group_wait("yn", k)
                act.activation(yn_hi[:, k, :], b[:], ACT.Copy).then_inc(sem["group_a"], 1)

            act.wait_ge(sem["group_done"], GROUPS["yn"] + 8)
            act.activation(projr[:, :, YS2:YS2 + S], proj[:, :, U2:U2 + S], ACT.Copy).then_inc(sem["ys_hi"], 1)
            his(0, lambda j: PAIR_M2)
            his(0, lambda j: PAIR_M2 + 4)

            def empty_gate2(b, k):
                banks = strip_wait(0, lambda j: STRIP_M2 + 4 * k + b)
                if b == 0 and k == 1:
                    act.wait_ge(sem["gated"], 8)
                for m in range(4):
                    mt = 4 * b + m
                    ins = act.activation(proj[:, mt // 2, GATED2 + S * (mt % 2):GATED2 + S * (mt % 2) + S],
                                         banks[m][:], ACT.Tanh, scale=0.5)
                ins.then_inc(sem["emptied_a"], 1)
            empty_gate2(0, 0)
            his(0, lambda j: PAIR_M2 + 8)
            empty_gate2(1, 0)
            his(0, lambda j: PAIR_M2 + 12)
            his(0, lambda j: PAIR_M2 + 16)
            empty_gate2(0, 1)
            his(0, lambda j: PAIR_M2 + 20)
            empty_gate2(1, 1)
            his(0, lambda j: PAIR_M2 + 24)
            his(0, lambda j: PAIR_OUT2)
            act.wait_ge(sem["merged_in"], 2)
            act.wait_ge(sem["pair_used"], strip_end(STRIP_OUT2 - 1))
            for t in range(TT):
                act.mul(xt_hi[:, 2 * t:2 * t + 2, :], proj[:, t, MERGED2:MERGED2 + D].rearrange("p (a n) -> p a n", a=2),
                        0.5).then_inc(sem["mhi"], 1)
            his(0, lambda j: PAIR_OUT2 + 4)
            act.wait_ge(sem["emptied_d"], strips_emptied("D", STRIP_FF - 1))
            his(0, lambda j: PAIR_FF)
            for t in (1, 3):
                act.activation(proj[:, t, D:2 * D], proj[:, t, XRES:XRES + D],
                               ACT.Square, accum_out=stat[:, t:t + 1]).then_inc(sem["squares"], 1)
                act.wait_ge(sem["squares"], 5 + t // 2 + 1)
            normed("x3", VEC["mlp"])

            relu = proj[:, :, D:D + S]
            square = proj[:, :, D + S:D + 2 * S]

            def ff_act(i, parity, s, p, f):
                his(i, p)
                empty_up(i, parity, s, f)

            def empty_up(i, parity, s, f):
                banks = strip_wait(i, s)
                wait(act, sem["sq_out"], at(i, lambda j: f(j)))
                for m in range(4):
                    ins = act.activation(relu[:, m, :], banks[m][:], ACT.Relu)
                ins.then_inc(sem["emptied_a"], 1)
                if not (isinstance(i, int) and f(i) < 2):
                    act.wait_ge(sem["pair_used"], at(i, lambda j: PAIR_FF + 12 + 8 * (f(j) - 2)))
                act.wait_ge(sem["sq_out"], at(i, lambda j: f(j) + 1))
                act.activation(ys[parity][0][:], square, ACT.Copy).then_inc(sem["h_hi"], 1)

            his(0, lambda j: PAIR_FF + 4)
            empty_up(0, 0, lambda j: STRIP_FF, lambda j: 0)

            def ff_step(i, parity, t):
                his(i, lambda j: PAIR_FF + 8 + 8 * t(j))
                empty_up(i, 1 - parity, lambda j: STRIP_FF + 1 + 3 * t(j), lambda j: t(j) + 1)
                his(i, lambda j: PAIR_FF + 12 + 8 * t(j))
            ff_step(0, 0, lambda j: 0)
            with act.Fori(1, 4) as i:
                ff_step(i, 1, lambda j: 2 * j - 1)
                ff_step(i, 0, lambda j: 2 * j)
            act.wait_ge(sem["emptied_d"], strips_emptied("D", len(STRIPS) - 1))
            for t in (1, 3):
                act.activation(proj[:, t, D:2 * D], proj[:, t, XRES:XRES + D],
                               ACT.Square, accum_out=stat[:, t:t + 1]).then_inc(sem["squares"], 1)
                act.wait_ge(sem["squares"], 7 + t // 2 + 1)

        @block.vector
        def _(dve):
            steps = [0]

            def step(ins):
                steps[0] += 1
                ins.then_inc(sem["dve_step"], 1)
                dve.wait_ge(sem["dve_step"], steps[0])

            def group_wait(name, n):
                dve.wait_ge(sem["group_done"], GROUPS[name] + n + 1)
                return bank[6 + (GROUPS[name] + n) % 2]

            def strip_wait(i, s):
                dve.wait_ge(sem["pair_used"], at(i, lambda j: strip_end(s(j))))
                sx = s(i if isinstance(i, int) else 1)
                return bank[4 * (sx % 2):4 * (sx % 2) + 4]

            powers = [0]

            def inv_rms(n, width, ready=None):
                dve.tensor_scalar(stat[:, 0:n], stat[:, 0:n], 1.0 / width, EPS, ALU.mult, ALU.add)\
                   .then_inc(sem["stat_ready"], 1)
                powers[0] += 1
                dve.wait_ge(sem["pow_done"], powers[0])

            def head_norm(v, h, d, gain):
                nt = v.shape[1]
                s = junk[:, 0:nt * h * d].rearrange("p (t h d) -> p t h d", t=nt, h=h)
                step(dve.tensor_tensor(s, v, v, ALU.mult))
                step(dve.tensor_reduce(stat[:, 0:nt * h].rearrange("p (t h) -> p t h", t=nt), s, AX.X, ALU.add))
                inv_rms(nt * h, d)
                r = rstd[:, 0:nt * h].rearrange("p (t h) -> p t h", t=nt).unsqueeze(3).to_broadcast([P, nt, h, d])
                step(dve.tensor_tensor(v, v, r, ALU.mult))
                step(dve.tensor_tensor(v, v, gain[:].unsqueeze(1).unsqueeze(1).to_broadcast([P, nt, h, d]), ALU.mult))

            def rotate(a, b, cos, sin, t1, t2):
                dve.tensor_tensor(t1[0], a, cos, ALU.mult)
                dve.tensor_tensor(t1[1], b, sin, ALU.mult)
                dve.tensor_tensor(t2[0], b, cos, ALU.mult)
                step(dve.tensor_tensor(t2[1], a, sin, ALU.mult))
                dve.tensor_tensor(a, t1[0], t1[1], ALU.subtract)
                return dve.tensor_tensor(b, t2[0], t2[1], ALU.add)

            def rotate_heads(c, h, d, r0, n, cos, sin, scratch):
                v = proj[:, :, c:c + h * d].rearrange("p t (h d) -> p t h d", h=h)
                a, b = v[:, :, :, r0:r0 + n], v[:, :, :, r0 + n:r0 + 2 * n]
                k = [scratch[j] .rearrange("p (t h n) -> p t h n", t=TT, h=h) for j in range(4)]
                cb, sb_ = (z.unsqueeze(2).to_broadcast([P, TT, h, n]) for z in (cos, sin))
                return rotate(a, b, cb, sb_, k[0:2], k[2:4])

            def rot_scratch(n):
                return [junk[:, n * j:n * j + n] for j in range(4)]

            dve.wait_ge(sem["pos_in"], 16)
            dve.wait_ge(sem["cst_in"], 16)
            step(dve.tensor_copy(pos_f[:], pos_i[:]))
            step(dve.tensor_tensor(ang[:, 0], pos_f[:].unsqueeze(2).to_broadcast([P, TT, 24]),
                                   col["inv"].unsqueeze(1).to_broadcast([P, TT, 24]), ALU.mult))
            step(dve.tensor_scalar(ang[:, 2], ang[:, 0], 1.0 / TWO_PI, ROUND, ALU.mult, ALU.add))
            step(dve.tensor_scalar(ang[:, 2], ang[:, 2], ROUND, None, ALU.subtract))
            c1 = 6.28125
            c2 = float(np.round((TWO_PI - c1) * 2 ** 20) / 2 ** 20)
            c3 = TWO_PI - c1 - c2
            for c, src in ((c1, 0), (c2, 3), (c3, 3)):
                step(dve.scalar_tensor_tensor(ang[:, 3], ang[:, 2], -float(c), ang[:, src], ALU.mult, ALU.add))
            dve.tensor_scalar(ang[:, 1], ang[:, 3], PI_LOW, -PI_LOW, ALU.min, ALU.max).then_inc(sem["sin_in"], 1)
            dve.wait_ge(sem["sin_out"], 2)
            step(dve.tensor_tensor(cos1[:], cos1[:], cos1[:], ALU.mult))
            step(dve.tensor_scalar(cos1[:], cos1[:], -2.0, 1.0, ALU.mult, ALU.add))
            dve.wait_ge(sem["x_in"], 16)
            for t in (0, 2):
                step(dve.tensor_tensor_reduce(junk[:, 0:D], proj[:, t, XRES:XRES + D], proj[:, t, XRES:XRES + D],
                                              1.0, 0.0, ALU.mult, ALU.add, stat[:, t:t + 1]))
            dve.wait_ge(sem["mem_in"], 16)
            step(dve.tensor_tensor_reduce(junk[:, 0:D], proj[:, 0, 2792:2792 + D], proj[:, 0, 2792:2792 + D],
                                          1.0, 0.0, ALU.mult, ALU.add, stat[:, 4:5]))
            dve.wait_ge(sem["squares"], 3)
            inv_rms(6, D)
            for t in range(TT):
                v = proj[:, t, XRES:XRES + D]
                dve.tensor_scalar(v, v, rstd[:, t:t + 1], None, ALU.mult).then_inc(sem["xs_ready"], 1)
            for t in range(2):
                v = proj[:, t, 2792:2792 + D]
                dve.tensor_scalar(v, v, rstd[:, 4 + t:5 + t], None, ALU.mult).then_inc(sem["xs_ready"], 1)
            dve.wait_ge(sem["group_a"], 1)
            for k in range(KT):
                b = group_wait("x", k)
                dve.wait_ge(sem["group_a"], groups_emptied("A", GROUPS["x"] + k))
                dve.scalar_tensor_tensor(xt_lo[:, k, :], b[:], vec[:, k:k + 1], xt_hi[:, k, :].bitcast(F32),
                                         ALU.mult, ALU.subtract).then_inc(sem["group_d"], 1)
            for k in range(4):
                b = group_wait("mem", k)
                dve.wait_ge(sem["group_a"], groups_emptied("A", GROUPS["mem"] + k))
                for j in range(2):
                    kt = 2 * k + j
                    ins = dve.scalar_tensor_tensor(mt_lo[:, kt, :], b[:, 256 * j:256 * j + 256], vec[:, 8 + kt:9 + kt],
                                                   mt_hi[:, kt, :].bitcast(F32), ALU.mult, ALU.subtract)
                ins.then_inc(sem["group_d"], 1)

            dve.wait_ge(sem["row_in"], 16 * 6)
            cosa, sina = cos1[:, :, 0:8], sin1[:, :, 0:8]
            cosb, sinb = cos1[:, :, 8:24], sin1[:, :, 8:24]

            def columns_in(c):
                dve.wait_ge(sem["emptied_a"], -(-c // IN1_W))

            def heads(c, h, d):
                return proj[:, :, c:c + h * d].rearrange("p t (h d) -> p t h d", h=h)

            columns_in(KA)
            head_norm(heads(QA, 8, 64), 8, 64, rows["qa"][0])
            columns_in(VA)
            head_norm(heads(KA, 8, 64), 8, 64, rows["ka"][0])
            step(rotate_heads(QA, 8, 64, 0, 8, cosa, sina, rot_scratch(256)))
            step(rotate_heads(KA, 8, 64, 0, 8, cosa, sina, rot_scratch(256)))
            columns_in(ZA)
            step(rotate_heads(QI, 8, 64, 0, 8, cosa, sina, rot_scratch(256)))
            step(rotate_heads(KI, 1, 64, 0, 8, cosa, sina, rot_scratch(32)))
            step(dve.tensor_scalar(wi8[:], proj[:, :, WI:WI + 8], HEADS ** -0.5, None, ALU.mult))
            columns_in(KR)
            for n, (c, w) in enumerate(((CQ, 384), (CKV, 256))):
                for t in range(TT):
                    v = proj[:, t, c:c + w]
                    step(dve.tensor_tensor_reduce(junk[:, 0:w], v, v, 1.0, 0.0, ALU.mult, ALU.add,
                                                  stat[:, 4 * n + t:4 * n + t + 1]))
            dve.tensor_scalar(stat[:, 0:4], stat[:, 0:4], 256.0 / 384.0, None, ALU.mult).then_inc(sem["dve_step"], 1)
            steps[0] += 1
            dve.wait_ge(sem["dve_step"], steps[0])
            inv_rms(8, 256)
            for n, (c, w) in enumerate(((CQ, 384), (CKV, 256))):
                v = proj[:, :, c:c + w]
                step(dve.tensor_tensor(v, v, rstd[:, 4 * n:4 * n + 4].unsqueeze(2).to_broadcast([P, TT, w]), ALU.mult))
            columns_in(ZM)
            head_norm(heads(QM, 4, P), 4, P, rows["qm"][0])
            dve.wait_ge(sem["emptied_a"], STRIP_MEM + 1)
            head_norm(kvm[:, :, 0:512].rearrange("p t (h d) -> p t h d", h=4), 4, P, rows["km"][0])
            dve.wait_ge(sem["emptied_a"], STRIP_MEM + 2)
            for n, c in enumerate((ZA, ZB, ZM)):
                dve.wait_ge(sem["z_tanh"], n + 1)
                z = proj[:, :, c:c + S]
                ins = dve.scalar_tensor_tensor(z, z_tanh[n % 2][:], 1.0, z, ALU.add, ALU.mult)
                ins.then_inc(sem["z_ready"], 1)
            dve.wait_ge(sem["z_ready"], 3)
            dve.sem_inc(sem["ready_for_t"], 1)

            index = {1: allow[:, 0:256], 2: allow[:, 256:640], 3: allow[:, 640:1152]}
            for n, (i, h) in enumerate((i, h) for i in range(1, TT) for h in range(HEADS)):
                dve.wait_ge(sem["ix_relu"], n + 1)
                if h:
                    dve.wait_ge(sem["ix_acc"], n)
                w = (i + 1) * P
                dve.scalar_tensor_tensor(index[i], sc[:, n % 2, 0:w], wi8[:, i, h:h + 1],
                                         causal_mask(i) if h == 0 else index[i], ALU.mult, ALU.add)\
                   .then_inc(sem["ix_acc"], 1)
            for k in range(4):
                b = group_wait("ak", k)
                if k == 0:
                    dve.wait_ge(sem["ix_scores"], 24)
                dve.tensor_copy(k_t[:, k, :], b[:]).then_inc(sem["group_d"], 1)
            dve.wait_ge(sem["ix_acc"], 24)
            for r in range(TOPK // 8):
                for i in range(1, TT):
                    step(dve.max(m8[:], index[i]))
                    step(dve.match_replace(index[i], m8[:], index[i], TAKEN))
            for i in range(1, TT):
                step(dve.tensor_scalar(index[i], index[i], 0.5 * TAKEN, NEG, ALU.is_gt, ALU.mult))
                step(dve.tensor_tensor(index[i], index[i], causal_mask(i), ALU.add))

            def attention(stage):
                u0, u1 = STAGE_UNITS[stage]
                for s in range(u0, u1 + 5):
                    u = s
                    if u < u1:
                        w = UNITS[u]
                        dve.wait_ge(sem["scores"], u + 1)
                        if u >= 2:
                            dve.wait_ge(sem["exps"], u - 1)
                        dve.tensor_tensor_reduce(sc[:, u % 2, 0:w["n"]], bank[u % 2][:, 0:w["n"]], w["mask"],
                                                 -w["scale"], BIG, ALU.add, ALU.min, negmax[:, u % 4:u % 4 + 1])\
                           .then_inc(sem["masked"], 1)
                    u = s - 2
                    if u0 <= u < u1 and copier(u) == "D":
                        w = UNITS[u]
                        dve.wait_ge(sem["probs_t"], u + 1)
                        if u >= 2:
                            dve.wait_ge(sem["applied"], u - 1)
                        n, r = (w["n"], P) if w["n"] >= P else (P, w["n"])
                        dve.tensor_copy(prob_t[0:r, u % 2, 0:n], bank[2 + u % 2][0:r, 0:n]).then_inc(sem["copied_d"], 1)
                    u = s - 4
                    if u0 <= u < u1 and UNITS[u]["last"]:
                        empty(UNITS[u]["pas"])

            def empty(q):
                w = PASSES[q]
                n, wd = w["n"], w["width"]
                dve.wait_ge(sem["applied"], w["last"] + 1)
                o = bank[4 + q % 2][:, 0:n * wd].rearrange("p (h d) -> p h d", h=n)
                y = w["y"].rearrange("p (h d) -> p h d", h=n)
                r = rsum[:, q % 2, 0:n]
                step(dve.reciprocal(r, sums[:, q % 2, 0:n]))
                if w["kind"] == "g":
                    step(dve.tensor_tensor(r, r, w["gate"], ALU.mult))
                rb = r.unsqueeze(2).to_broadcast([P, n, wd])
                if w["kind"] == "z" or w["first"]:
                    step(dve.tensor_tensor(y, o, rb, ALU.mult))
                else:
                    t = junk2[:, 0:n * wd].rearrange("p (h d) -> p h d", h=n)
                    step(dve.tensor_tensor(t, o, rb, ALU.mult))
                    step(dve.tensor_tensor(y, y, t, ALU.add))
                if w["kind"] == "z":
                    step(dve.tensor_tensor(w["y"], w["y"], w["z"], ALU.mult))
                dve.sem_inc(sem["o_emptied"], 1)

            attention("a")
            dve.sem_inc(sem["y_ready"], 1)
            dve.sem_inc(sem["ready_for_t"], 1)
            for name, parts, v, n in (("cq", (cq_hi, cq_lo), "cq", 3), ("ckv", (ckv_hi, ckv_lo), "ckv", 2)):
                for k in range(n):
                    b = group_wait(name, k)
                    dve.wait_ge(sem["group_a"], groups_emptied("A", GROUPS[name] + k))
                    dve.scalar_tensor_tensor(parts[1][:, k, :], b[:], vec[:, VEC[v] + k:VEC[v] + k + 1],
                                             parts[0][:, k, :].bitcast(F32), ALU.mult, ALU.subtract)\
                       .then_inc(sem["group_d"], 1)
            dve.wait_ge(sem["emptied_a"], strips_emptied("A", STRIP_UQ + 1))
            dve.wait_ge(sem["pair_used"], strip_end(STRIP_MERGE - 1))
            head_norm(heads(QB, 8, 96), 8, 96, rows["qb"][0])
            dve.wait_ge(sem["emptied_a"], strips_emptied("A", STRIP_UKV + 1))
            kb = heads(KB, 8, 96)
            dve.tensor_copy(kb[:, :, :, 0:64], proj[:, :, KVB:KVB + D].rearrange("p t (h d) -> p t h d", h=8)[:, :, :, 0:64])
            step(dve.tensor_copy(kb[:, :, :, 64:96], proj[:, :, KR:KR + 32].unsqueeze(2).to_broadcast([P, TT, 8, 32])))
            head_norm(kb, 8, 96, rows["kb"][0])
            step(rotate_heads(QB, 8, 96, 64, 16, cosb, sinb, rot_scratch(512)))
            step(rotate_heads(KB, 8, 96, 64, 16, cosb, sinb, rot_scratch(512)))
            dve.sem_inc(sem["ready_for_t"], 1)
            attention("b0")
            attention("b1")
            dve.sem_inc(sem["y_ready"], 1)
            attention("m")
            dve.sem_inc(sem["y_ready"], 1)

            def cols(c, m):
                return proj[:, m // 2, c + S * (m % 2):c + S * (m % 2) + S]

            def weigh(strip, first, gated, merged):
                b = strip % 2
                banks = strip_wait(0, lambda j: strip)
                dve.wait_ge(sem["emptied_a"], strips_emptied("A", strip - 2))
                for m in range(4):
                    g = cols(gated, 4 * b + m)
                    o = cols(merged, 4 * b + m) if first else g
                    ins = dve.scalar_tensor_tensor(o, g, 1.0, banks[m][:], ALU.add, ALU.mult)
                ins.then_inc(sem["emptied_d"], 1)
                dve.wait_ge(sem["emptied_d"], strips_emptied("D", strip))
                if not first:
                    for m in range(4):
                        o = cols(merged, 4 * b + m)
                        ins = dve.tensor_tensor(o, o, cols(gated, 4 * b + m), ALU.add)
                    step(ins)
                dve.sem_inc(sem["gated"], 1)

            def merged_lo(c, n):
                dve.sem_inc(sem["merged_in"], 1)
                for t in range(TT):
                    dve.wait_ge(sem["mhi"], 4 * n + t + 1)
                    dve.scalar_tensor_tensor(
                        xt_lo[:, 2 * t:2 * t + 2, :], proj[:, t, c:c + D].rearrange("p (a n) -> p a n", a=2), 0.5,
                        xt_hi[:, 2 * t:2 * t + 2, :].bitcast(F32), ALU.mult, ALU.subtract).then_inc(sem["mlo"], 1)

            def add_strip(i, s, half_of):
                banks = strip_wait(i, s)
                for t in range(TT):
                    v = proj[:, t, XRES + S * half_of:XRES + S * half_of + S]
                    ins = dve.tensor_tensor(v, v, banks[t][:], ALU.add)
                ins.then_inc(sem["emptied_d"], 1)

            for n, c in enumerate((YTA, YTB, YTM)):
                dve.wait_ge(sem["ys_hi"], n + 1)
                dve.tensor_tensor(ys[n % 2][1][:], proj[:, :, c:c + S], ys[n % 2][0][:].bitcast(F32), ALU.subtract)\
                   .then_inc(sem["ys_lo"], 1)
                for b in range(2):
                    weigh(STRIP_MERGE + 4 * n + 2 + b, n == 0, GATED, MERGED)
            merged_lo(MERGED, 0)
            dve.wait_ge(sem["xres_in"], 16)
            for b in range(2):
                add_strip(0, lambda j: STRIP_OUT1 + b, b)

            def norm_x(n, strips, scratch, squares):
                dve.wait_ge(sem["emptied_d"], strips_emptied("D", strips - 1))
                for t in (0, 2):
                    v = proj[:, t, XRES:XRES + D]
                    step(dve.tensor_tensor_reduce(scratch(t), v, v, 1.0, 0.0, ALU.mult, ALU.add, stat[:, t:t + 1]))
                dve.wait_ge(sem["squares"], squares)
                inv_rms(4, D)

            def norm_to_xt(name, v):
                for t in range(TT):
                    dve.tensor_scalar(proj[:, t, 0:D], proj[:, t, XRES:XRES + D], rstd[:, t:t + 1], None, ALU.mult)\
                       .then_inc(sem["xs_ready"], 1)
                for k in range(KT):
                    b = group_wait(name, k)
                    dve.wait_ge(sem["group_a"], groups_emptied("A", GROUPS[name] + k))
                    dve.scalar_tensor_tensor(xt_lo[:, k, :], b[:], vec[:, v + k:v + k + 1], xt_hi[:, k, :].bitcast(F32),
                                             ALU.mult, ALU.subtract).then_inc(sem["group_d"], 1)

            norm_x(0, STRIP_IN2, lambda t: junk[:, 0:D], 5)
            norm_to_xt("x2", VEC["mix"])

            def columns2_in(c):
                dve.wait_ge(sem["emptied_a"], strips_emptied("A", STRIP_IN2 - 1) + -(-c // IN2_W))

            columns2_in(KC2)
            for t in range(TT):
                v = proj[:, t, Q2:Q2 + D].rearrange("p (h d) -> p h d", h=16)
                c, s_ = (col[k][:, 32 * t:32 * t + 32].unsqueeze(1).to_broadcast([P, 16, 32]) for k in ("cos2", "sin2"))
                k = [rot_q[:, j, :].rearrange("p (h n) -> p h n", h=16) for j in range(4)]
                step(rotate(v[:, :, 0:32], v[:, :, 32:64], c, s_, k[0:2], k[2:4]))
            columns2_in(GATES2)
            cos2, sin2 = (col[k].rearrange("p (t n) -> p t n", t=TT) for k in ("cos2", "sin2"))
            for c in (KS2, KW2):
                step(rotate_heads(c, 2, 64, 0, 32, cos2, sin2, [rot_q[:, j, 0:256] for j in range(4)]))
            dve.wait_ge(sem["tanh_out"], 1)
            step(dve.tensor_scalar(gsig[:], gsig[:], 1.0, 0.5, ALU.add, ALU.mult))
            step(dve.tensor_tensor(gsig[:, :, 0:48:3], gsig[:, :, 0:48:3],
                                   col["anyc"].unsqueeze(2).to_broadcast([P, TT, 16]), ALU.mult))
            dve.sem_inc(sem["ready_for_t"], 1)

            for k, (name, pe_col) in enumerate((("ck", VEC["pek"]), ("cv", VEC["pev"]))):
                b = group_wait(name, 0)
                for par in range(2):
                    for g in range(2):
                        r = slice(64 * par, 64 * par + 64)
                        src = b[64 * g:64 * g + 64, :].rearrange("p (n l two) -> p two l n", l=8, two=2)[:, par]
                        lo = src[:, :, 0:NCMP], src[:, :, 1:NCMP + 1]
                        for k2 in range(2):
                            c = pe_col + 8 * k2
                            ins = dve.tensor_tensor(flat[r, 8 * k2:8 * k2 + 8, g, :], lo[k2],
                                                    vec[r, c:c + 8].unsqueeze(2).to_broadcast([64, 8, NCMP]), ALU.add)
                ins.then_inc(sem["group_d"], 1)
                b = group_wait(name + "h", 0)
                dve.tensor_copy(hid[0:62, 0, :], b[0:62, 0:256]).then_inc(sem["group_d"], 1)
                dve.wait_ge(sem["group_d"], groups_emptied("D", GROUPS[name + "h"]))
                h, s_ = hid[0:62, 0, :], hid[0:62, 1, :]
                step(dve.tensor_tensor(s_, h, h, ALU.mult))
                step(dve.tensor_scalar(s_, s_, 0.044715, 1.0, ALU.mult, ALU.add))
                dve.tensor_tensor(s_, s_, h, ALU.mult).then_inc(sem["tanh_in"], 1)
                dve.wait_ge(sem["tanh_out"], k + 2)
                dve.scalar_tensor_tensor(hid[0:62, 2 + k, :], s_, 1.0, h, ALU.add, ALU.mult).then_inc(sem["hid_in"], 1)
                dve.wait_ge(sem["hid_in"], k + 1)
            for k, name in enumerate(("kcmp", "vcmp")):
                b = group_wait(name, 0)
                dve.tensor_copy(kcv[0:NCMP, k], b[0:NCMP, 0:128].rearrange("p (g d) -> p g d", g=2)).then_inc(sem["group_d"], 1)
                dve.wait_ge(sem["group_d"], groups_emptied("D", GROUPS[name]))
            c, s_ = (col[k][0:NCMP, :].unsqueeze(1).to_broadcast([NCMP, 2, 32]) for k in ("cosc", "sinc"))
            k = [rot_c[0:NCMP, j, :].rearrange("p (g n) -> p g n", g=2) for j in range(4)]
            step(rotate(kcv[0:NCMP, 0, :, 0:32], kcv[0:NCMP, 0, :, 32:64], c, s_, k[0:2], k[2:4]))
            dve.sem_inc(sem["ready_for_t"], 1)
            attention("n0")
            attention("n1")
            dve.sem_inc(sem["y_ready"], 1)
            for k in range(KT):
                b = group_wait("yn", k)
                dve.wait_ge(sem["group_a"], groups_emptied("A", GROUPS["yn"] + k))
                dve.tensor_tensor(yn_lo[:, k, :], b[:], yn_hi[:, k, :].bitcast(F32), ALU.subtract).then_inc(sem["group_d"], 1)

            dve.wait_ge(sem["ys_hi"], 4)
            dve.tensor_tensor(projr[:, :, YS2 + S:YS2 + 2 * S], proj[:, :, U2:U2 + S],
                              projr[:, :, YS2:YS2 + S].bitcast(F32), ALU.subtract).then_inc(sem["ys_lo"], 1)
            for n in range(2):
                for b in range(2):
                    weigh(STRIP_M2 + 4 * n + 2 + b, n == 0, GATED2, MERGED2)
            merged_lo(MERGED2, 1)
            for b in range(2):
                add_strip(0, lambda j: STRIP_OUT2 + b, b)
            norm_x(1, STRIP_FF, lambda t: proj[:, t, D:2 * D], 7)
            norm_to_xt("x3", VEC["mlp"])

            relu = proj[:, :, D:D + S]
            square = proj[:, :, D + S:D + 2 * S]

            def hidden(i, parity, f):
                dve.wait_ge(sem["emptied_a"], at(i, lambda j: strips_emptied("A", STRIP_FF - 1) + f(j) + 1))
                wait(dve, sem["h_hi"], at(i, f))
                wait(dve, sem["h_lo"], at(i, f))
                dve.tensor_tensor(square, relu, relu, ALU.mult).then_inc(sem["sq_out"], 1)
                dve.wait_ge(sem["h_hi"], at(i, lambda j: f(j) + 1))
                dve.tensor_tensor(ys[parity][1][:], square, ys[parity][0][:].bitcast(F32), ALU.subtract)\
                   .then_inc(sem["h_lo"], 1)

            def ff_step(i, parity, t):
                hidden(i, 1 - parity, lambda j: t(j) + 1)
                for b in range(2):
                    add_strip(i, lambda j: STRIP_FF + 2 + b + 3 * t(j), b)
            hidden(0, 0, lambda j: 0)
            ff_step(0, 0, lambda j: 0)
            with dve.Fori(1, 4) as i:
                ff_step(i, 1, lambda j: 2 * j - 1)
                ff_step(i, 0, lambda j: 2 * j)
            for b in range(2):
                add_strip(0, lambda j: STRIP_FF + 22 + b, b)
            norm_x(2, len(STRIPS), lambda t: proj[:, t, D:2 * D], 9)
            dve.wait_ge(sem["fin_in"], 16)
            for t in range(TT):
                dve.scalar_tensor_tensor(proj[:, t, 0:D], proj[:, t, XRES:XRES + D], rstd[:, t:t + 1], gfin[:],
                                         ALU.mult, ALU.mult).then_inc(sem["x_out"], 1)


_INS = ["x", "mem", "positions", "g_norm", "w_in", "g_qn_a", "g_kn_a", "g_cq", "g_ckv", "w_uq", "w_ukv", "g_qn_b",
        "g_kn_b", "g_mem", "w_mem_kv", "g_qn_m", "g_kn_m", "w_branch", "w_out", "norm_mix_2", "w_in_2", "w_pool_2",
        "pool_scale_2", "pe_k_2", "pe_v_2", "w_ck1_2", "w_ck2_2", "w_cv1_2", "w_cv2_2", "w_proj_pool_2",
        "w_proj_nsa_2", "w_out_2", "norm_mlp_2", "w_ff1_2", "w_ff2_2", "norm_final_2"]


def kernel(**inputs):
    import concourse.bacc as bacc
    from concourse.bass_utils import run_bass_kernel_spmd

    nc = bacc.Bacc("TRN2", target_bir_lowering=False, num_devices=1)
    arrays, args = {}, {}
    for name in _INS:
        a = np.ascontiguousarray(inputs[name])
        arrays[f"in_{name}"] = a
        args[name] = nc.dram_tensor(f"in_{name}", a.shape, mybir.dt.from_np(a.dtype), kind="ExternalInput").ap()
    out = nc.dram_tensor("out_0", (1, S, D), F32, kind="ExternalOutput").ap()
    two_block_kernel(nc, out=out, **args)
    r = run_bass_kernel_spmd(nc, [arrays], core_ids=[0])
    return r.results[0]["out_0"]
```

```python
from contextlib import ExitStack

import numpy as np

import concourse.bass as bass
from concourse import mybir

ALU = mybir.AluOpType
ACT = mybir.ActivationFunctionType
AX = mybir.AxisListType
F32 = mybir.dt.float32
F32R = mybir.dt.float32r
I32 = mybir.dt.int32

P = 128
S = 512
TT = S // P
D = 1024
KT = D // P
NEG = -1e30
TAKEN = -3e38
BIG = 3e38
EPS = 1e-6
TOPK = 128
TWO_PI = 2 * np.pi
ROUND = 1.5 * 2.0 ** 23
PI_LOW = 3.1415925

QA, KA, VA, QI, KI, WI, ZA, CQ, CKV, KR, ZB, QM, ZM, GATES = (
    0, 512, 1024, 1536, 2048, 2112, 2120, 2632, 3016, 3272, 3304, 3816, 4328, 4840)
IN1_W = GATES // 10
KVB, QB, KB, YTA, YTB, YTM = 0, 1024, 1792, 2760, ZB, ZM
GATED, MERGED, XRES = 512, 1536, 3816
U2, Q2, KC2, VC2, KS2, VS2, KW2, VW2, GN2, GATES2 = (
    0, 512, 1536, 1664, 1792, 1920, 2048, 2176, 2304, 2352)
IN2_W = GATES2 // 6
W1C = 2352
YS2, GATED2, MERGED2 = 512, 1536, 2560
NCMP = 31
HEADS = 8
WINDOWS = (2, 4, 8, 16)
SC = 4
LAG_T, LAG_COPY, LAG_PV = 3, 4, 5

PAIR_MEM, PAIR_IN1, PAIR_UQ, PAIR_UKV, PAIR_MERGE, PAIR_OUT1, PAIR_IN2, PAIR_M2, PAIR_OUT2, PAIR_FF = (
    0, 8, 48, 52, 54, 90, 98, 122, 150, 158)
RING = 4

STRIP_MEM, STRIP_IN1, STRIP_UQ, STRIP_UKV, STRIP_MERGE, STRIP_OUT1, STRIP_IN2, STRIP_M2, STRIP_OUT2, STRIP_FF = (
    0, 2, 12, 14, 16, 28, 30, 36, 44, 46)
STRIPS = ("AA" + "A" * 10 + "AA" + "AA" + "AADD" * 3 + "DD" + "A" * 6 + "AADDAADD" + "DD"
          + "A" + "ADD" * 7 + "DD")

PAIRS_OF = [4] * 12 + [2, 2, 1, 1] + [4, 4, 2, 2] * 3 + [4] * 8 + [4, 4, 2, 2, 4, 4, 4, 4] + [4, 4] + [4] + [4, 2, 2] * 7 + [2, 2]

GROUPS = {}
GROUP_OF = []
for _name, _n, _who in (
        ("vec", 1, "A"), ("mem", 4, "AD"), ("x", 8, "AD"), ("iq", 4, "A"), ("ik", 1, "A"),
        ("aq", 4, "A"), ("ak", 4, "A"), ("cq", 3, "AD"), ("ckv", 2, "AD"),
        ("b0", 8, "A"), ("b1", 8, "A"), ("mq", 4, "A"), ("mk", 2, "A"),
        ("x2", 8, "AD"), ("ck", 1, "D"), ("ckh", 1, "D"), ("cv", 1, "D"), ("cvh", 1, "D"),
        ("ckt", 1, "A"), ("cvt", 1, "A"), ("kcmp", 1, "D"), ("vcmp", 1, "D"), ("kct", 1, "A"),
        ("pd", 4, "A"), ("py", 4, "A"),
        ("n0", 6, "A"), ("n1", 6, "A"), ("x3", 8, "AD")):
    GROUPS[_name] = len(GROUP_OF)
    GROUP_OF += [_who] * _n


def groups_emptied(who, through):
    return sum(who in g for g in GROUP_OF[:through + 1])


def strip_end(s):
    return sum(PAIRS_OF[:s + 1])


def strips_emptied(who, through):
    return sum(who == g for g in STRIPS[:through + 1])


def at(i, count):
    if isinstance(i, int):
        return count(i)
    step = count(2) - count(1)
    return i * step + (count(1) - step)


def wait(eng, sem, value):
    if not isinstance(value, int) or value > 0:
        eng.wait_ge(sem, value)


def constants():
    p = np.arange(P)
    out = {"ident": np.eye(P)}
    causal = np.zeros((P, S))
    causal[:, S - P:] = np.where(p[None, :] <= p[:, None], 0.0, NEG)
    out["causal"] = causal
    pos = (np.arange(TT)[None, :] * P + p[:, None]).astype(np.float64)
    inv2 = 10000.0 ** (-np.arange(0, 64, 2) / 64)
    ang = (pos[:, :, None].astype(np.float32) * inv2.astype(np.float32)).astype(np.float64)
    out["cos2"], out["sin2"] = np.cos(ang).reshape(P, -1), np.sin(ang).reshape(P, -1)
    end = p * 16 + 31
    angc = (end[:, None].astype(np.float32) * inv2.astype(np.float32)).astype(np.float64)
    out["cosc"], out["sinc"] = np.cos(angc), np.sin(angc)
    end = np.arange(NCMP) * 16 + 31
    out["cmask"] = np.where(end[None, None, :] <= pos[:, :, None], 0.0, NEG).reshape(P, -1)
    out["anyc"] = (pos >= 31).astype(np.float64)
    inva = 500000.0 ** (-np.arange(0, 16, 2) / 16)
    invb = 500000.0 ** (-np.arange(0, 32, 2) / 32)
    out["inv"] = np.tile(np.concatenate([inva, invb])[None], (P, 1))
    first, rest, halo = (np.zeros((P, 4, n)) for n in (P, P, 16))
    for g, w in enumerate(WINDOWS):
        for t in range(P):
            lo = max(0, t - w + 1)
            first[lo:t + 1, g, t] += 1.0 / min(t + 1, w)
            rest[lo:t + 1, g, t] += 1.0 / w
            first[t, g, t] -= 1.0
            rest[t, g, t] -= 1.0
            if t < w - 1:
                halo[P + t - w + 1:, g, t] = 1.0 / w
    out["pool0"], out["pool1"], out["poolh"] = (a.reshape(P, -1) for a in (first, rest, halo))
    return {k: v.astype(np.float32) for k, v in out.items()}


POOLS = ("pool0", "pool1", "poolh")


def two_block_kernel(
        nc, x, mem, positions, g_norm, w_in, g_qn_a, g_kn_a, g_cq, g_ckv, w_uq, w_ukv, g_qn_b, g_kn_b,
        g_mem, w_mem_kv, g_qn_m, g_kn_m, w_branch, w_out, norm_mix_2, w_in_2, w_pool_2,
        pool_scale_2, pe_k_2, pe_v_2, w_ck1_2, w_ck2_2, w_cv1_2, w_cv2_2, w_proj_pool_2,
        w_proj_nsa_2, w_out_2, norm_mlp_2, w_ff1_2, w_ff2_2, norm_final_2, out):
    with ExitStack() as ctx:
        SIZE = 53100
        arena = ctx.enter_context(nc.sbuf_tensor("arena", [P, SIZE], F32))
        base = nc.sbuf_base - SIZE * 4
        top = [0]

        def place(name, shape, dt=F32, where=None):
            n = int(np.prod(shape[1:]))
            if where is None:
                where = top[0]
                top[0] += -(-n // 8) * 8
                assert top[0] <= SIZE, (name, top[0])
            return nc.alloc_sbuf_tensor_at(name, shape, dt, offset=base + 4 * where)

        proj = place("proj", [P, TT, GATES])
        projr = place("projr", [P, TT, GATES], F32R, where=0)
        xt_hi = place("xt_hi", [P, KT, S], F32R)
        xt_lo = place("xt_lo", [P, KT, S], F32R)
        raw = place("raw", [P, RING, 2, S])
        w_hi = place("w_hi", [P, RING, 2, S], F32R)
        w_lo = place("w_lo", [P, RING, 2, S], F32R)
        E = top[0]
        top[0] += 9216
        mt_hi = place("mt_hi", [P, KT, 256], F32R, where=E)
        mt_lo = place("mt_lo", [P, KT, 256], F32R, where=E + 2048)
        kvm = place("kvm", [P, 2, D], where=E + 4096)
        q_t = place("q_t", [P, 4, S], where=E)
        k_t = place("k_t", [P, 4, S], where=E + 2048)
        z_tanh = [place(f"z_tanh{b}", [P, TT, S], where=E + 2048 * b) for b in range(2)]
        z_tanh.append(proj[:, :, QI:QI + S])
        cq_hi = place("cq_hi", [P, 3, S], F32R, where=E)
        cq_lo = place("cq_lo", [P, 3, S], F32R, where=E + 1536)
        ckv_hi = place("ckv_hi", [P, 2, S], F32R, where=E + 6144)
        ckv_lo = place("ckv_lo", [P, 2, S], F32R, where=E + 7168)
        junk = place("junk", [P, 3072], where=E + 6144)
        sq_q = place("sq_q", [P, TT, 768], where=E)
        sq_k = place("sq_k", [P, TT, S], where=E + 6144)
        prob_t = place("prob_t", [P, 2, S], where=E + 6144)
        sc = place("sc", [P, SC, S], where=E + 7168)
        ys = [[place(f"ys_{part}{b}", [P, 4, S], F32R, where=E + 4096 * b + 2048 * k)
               for k, part in enumerate(("hi", "lo"))] for b in range(2)]
        kd_t = place("kd_t", [P, 2, S], where=E + 2048)
        flat = place("flat", [P, 16, 2, NCMP], where=E + 3072)
        rot_q = place("rot_q", [P, 4, 512], where=E)
        rot_c = place("rot_c", [32, 4, 64], where=E + 4096)
        hid = place("hid", [64, 4, 256], where=E + 5120)
        hid_t = place("hid_t", [P, 2, 2, 62], where=E + 6144)
        pools = place("pools", [P, 1088], where=E + 6144)
        d_t = place("d_t", [P, 4, S], where=E)
        wpool = place("wpool", [P, 4, P], where=E + 2048)
        yn_hi = place("yn_hi", [P, KT, S], F32R, where=E)
        yn_lo = place("yn_lo", [P, KT, S], F32R, where=E + 4096)
        gfin = place("gfin", [P, D], where=E + 8192)

        consts = constants()
        cw = sum(v.shape[1] for k, v in consts.items() if k not in POOLS)
        cst = place("cst", [P, cw])
        col, o = {}, 0
        for k, v in consts.items():
            if k not in POOLS:
                col[k] = cst[:, o:o + v.shape[1]]
                o += v.shape[1]
        ident = col["ident"]
        causal = col["causal"]
        cst_d = nc.inline_tensor(np.concatenate([v for k, v in consts.items() if k not in POOLS], 1), "cst_d").ap()
        pool_d = nc.inline_tensor(np.concatenate([consts[k] for k in POOLS], 1), "pool_d").ap()

        vec_rows = place("vec_rows", [73, P], where=E + 8192)
        vec = place("vec", [P, 73])
        rows = {}
        for name, src, n in (("qa", g_qn_a, 64), ("ka", g_kn_a, 64), ("qb", g_qn_b, 96), ("kb", g_kn_b, 96),
                             ("qm", g_qn_m, P), ("km", g_kn_m, P)):
            rows[name] = (place("row_" + name, [P, n]), src)
        A = top[0]
        allow = place("allow", [P, 1280 - P])
        kcv = place("kcv", [32, 2, 2, 64], where=A)
        kc_t = place("kc_t", [P, 2, 32], where=A + 256)
        wc2 = place("wc2", [P, 2, 2, 64], where=A + 320)
        pos_i = place("pos_i", [P, TT], I32)
        pos_f = place("pos_f", [P, TT])
        gained = place("gained", [P, 4, TT, 16], where=top[0])
        ang = place("ang", [P, 4, TT, 24])
        cos1 = place("cos1", [P, TT, 24])
        sin1 = place("sin1", [P, TT, 24])
        stat = place("stat", [P, 64])
        kr_sq = place("kr_sq", [P, TT])
        nope_gain = place("nope_gain", [P, 2])
        rstd = place("rstd", [P, 64])
        half = place("half", [P, 64])
        m8 = place("m8", [P, 8])
        wi8 = place("wi8", [P, TT, HEADS])
        negmax = place("negmax", [P, 4])
        sums = place("sums", [P, SC])
        rsum = place("rsum", [P, SC])
        gsig = place("gsig", [P, TT, 48])

        bank = [ctx.enter_context(nc.psum_tensor(f"bank{i}", [P, 512], F32)) for i in range(8)]

        VEC = dict(norm=0, mem=8, mix=16, mlp=24, pool=32, cq=36, ckv=39, pek=41, pev=57)

        names = (
            "x_in", "mem_in", "cst_in", "vec_in", "pos_in", "row_in", "xres_in", "w1_in", "wc2_in", "w1v_in",
            "pool_in", "wpool_in", "fin_in", "stored",
            "hi_made", "lo_made", "pair_used", "emptied_a", "emptied_d",
            "group_done", "group_a", "group_d",
            "squares", "b_squares", "gain_in", "xs_ready", "stat_ready", "pow_done", "dve_step", "act_step", "sin_in", "sin_out", "half_set",
            "prep", "ready_for_t", "ix_scores", "ix_relu", "ix_acc", "allowed", "z_ready", "z_tanh",
            "zt_done", "zt_emptied",
            "scores", "masked", "exps", "rsums", "normed", "probs_t", "copied_a", "copied_d", "applied", "o_emptied",
            "y_moved", "yn_hi", "yn_lo", "ys_hi", "ys_lo", "gated", "merged_in", "mhi", "mlo", "x2_ready",
            "tanh_in", "tanh_out", "hid_in", "w1_used", "relu_out", "sq_out", "h_hi", "h_lo",
            "x_out")
        sem = {n: ctx.enter_context(nc.semaphore(n)) for n in names}
        landed = [ctx.enter_context(nc.semaphore(f"landed{i}")) for i in range(RING)]

        UNITS, PASSES = [], []
        STAGE_UNITS, STAGE_PASSES = {}, {}

        def add_pass(stage, units, **empty):
            STAGE_UNITS.setdefault(stage, [len(UNITS), 0])
            STAGE_PASSES.setdefault(stage, [len(PASSES), 0])
            for j, u in enumerate(units):
                UNITS.append(dict(dict(start=True, stop=True, gate=None), **u,
                                  pas=len(PASSES), first=j == 0, last=j == len(units) - 1))
            PASSES.append(dict(last=len(UNITS) - 1, **empty))
            STAGE_UNITS[stage][1] = len(UNITS)
            STAGE_PASSES[stage][1] = len(PASSES)

        def causal_mask(i):
            return causal[:, (TT - 1 - i) * P:S]

        def allow_mask(i):
            o = 0 if i == 1 else 256 if i == 2 else 640
            return causal_mask(0) if i == 0 else allow[:, o:o + (i + 1) * P]

        def half_rows(h):
            return slice(64 * (h % 2), 64 * (h % 2) + 64)

        def unit(h, i, c=None, width=64, **rest):
            return dict(rows=half_rows(h) if width == 64 else slice(0, P), cols=slice(i * P, (i + 1) * P), **rest)

        for pair in range(HEADS // 2):
            add_pass("a", [unit(h, i, q=q_t[half_rows(h), pair, i * P:(i + 1) * P],
                                k=k_t[half_rows(h), pair, 0:(i + 1) * P], mask=allow_mask(i), n=(i + 1) * P,
                                v=[proj[:, t, VA + 64 * h:VA + 64 * h + 64] for t in range(i + 1)], scale=64 ** -0.5)
                           for i in range(TT) for h in (2 * pair, 2 * pair + 1)],
                     z=proj[:, pair, ZA:ZA + S], y=proj[:, pair, ZA:ZA + S])
        for pair in range(HEADS // 2):
            add_pass(f"b{pair // 2}", [
                unit(h, i, q=q_t[0:96, h % 4, i * P:(i + 1) * P], k=k_t[0:96, h % 4, 0:(i + 1) * P],
                     mask=causal_mask(i), n=(i + 1) * P, scale=96 ** -0.5,
                     v=[proj[:, t, KVB + 128 * h + 64:KVB + 128 * h + 128] for t in range(i + 1)])
                for i in range(TT) for h in (2 * pair, 2 * pair + 1)],
                     z=proj[:, pair, ZB:ZB + S], y=proj[:, pair, ZB:ZB + S])
        for h in range(4):
            add_pass("m", [unit(h, i, width=P, q=q_t[:, h, i * P:(i + 1) * P], k=k_t[:, h, 0:256],
                                mask=causal[:, 0:256], n=256, scale=P ** -0.5,
                                v=[kvm[:, t, 512 + P * h:512 + P * h + P] for t in range(2)]) for i in range(TT)],
                     z=proj[:, h, ZM:ZM + S], y=proj[:, h, ZM:ZM + S])

        def nsa_unit(g, pair, i, kind, odd):
            h = 2 * pair + odd
            hr = half_rows(h)
            u = dict(q=q_t[hr, pair, i * P:(i + 1) * P], scale=64 ** -0.5, start=kind == 0, stop=kind == 2,
                     gate=gsig[:, i, 24 * g + 3 * h + kind:24 * g + 3 * h + kind + 1])
            if kind == 0:
                u.update(k=kc_t[hr, g, 0:NCMP], n=NCMP, mask=col["cmask"][:, NCMP * i:NCMP * (i + 1)],
                         v=[kcv[0:NCMP, 1, g, :]])
            else:
                vc = (VS2, VW2)[kind - 1] + 64 * g
                u.update(k=kd_t[hr, kind - 1, 0:(i + 1) * P], n=(i + 1) * P, mask=causal_mask(i),
                         v=[proj[:, t, vc:vc + 64] for t in range(i + 1)])
            return unit(h, i, **u)

        for g in range(2):
            for pair in range(HEADS // 2):
                add_pass(f"n{g}", [nsa_unit(g, pair, i, kind, odd)
                                   for i in range(TT) for kind in range(3) for odd in range(2)],
                         z=None, y=proj[:, pair, Q2 + S * g:Q2 + S * g + S])

        def copier(u):
            return "D" if u % 2 == 0 else "A"

        def copies(who, through):
            return sum(copier(u) == who for u in range(through + 1))

        def wait_copied(eng, u):
            if u >= 0:
                eng.wait_ge(sem["copied_d" if copier(u) == "D" else "copied_a"], copies(copier(u), u))

        block = ctx.enter_context(nc.Block())

        def pairs_of(w, c0, n):
            return w.rearrange("(q two p) c -> q p two c", two=2, p=P)

        @block.sync
        def _(sp):
            sp.dma_start(proj[:, 0:2, 2792:2792 + D], mem[0].rearrange("(t p) d -> p t d", p=P)).then_inc(sem["mem_in"], 16)
            sp.dma_start(cst[:], cst_d).then_inc(sem["cst_in"], 16)

            def load(p, slot, src, halves, width):
                if not isinstance(p, int) or p >= RING:
                    sp.wait_ge(sem["hi_made"], p - (RING - 1))
                    sp.wait_ge(sem["lo_made"], p - (RING - 1))
                sp.dma_start(raw[:, slot, 0:halves, 0:width], src).then_inc(landed[slot], 16)

            def stream(p0, w, col0, width, strips, looped=True):
                v = pairs_of(w, 0, 0)
                for q in range(4):
                    load(p0 + q, (p0 + q) % RING, v[q][:, :, col0:col0 + width], 2, width)
                if strips > 1:
                    with sp.Fori(1, strips) as i:
                        for q in range(4):
                            load(i * 4 + (p0 + q), (p0 + q) % RING,
                                 v[q][:, :, bass.ds(i * width + col0, width)], 2, width)

            mem_w = pairs_of(w_mem_kv[0], 0, 0)
            for q in range(4):
                load(PAIR_MEM + q, q, mem_w[q][:, :, 0:S], 2, S)
            sp.dma_start(proj[:, 0:TT, XRES:XRES + D], x[0].rearrange("(t p) d -> p t d", p=P)).then_inc(sem["x_in"], 16)
            for q in range(4):
                load(PAIR_MEM + 4 + q, q, mem_w[q][:, :, S:2 * S], 2, S)
            stream(PAIR_IN1, w_in[0], 0, IN1_W, 10)
            for s in range(2):
                for q, halves in enumerate((2, 1)):
                    p = PAIR_UQ + 2 * s + q
                    src = w_uq[0, 256 * q:256 * q + 128 * halves, 384 * s:384 * s + 384]
                    load(p, p % RING, src.rearrange("(two p) c -> p two c", p=P), halves, 384)
            for s in range(2):
                p = PAIR_UKV + s
                load(p, p % RING, w_ukv[0, :, S * s:S * s + S].rearrange("(two p) c -> p two c", p=P), 2, S)

            def merge_weights(n):
                for s in range(2):
                    for q in range(4):
                        p = n * 12 + (PAIR_MERGE + 4 * s + q)
                        load(p, (PAIR_MERGE + q) % RING,
                             pairs_of(w_in[0], 0, 0)[q][:, :, bass.ds(n * D + (GATES + S * s), S)], 2, S)
                for s in range(2):
                    for q in range(2):
                        p = n * 12 + (PAIR_MERGE + 8 + 2 * s + q)
                        src = w_branch[0].rearrange("n (q two p) c -> (n q) p two c", two=2, p=P)
                        load(p, (PAIR_MERGE + 2 * s + q) % RING, src[n * 2 + q][:, :, S * s:S * s + S], 2, S)

            merge_weights(0)
            with sp.Fori(1, 3) as n:
                merge_weights(n)
            stream(PAIR_OUT1, w_out[0], 0, S, 2)
            sp.wait_ge(sem["pair_used"], strip_end(STRIP_OUT1 - 1))
            sp.dma_start(proj[:, 0:TT, XRES:XRES + D], x[0].rearrange("(t p) d -> p t d", p=P)).then_inc(sem["xres_in"], 16)
            stream(PAIR_IN2, w_in_2[0], 0, IN2_W, 6)
            def w1_load(w, name):
                for t in range(TT):
                    sp.dma_start(proj[:, t, W1C:W1C + D].rearrange("p (l c) -> p l c", l=4),
                                 w[S * t:S * t + S, :].rearrange("(l p) c -> p l c", p=P)).then_inc(sem[name], 16)
            sp.wait_ge(sem["pair_used"], strip_end(STRIP_OUT1 + 2 - 1))
            w1_load(w_ck1_2[0], "w1_in")
            for k, w in enumerate((w_ck2_2, w_cv2_2)):
                sp.dma_start(wc2[:, k], w[0].rearrange("(j p) c -> p j c", p=P)).then_inc(sem["wc2_in"], 16)
            sp.wait_ge(sem["group_done"], GROUPS["ckh"] + 1)
            w1_load(w_cv1_2[0], "w1v_in")
            sp.wait_ge(sem["group_done"], GROUPS["kct"] + 1)
            sp.dma_start(pools[:], pool_d).then_inc(sem["pool_in"], 16)
            sp.dma_start(wpool[:], w_pool_2[0].rearrange("g c d -> c g d")).then_inc(sem["wpool_in"], 16)
            stream(PAIR_M2, w_in_2[0], GATES2, S, 2)
            sp.wait_ge(sem["applied"], len(UNITS))
            sp.dma_start(gfin[:], norm_final_2.rearrange("(o d) -> o d", o=1).to_broadcast([P, D])).then_inc(sem["fin_in"], 16)
            for s in range(2):
                for q in range(2):
                    p = PAIR_M2 + 8 + 2 * s + q
                    load(p, p % RING, pairs_of(w_proj_pool_2[0], 0, 0)[q][:, :, S * s:S * s + S], 2, S)
            stream(PAIR_M2 + 12, w_in_2[0], GATES2 + D, S, 2)
            stream(PAIR_M2 + 20, w_proj_nsa_2[0], 0, S, 2)
            stream(PAIR_OUT2, w_out_2[0], 0, S, 2)

            def ff1_weights(f, p0):
                for q in range(4):
                    load(p0 + q, (PAIR_FF + q) % RING, pairs_of(w_ff1_2[0], 0, 0)[q][:, :, bass.ds(f * S, S)], 2, S)

            def ff2_weights(f, p0):
                for s in range(2):
                    for q in range(2):
                        src = pairs_of(w_ff2_2[0], 0, 0)[f * 2 + q]
                        load(p0 + 2 * s + q, (PAIR_FF + 2 * s + q) % RING, src[:, :, S * s:S * s + S], 2, S)

            ff1_weights(0, PAIR_FF)
            with sp.Fori(1, 8) as f:
                ff1_weights(f, f * 8 + (PAIR_FF - 4))
                ff2_weights(f - 1, f * 8 + PAIR_FF)
            ff2_weights(7, PAIR_FF + 60)
            sp.wait_ge(sem["x_out"], TT)
            sp.dma_start(out[0].rearrange("(t p) d -> p t d", p=P), proj[:, 0:TT, 0:D]).then_inc(sem["stored"], 16)
            sp.wait_ge(sem["stored"], 16)

        @block.gpsimd
        def _(pool):
            pool.memset(nope_gain[64:96, :], 1.0).then_inc(sem["half_set"], 1)
            pool.wait_ge(sem["half_set"], 1)
            pool.memset(half[:], -0.5).then_inc(sem["half_set"], 1)
            pool.wait_ge(sem["half_set"], 2)
            pows = [0]

            def inv_sqrt(n):
                pool.wait_ge(sem["stat_ready"], pows[0] + 1)
                pool.tensor_tensor(rstd[:, 0:n], stat[:, 0:n], half[:, 0:n], ALU.pow).then_inc(sem["pow_done"], 1)
                pows[0] += 1

            def split(p, slot, halves, width):
                pool.wait_ge(sem["hi_made"], p + 1)
                if not isinstance(p, int) or p >= RING:
                    pool.wait_ge(sem["pair_used"], p - (RING - 1))
                pool.tensor_tensor(w_lo[:, slot, 0:halves, 0:width], raw[:, slot, 0:halves, 0:width],
                                   w_hi[:, slot, 0:halves, 0:width].bitcast(F32), ALU.subtract).then_inc(sem["lo_made"], 1)

            def split_run(p0, p1, width):
                if p0 == 0:
                    for q in range(RING):
                        split(q, q, 2, width)
                    p0 = RING
                with pool.Fori(0, (p1 - p0) // RING) as i:
                    for q in range(RING):
                        split(i * RING + (p0 + q), (p0 + q) % RING, 2, width)

            def attention(stage):
                for u in range(*STAGE_UNITS[stage]):
                    w = UNITS[u]
                    v = sc[:, u % SC, 0:w["n"]]
                    pool.wait_ge(sem["rsums"], u + 1)
                    gate = 1.0 if w["gate"] is None else w["gate"]
                    pool.tensor_scalar(v, v, rsum[:, u % SC:u % SC + 1], gate, ALU.mult, ALU.mult)\
                        .then_inc(sem["normed"], 1)

            inv_sqrt(2)
            inv_sqrt(4)
            split_run(PAIR_MEM, PAIR_IN1 + 4, S)
            inv_sqrt(8)
            split_run(PAIR_IN1 + 4, PAIR_IN1 + 16, IN1_W)
            inv_sqrt(32)
            split_run(PAIR_IN1 + 16, PAIR_IN1 + 20, IN1_W)
            inv_sqrt(32)
            split_run(PAIR_IN1 + 20, PAIR_UQ, IN1_W)
            inv_sqrt(8)
            inv_sqrt(16)
            for p in range(PAIR_UQ, PAIR_UKV):
                split(p, p % RING, 2 - p % 2, 384)
            attention("a")
            for p in range(PAIR_UKV, PAIR_MERGE):
                split(p, p % RING, 2, S)
            inv_sqrt(64)
            split_run(PAIR_MERGE, PAIR_MERGE + 4, S)
            attention("b0")
            attention("b1")
            attention("m")
            split_run(PAIR_MERGE + 4, PAIR_IN2, S)
            inv_sqrt(4)
            split_run(PAIR_IN2, PAIR_M2, IN2_W)
            split_run(PAIR_M2, PAIR_M2 + 4, S)
            attention("n0")
            attention("n1")
            split_run(PAIR_M2 + 4, PAIR_FF, S)
            inv_sqrt(4)
            split_run(PAIR_FF, PAIR_FF + 64, S)
            inv_sqrt(4)

        @block.tensor
        def _(pe):
            def group(name, n, work):
                t = GROUPS[name] + n
                if t >= 2:
                    for who, s in (("A", "group_a"), ("D", "group_d")):
                        if who in GROUP_OF[t - 2]:
                            pe.wait_ge(sem[s], groups_emptied(who, t - 2))
                work(bank[6 + t % 2]).then_inc(sem["group_done"], 1)

            def enter_banks(strips):
                for who, s in (("A", "emptied_a"), ("D", "emptied_d")):
                    wait(pe, sem[s], strips_emptied(who, strips - 1))

            def enter_strips(name, passes):
                t = GROUPS[name] - 1
                pe.wait_ge(sem["group_a"], groups_emptied("A", t))
                pe.wait_ge(sem["group_d"], groups_emptied("D", t))
                wait(pe, sem["o_emptied"], passes)

            def transposes(pieces):
                def work(b):
                    o = 0
                    for src, k, m in pieces:
                        ins = pe.transpose(b[0:m, o:o + k], src, ident[0:k, 0:k])
                        o += k
                    return ins
                return work

            def columns(c, n=P):
                return transposes([(proj[:, t, c:c + n], P, n) for t in range(TT)])

            def wait_pair(p):
                pe.wait_ge(sem["hi_made"], p + 1)
                pe.wait_ge(sem["lo_made"], p + 1)

            def free_banks(i, strip):
                s0 = strip(i if isinstance(i, int) else 1) - 2
                if s0 >= 0:
                    who = STRIPS[s0]
                    pe.wait_ge(sem["emptied_a" if who == "A" else "emptied_d"],
                               at(i, lambda j: strips_emptied(who, strip(j) - 2)))

            def strip_products(s, p0, tiles, halves, kt0, x_parts, width, feature_major, first=True, last=True,
                               tok=TT, merged=None):
                x_hi, x_lo = x_parts
                for q in range(tiles):
                    p = p0[q]
                    wait_pair(p[0])
                    if merged is not None:
                        pe.wait_ge(sem["mhi"], merged + q + 1)
                        pe.wait_ge(sem["mlo"], merged + q + 1)
                    slot = p[1]
                    n_half = halves[q]
                    for kk in range(n_half):
                        kt = kt0 + 2 * q + kk
                        st, en = first and q == 0 and kk == 0, last and q == tiles - 1 and kk == n_half - 1
                        wh, wl = w_hi[:, slot, kk, 0:width], w_lo[:, slot, kk, 0:width]
                        for b in range(tok):
                            dst = bank[4 * (s % 2) + b]
                            if feature_major:
                                c = slice(b * P, b * P + P)
                                terms = [(w_hi[:, slot, kk, c], x_hi[:, kt, :]), (w_hi[:, slot, kk, c], x_lo[:, kt, :]),
                                         (w_lo[:, slot, kk, c], x_hi[:, kt, :])]
                                o = dst[:, 0:S]
                            else:
                                c = slice(b * P, b * P + P)
                                terms = [(x_hi[:, kt, c], wh), (x_hi[:, kt, c], wl), (x_lo[:, kt, c], wh)]
                                o = dst[:, 0:width]
                            for j, (lhs, rhs) in enumerate(terms):
                                ins = pe.matmul(o, lhs, rhs, start=st and j == 0, stop=en and j == 2)
                    ins.then_inc(sem["pair_used"], 1)

            def slots(i, p0, n):
                return [(at(i, lambda j, q=q: p0(j) + q), (p0(i if isinstance(i, int) else 1) + q) % RING)
                        for q in range(n)]

            def strip(i, s, p0, n, x_parts, width, feature_major, halves=None, kt0=0, tok=TT, merged=None):
                free_banks(i, s)
                sx = s(i if isinstance(i, int) else 1)
                strip_products(sx, slots(i, p0, n), n, halves or [2] * n, kt0, x_parts, width, feature_major, tok=tok,
                               merged=merged)

            pe.wait_ge(sem["cst_in"], 16)
            pe.wait_ge(sem["vec_in"], 16 * 9)
            group("vec", 0, transposes([(vec_rows[:, :], 73, P)]))
            pe.wait_ge(sem["xs_ready"], 2)
            for k in range(4):
                group("mem", k, transposes([(proj[:, t, 2792 + P * (2 * k + j):2792 + P * (2 * k + j) + P], P, P)
                                            for j in range(2) for t in range(2)]))
            pe.wait_ge(sem["group_a"], groups_emptied("A", GROUPS["mem"] + 3))
            pe.wait_ge(sem["group_d"], groups_emptied("D", GROUPS["mem"] + 3))
            for b in range(2):
                strip(0, lambda j: STRIP_MEM + b, lambda j: PAIR_MEM + 4 * b, 4, (mt_hi, mt_lo), S, False, tok=2)
            pe.wait_ge(sem["xs_ready"], 6)
            for k in range(KT):
                group("x", k, columns(XRES + P * k))
            enter_strips("iq", 0)

            xt = (xt_hi, xt_lo)

            def in1(i):
                for b in range(2):
                    strip(i, lambda j: STRIP_IN1 + 2 * j + b, lambda j: PAIR_IN1 + 8 * j + 4 * b, 4, xt, IN1_W, False)
            in1(0)
            with pe.Fori(1, 3) as i:
                in1(i)

            enter_banks(STRIP_IN1 + 6)
            pe.wait_ge(sem["ready_for_t"], 1)
            for k in range(4):
                group("iq", k, columns(QI + P * k))
            group("ik", 0, transposes([(proj[:, t, KI:KI + 64], P, 64) for t in range(TT)]))
            pe.wait_ge(sem["group_a"], groups_emptied("A", GROUPS["ik"]))
            for n, (i, h) in enumerate((i, h) for i in range(1, TT) for h in range(HEADS)):
                if n >= 2:
                    pe.wait_ge(sem["ix_relu"], n - 1)
                pe.matmul(bank[n % 2][:, 0:(i + 1) * P], q_t[half_rows(h), h // 2, i * P:(i + 1) * P],
                          k_t[half_rows(h), 0, 0:(i + 1) * P], start=True, stop=True).then_inc(sem["ix_scores"], 1)
            pe.wait_ge(sem["ix_relu"], 24)
            with pe.Fori(3, 5) as i:
                in1(i)
            enter_banks(STRIP_UQ)

            pe.wait_ge(sem["z_ready"], 2)
            for k in range(4):
                group("aq", k, columns(QA + P * k))
            for k in range(4):
                group("ak", k, columns(KA + P * k))

            for n, c in enumerate((ZA, ZB, ZM)):
                wait(pe, sem["zt_emptied"], 4 * n)
                pe.wait_ge(sem["z_ready"], n + 1)
                for k in range(4):
                    transposes([(proj[:, t, c + P * k:c + P * k + P], P, P) for t in range(TT)])(bank[k])\
                        .then_inc(sem["zt_done"], 1)

            def attention(stage):
                u0, u1 = STAGE_UNITS[stage]
                for step in range(u0, u1 + LAG_PV):
                    u = step
                    if u < u1:
                        w = UNITS[u]
                        if u >= 2:
                            pe.wait_ge(sem["masked"], u - 1)
                        pe.matmul(bank[u % 2][:, 0:w["n"]], w["q"], w["k"], start=True, stop=True)\
                          .then_inc(sem["scores"], 1)
                    u = step - LAG_T
                    if u0 <= u < u1:
                        w = UNITS[u]
                        pe.wait_ge(sem["normed"], u + 1)
                        wait_copied(pe, u - 2)
                        for t in range(-(-w["n"] // P)):
                            n = min(P, w["n"] - t * P)
                            ins = pe.transpose(bank[2 + u % 2][0:n, t * P:(t + 1) * P],
                                               sc[:, u % SC, t * P:t * P + n], ident)
                        ins.then_inc(sem["probs_t"], 1)
                    u = step - LAG_PV
                    if u0 <= u < u1:
                        w = UNITS[u]
                        wait_copied(pe, u)
                        if w["first"] and w["pas"] >= 2:
                            pe.wait_ge(sem["o_emptied"], w["pas"] - 1)
                        nt = len(w["v"])
                        for t in range(nt):
                            n = min(P, w["n"] - t * P)
                            ins = pe.matmul(bank[4 + w["pas"] % 2][w["rows"], w["cols"]], w["v"][t],
                                            prob_t[0:n, u % 2, t * P:(t + 1) * P],
                                            start=w["start"] and t == 0, stop=w["stop"] and t == nt - 1,
                                            skip_group_check=True)
                        ins.then_inc(sem["applied"], 1)

            pe.wait_ge(sem["group_a"], groups_emptied("A", GROUPS["ak"] + 3))
            pe.wait_ge(sem["zt_emptied"], 12)
            attention("a")

            pe.wait_ge(sem["ready_for_t"], 2)
            for k in range(3):
                group("cq", k, columns(CQ + P * k))
            for k in range(2):
                group("ckv", k, columns(CKV + P * k))
            enter_strips("b0", STAGE_PASSES["a"][1])
            for b in range(2):
                strip(0, lambda j: STRIP_UQ + b, lambda j: PAIR_UQ + 2 * b, 2, (cq_hi, cq_lo), 384, False, halves=[2, 1])
            for b in range(2):
                strip(0, lambda j: STRIP_UKV + b, lambda j: PAIR_UKV + b, 1, (ckv_hi, ckv_lo), S, False)
            enter_banks(STRIP_MERGE)
            pe.wait_ge(sem["ready_for_t"], 3)
            for r in range(2):
                for h in range(4):
                    group(f"b{r}", h, columns(QB + 96 * (4 * r + h), 96))
                for h in range(4):
                    group(f"b{r}", 4 + h, columns(KB + 96 * (4 * r + h), 96))
                pe.wait_ge(sem["group_a"], groups_emptied("A", GROUPS[f"b{r}"] + 7))
                attention(f"b{r}")
            for k in range(4):
                group("mq", k, columns(QM + P * k))
            for k in range(2):
                group("mk", k, transposes([(kvm[:, t, P * (2 * k + j):P * (2 * k + j) + P], P, P)
                                           for j in range(2) for t in range(2)]))
            pe.wait_ge(sem["group_a"], groups_emptied("A", GROUPS["mk"] + 1))
            attention("m")

            enter_strips("x2", STAGE_PASSES["m"][1])

            def merge(n, buf):
                for b in range(2):
                    strip(n, lambda j: STRIP_MERGE + 4 * j + b, lambda j: PAIR_MERGE + 12 * j + 4 * b, 4, xt, S, True)
                pe.wait_ge(sem["ys_hi"], at(n, lambda j: j + 1))
                pe.wait_ge(sem["ys_lo"], at(n, lambda j: j + 1))
                for b in range(2):
                    strip(n, lambda j: STRIP_MERGE + 4 * j + 2 + b, lambda j: PAIR_MERGE + 12 * j + 8 + 2 * b, 2,
                          buf, S, True)
            for n in range(3):
                merge(n, ys[n % 2])
            for b in range(2):
                strip(0, lambda j: STRIP_OUT1 + b, lambda j: PAIR_OUT1 + 4 * b, 4, xt, S, False, merged=0)

            enter_banks(STRIP_IN2)
            pe.wait_ge(sem["xs_ready"], 10)
            for k in range(KT):
                group("x2", k, columns(P * k))
            enter_strips("ck", STAGE_PASSES["m"][1])

            def in2(i):
                for b in range(2):
                    strip(i, lambda j: STRIP_IN2 + 2 * j + b, lambda j: PAIR_IN2 + 8 * j + 4 * b, 4, xt, IN2_W, False)
            in2(0)
            with pe.Fori(1, 3) as i:
                in2(i)

            enter_banks(STRIP_M2)
            pe.wait_ge(sem["ready_for_t"], 4)
            for k, (name, w_in_sem) in enumerate((("ck", "w1_in"), ("cv", "w1v_in"))):
                group(name, 0, columns((KC2, VC2)[k]))
                pe.wait_ge(sem["group_d"], groups_emptied("D", GROUPS[name]))
                pe.wait_ge(sem[w_in_sem], 64)

                def hidden(b):
                    for lp in range(16):
                        c = W1C + 256 * (lp % 4)
                        ins = pe.matmul(b[0:62, 0:256], flat[:, lp].rearrange("p g n -> p (g n)"),
                                        proj[:, lp // 4, c:c + 256], start=lp == 0, stop=lp == 15)
                    return ins
                group(name + "h", 0, hidden)
            for k, name in enumerate(("ckt", "cvt")):
                pe.wait_ge(sem["hid_in"], k + 1)
                group(name, 0, transposes([(hid[0:62, 3, j * P:j * P + P] if k else hid[0:62, 2, j * P:j * P + P], 62, P)
                                           for j in range(2)]))
            pe.wait_ge(sem["wc2_in"], 32)
            for k, name in enumerate(("kcmp", "vcmp")):
                pe.wait_ge(sem["group_a"], groups_emptied("A", GROUPS["ckt"] + k))

                def second(b):
                    for g in range(2):
                        for j in range(2):
                            ins = pe.matmul(b[0:NCMP, 64 * g:64 * g + 64], hid_t[:, k, j, NCMP * g:NCMP * g + NCMP],
                                            wc2[:, k, j, :], start=j == 0, stop=j == 1)
                    return ins
                group(name, 0, second)
            pe.wait_ge(sem["ready_for_t"], 5)

            group("kct", 0, transposes([(kcv[0:NCMP, 0].rearrange("p g d -> p (g d)"), NCMP, P)]))

            pe.wait_ge(sem["pool_in"], 16)
            for g in range(4):
                def means(b):
                    c = slice(U2 + P * g, U2 + P * g + P)
                    for t in range(TT):
                        w = pools[:, (512 if t else 0) + P * g:(512 if t else 0) + P * g + P]
                        pe.matmul(b[:, t * P:t * P + P], proj[:, t, c], w, start=t == 0, stop=False,
                                  skip_group_check=True)
                    for t in range(1, TT):
                        ins = pe.matmul(b[:, t * P:t * P + 16], proj[:, t - 1, c],
                                        pools[:, 1024 + 16 * g:1040 + 16 * g], start=False, stop=t == TT - 1,
                                        skip_group_check=True)
                    return ins
                group("pd", g, means)
            pe.wait_ge(sem["wpool_in"], 16)
            pe.wait_ge(sem["group_a"], groups_emptied("A", GROUPS["pd"] + 3))
            for g in range(4):
                group("py", g, lambda b: pe.matmul(b[:, 0:S], wpool[:, g, :], d_t[:, g, :], start=True, stop=True))

            for g in range(2):
                for k in range(4):
                    group(f"n{g}", k, columns(Q2 + 512 * g + P * k))
                for k, c in enumerate((KS2, KW2)):
                    group(f"n{g}", 4 + k, columns(c))
                pe.wait_ge(sem["group_a"], groups_emptied("A", GROUPS[f"n{g}"] + 5))
                attention(f"n{g}")

            enter_strips("x3", STAGE_PASSES["n1"][1])
            m2 = PAIR_M2
            pool_parts = (projr[:, :, YS2:YS2 + S], projr[:, :, YS2 + S:YS2 + 2 * S])
            for b in range(2):
                strip(0, lambda j: STRIP_M2 + b, lambda j: m2 + 4 * b, 4, xt, S, True)
            pe.wait_ge(sem["ys_hi"], 4)
            pe.wait_ge(sem["ys_lo"], 4)
            for b in range(2):
                strip(0, lambda j: STRIP_M2 + 2 + b, lambda j: m2 + 8 + 2 * b, 2, pool_parts, S, True)
            for b in range(2):
                strip(0, lambda j: STRIP_M2 + 4 + b, lambda j: m2 + 12 + 4 * b, 4, xt, S, True)
            pe.wait_ge(sem["yn_hi"], 1)
            pe.wait_ge(sem["yn_lo"], 1)
            for b in range(2):
                strip(0, lambda j: STRIP_M2 + 6 + b, lambda j: m2 + 20 + 4 * b, 4, (yn_hi, yn_lo), S, True)
            for b in range(2):
                strip(0, lambda j: STRIP_OUT2 + b, lambda j: PAIR_OUT2 + 4 * b, 4, xt, S, False, merged=4)

            enter_banks(STRIP_FF)
            pe.wait_ge(sem["xs_ready"], 14)
            for k in range(KT):
                group("x3", k, columns(P * k))
            pe.wait_ge(sem["group_a"], groups_emptied("A", GROUPS["x3"] + 7))
            pe.wait_ge(sem["group_d"], groups_emptied("D", GROUPS["x3"] + 7))

            def ff_up(f, s, p):
                strip(f, s, p, 4, xt, S, True)

            def ff_down(f, buf, s, p):
                pe.wait_ge(sem["h_hi"], at(f, lambda j: j))
                pe.wait_ge(sem["h_lo"], at(f, lambda j: j))
                for b in range(2):
                    strip(f, lambda j: s(j) + b, lambda j: p(j) + 2 * b, 2, ys[buf], S, False)

            def ff_step(i, parity, t):
                ff_up(i, lambda j: STRIP_FF + 1 + 3 * t(j), lambda j: PAIR_FF + 4 + 8 * t(j))
                pe.wait_ge(sem["h_hi"], at(i, lambda j: t(j) + 1))
                pe.wait_ge(sem["h_lo"], at(i, lambda j: t(j) + 1))
                for b in range(2):
                    strip(i, lambda j: STRIP_FF + 2 + b + 3 * t(j), lambda j: PAIR_FF + 8 + 2 * b + 8 * t(j), 2,
                          ys[parity], S, False)
            ff_up(0, lambda j: STRIP_FF, lambda j: PAIR_FF)
            ff_step(0, 0, lambda j: 0)
            with pe.Fori(1, 4) as i:
                ff_step(i, 1, lambda j: 2 * j - 1)
                ff_step(i, 0, lambda j: 2 * j)
            ff_down(8, 1, lambda j: STRIP_FF + 22, lambda j: PAIR_FF + 60)

        @block.scalar
        def _(act):
            r = 0
            for src in (g_norm[0].rearrange("(r c) -> r c", c=P), g_mem[0].rearrange("(r c) -> r c", c=P),
                        norm_mix_2[0].rearrange("(r c) -> r c", c=P), norm_mlp_2[0].rearrange("(r c) -> r c", c=P),
                        pool_scale_2[0].rearrange("(r c) -> r c", c=P), g_cq[0].rearrange("(r c) -> r c", c=P),
                        g_ckv[0].rearrange("(r c) -> r c", c=P), pe_k_2[0].rearrange("(r two) c -> r (two c)", two=2),
                        pe_v_2[0].rearrange("(r two) c -> r (two c)", two=2)):
                act.dma_start(vec_rows[r:r + src.shape[0], :], src).then_inc(sem["vec_in"], 16)
                r += src.shape[0]
            def part_hi(p, slot, halves, width):
                act.wait_ge(landed[slot], p // RING * 16 + 16 if isinstance(p, int) else (p + (RING - slot)) * 4)
                if not isinstance(p, int) or p >= RING:
                    act.wait_ge(sem["pair_used"], p - (RING - 1))
                act.activation(w_hi[:, slot, 0:halves, 0:width], raw[:, slot, 0:halves, 0:width], ACT.Copy)\
                   .then_inc(sem["hi_made"], 1)

            def his(i, p0, n=RING, width=S):
                for q in range(n):
                    slot = (p0(i if isinstance(i, int) else 1) + q) % RING
                    part_hi(at(i, lambda j: p0(j) + q), slot, 2, width)

            def group_wait(name, n):
                act.wait_ge(sem["group_done"], GROUPS[name] + n + 1)
                return bank[6 + (GROUPS[name] + n) % 2]

            def strip_wait(i, s):
                act.wait_ge(sem["pair_used"], at(i, lambda j: strip_end(s(j))))
                sx = s(i if isinstance(i, int) else 1)
                return bank[4 * (sx % 2):4 * (sx % 2) + 4]

            act.wait_ge(sem["mem_in"], 16)
            act.activation(junk[:, D:2 * D], proj[:, 1, 2792:2792 + D], ACT.Square, accum_out=stat[:, 1:2])\
               .then_inc(sem["squares"], 1)
            act.wait_ge(sem["squares"], 1)
            act.wait_ge(sem["x_in"], 16)
            for t in (1, 3):
                act.activation(junk[:, D:2 * D], proj[:, t, XRES:XRES + D], ACT.Square, accum_out=stat[:, 4 + t:5 + t])\
                   .then_inc(sem["squares"], 1)
                act.wait_ge(sem["squares"], t // 2 + 2)
            his(0, lambda j: PAIR_MEM, 2)
            b = group_wait("vec", 0)
            act.activation(vec[:], b[:, 0:73], ACT.Copy).then_inc(sem["group_a"], 1)
            act.wait_ge(sem["group_a"], 1)
            for k in range(4):
                b = group_wait("mem", k)
                act.mul(mt_hi[:, 2 * k, :], b[:, 0:256], vec[:, 8 + 2 * k:9 + 2 * k])
                act.mul(mt_hi[:, 2 * k + 1, :], b[:, 256:512], vec[:, 9 + 2 * k:10 + 2 * k]).then_inc(sem["group_a"], 1)
            his(0, lambda j: PAIR_MEM + 2, 2)
            act.dma_start(pos_i[:], positions[0].rearrange("(t p) -> p t", p=P), allow_slow_non_contiguous=True)\
               .then_inc(sem["pos_in"], 16)
            for k, src in enumerate((g_qn_b, g_kn_b)):
                act.dma_start(nope_gain[0:64, k:k + 1], src[0, 0:64].rearrange("(p o) -> p o", o=1),
                              allow_slow_non_contiguous=True).then_inc(sem["gain_in"], 16)
            for dst, src in rows.values():
                act.dma_start(dst[:], src.to_broadcast(dst.shape)).then_inc(sem["row_in"], 16)
            his(0, lambda j: PAIR_MEM + 4)
            for b in range(2):
                banks = strip_wait(0, lambda j: STRIP_MEM + b)
                for t in range(2):
                    ins = act.activation(kvm[:, t, S * b:S * b + S], banks[t][:], ACT.Copy)
                ins.then_inc(sem["emptied_a"], 1)
            for k in range(KT):
                b = group_wait("x", k)
                act.mul(xt_hi[:, k, :], b[:], vec[:, k:k + 1]).then_inc(sem["group_a"], 1)

            def empty_in1(i, b):
                banks = strip_wait(i, lambda j: STRIP_IN1 + 2 * j + b)
                for t in range(TT):
                    c = at(i, lambda j: (2 * j + b) * IN1_W)
                    ins = act.activation(proj[:, t, bass.ds(c, IN1_W)], banks[t][:, 0:IN1_W], ACT.Copy)
                ins.then_inc(sem["emptied_a"], 1)
            his(0, lambda j: PAIR_IN1, width=IN1_W)
            act.wait_ge(sem["sin_in"], 1)
            act.activation(sin1[:], ang[:, 1], ACT.Sin).then_inc(sem["sin_out"], 1)
            act.activation(cos1[:], ang[:, 1], ACT.Sin, scale=0.5).then_inc(sem["sin_out"], 1)

            def in1(i, last=False):
                his(i, lambda j: PAIR_IN1 + 8 * j + 4, width=IN1_W)
                empty_in1(i, 0)
                if not last:
                    his(i, lambda j: PAIR_IN1 + 8 * j + 8, width=IN1_W)
                empty_in1(i, 1)
            in1(0)
            with act.Fori(1, 3) as i:
                in1(i)

            for k in range(4):
                b = group_wait("iq", k)
                act.activation(q_t[:, k, :], b[:], ACT.Copy).then_inc(sem["group_a"], 1)
            b = group_wait("ik", 0)
            act.activation(k_t[0:64, 0, :], b[0:64, :], ACT.Copy)
            act.activation(k_t[64:128, 0, :], b[0:64, :], ACT.Copy).then_inc(sem["group_a"], 1)
            for n, i in enumerate(i for i in range(1, TT) for h in range(HEADS)):
                act.wait_ge(sem["ix_scores"], n + 1)
                if n >= 2:
                    act.wait_ge(sem["ix_acc"], n - 1)
                act.activation(sc[:, n % 2, 0:(i + 1) * P], bank[n % 2][:, 0:(i + 1) * P], ACT.Relu,
                               scale=64 ** -0.5).then_inc(sem["ix_relu"], 1)
            act.activation(z_tanh[0][:], proj[:, :, ZA:ZA + S], ACT.Tanh, scale=0.5).then_inc(sem["z_tanh"], 1)
            in1(3)
            act.wait_ge(sem["emptied_a"], STRIP_IN1 + 8)
            act.activation(z_tanh[1][:], proj[:, :, ZB:ZB + S], ACT.Tanh, scale=0.5).then_inc(sem["z_tanh"], 1)
            in1(4, last=True)
            act.wait_ge(sem["emptied_a"], STRIP_IN1 + 10)
            act.activation(z_tanh[2], proj[:, :, ZM:ZM + S], ACT.Tanh, scale=0.5).then_inc(sem["z_tanh"], 1)
            for b in range(2):
                for q in range(2):
                    p = PAIR_UQ + 2 * b + q
                    part_hi(p, p % RING, 2 - q, 384)
            for name, dst in (("aq", q_t), ("ak", k_t)):
                for k in range(4):
                    b = group_wait(name, k)
                    act.activation(dst[:, k, :], b[:], ACT.Copy).then_inc(sem["group_a"], 1)

            for n, c in enumerate((ZA, ZB, ZM)):
                act.wait_ge(sem["zt_done"], 4 * n + 4)
                for k in range(4):
                    act.mul(proj[:, k, c:c + S], bank[k][:], 0.5).then_inc(sem["zt_emptied"], 1)

            def attention(stage):
                u0, u1 = STAGE_UNITS[stage]
                for step in range(u0, u1 + LAG_COPY):
                    u = step - LAG_COPY
                    if u0 <= u < u1 and copier(u) == "A":
                        w = UNITS[u]
                        act.wait_ge(sem["probs_t"], u + 1)
                        if u >= 2:
                            act.wait_ge(sem["applied"], u - 1)
                        n, r = (w["n"], P) if w["n"] >= P else (P, w["n"])
                        act.activation(prob_t[0:r, u % 2, 0:n], bank[2 + u % 2][0:r, 0:n], ACT.Copy)\
                           .then_inc(sem["copied_a"], 1)
                    u = step
                    if u < u1:
                        w = UNITS[u]
                        act.wait_ge(sem["masked"], u + 1)
                        v = sc[:, u % SC, 0:w["n"]]
                        act.activation(v, v, ACT.Exp, scale=-1.0, bias=negmax[:, u % SC:u % SC + 1],
                                       accum_out=sums[:, u % SC:u % SC + 1]).then_inc(sem["exps"], 1)

            attention("a")

            yt = {"ya": proj[:, :, YTA:YTA + S], "yb": proj[:, :, YTB:YTB + S], "ym": proj[:, :, YTM:YTM + S]}

            for k in range(3):
                b = group_wait("cq", k)
                act.mul(cq_hi[:, k, :], b[:], vec[:, VEC["cq"] + k:VEC["cq"] + k + 1]).then_inc(sem["group_a"], 1)
            for k in range(2):
                b = group_wait("ckv", k)
                act.mul(ckv_hi[:, k, :], b[:], vec[:, VEC["ckv"] + k:VEC["ckv"] + k + 1]).then_inc(sem["group_a"], 1)
            act.wait_ge(sem["o_emptied"], STAGE_PASSES["a"][1])
            act.wait_ge(sem["group_d"], groups_emptied("D", GROUPS["ckv"] + 1))
            act.activation(yt["ya"], proj[:, :, ZA:ZA + S], ACT.Copy).then_inc(sem["y_moved"], 1)
            for p in range(PAIR_UKV, PAIR_MERGE):
                part_hi(p, p % RING, 2, S)
            for b in range(2):
                banks = strip_wait(0, lambda j: STRIP_UQ + b)
                for t in range(TT):
                    ins = act.activation(proj[:, t, QB + 384 * b:QB + 384 * b + 384], banks[t][:, 0:384], ACT.Copy)
                ins.then_inc(sem["emptied_a"], 1)
            act.wait_ge(sem["emptied_a"], strips_emptied("A", STRIP_UQ + 1))
            act.activation(sq_q[:], proj[:, :, QB:QB + 768], ACT.Square).then_inc(sem["b_squares"], 1)
            for b in range(2):
                banks = strip_wait(0, lambda j: STRIP_UKV + b)
                for t in range(TT):
                    ins = act.activation(proj[:, t, KVB + S * b:KVB + S * b + S], banks[t][:], ACT.Copy)
                ins.then_inc(sem["emptied_a"], 1)
            act.wait_ge(sem["emptied_a"], strips_emptied("A", STRIP_UKV + 1))
            act.activation(sq_k[:].rearrange("p t (h d) -> p t h d", h=8),
                           proj[:, :, KVB:KVB + D].rearrange("p t (h d) -> p t h d", h=8)[:, :, :, 0:64], ACT.Square)\
               .then_inc(sem["b_squares"], 1)
            act.wait_ge(sem["gain_in"], 32)
            act.wait_ge(sem["half_set"], 1)
            his(0, lambda j: PAIR_MERGE)
            for r in range(2):
                for h in range(8):
                    b = group_wait(f"b{r}", h)
                    dst = q_t if h < 4 else k_t
                    act.mul(dst[0:96, h % 4, :], b[0:96, :], nope_gain[0:96, h // 4:h // 4 + 1]).then_inc(sem["group_a"], 1)
                attention(f"b{r}")
            for k in range(4):
                b = group_wait("mq", k)
                act.activation(q_t[:, k, :], b[:], ACT.Copy).then_inc(sem["group_a"], 1)
            for k in range(2):
                b = group_wait("mk", k)
                act.activation(k_t[:, 2 * k:2 * k + 2, 0:256], b[:].rearrange("p (a n) -> p a n", a=2), ACT.Copy)\
                   .then_inc(sem["group_a"], 1)
            attention("m")

            def merge_act(n, nxt=None):
                for b in range(2):
                    if n or b:
                        his(n, lambda j: PAIR_MERGE + 12 * j + 4 * b)
                    if b == 1:
                        empty_gate(n, 0)
                his(n, lambda j: PAIR_MERGE + 12 * j + 8)
                empty_gate(n, 1)

            def empty_gate(n, b, s0=STRIP_MERGE, per=4, dst=GATED):
                banks = strip_wait(n, lambda j: s0 + per * j + b)
                if b == 0:
                    wait(act, sem["gated"], at(n, lambda j: 2 * j))
                for m in range(4):
                    mt = 4 * b + m
                    ins = act.activation(proj[:, mt // 2, dst + S * (mt % 2):dst + S * (mt % 2) + S],
                                         banks[m][:], ACT.Tanh, scale=0.5)
                ins.then_inc(sem["emptied_a"], 1)

            act.wait_ge(sem["o_emptied"], STAGE_PASSES["m"][1])
            for n, name in enumerate(("ya", "yb", "ym")):
                if n == 2:
                    act.wait_ge(sem["pair_used"], strip_end(STRIP_MERGE + 4 - 1))
                act.activation(ys[n % 2][0][:], yt[name], ACT.Copy).then_inc(sem["ys_hi"], 1)
                merge_act(n)
            his(0, lambda j: PAIR_OUT1)
            act.wait_ge(sem["pair_used"], strip_end(STRIP_OUT1 - 3))
            for t in range(TT):
                act.wait_ge(sem["merged_in"], t // 2 + 1)
                act.mul(xt_hi[:, 2 * t:2 * t + 2, :], proj[:, t, MERGED:MERGED + D].rearrange("p (a n) -> p a n", a=2),
                        0.5).then_inc(sem["mhi"], 1)
            his(0, lambda j: PAIR_OUT1 + 4)

            def normed(name, v):
                for k in range(KT):
                    b = group_wait(name, k)
                    if k == 0:
                        act.wait_ge(sem["pair_used"], strip_end((STRIP_IN2 if name == "x2" else STRIP_FF) - 1))
                    act.mul(xt_hi[:, k, :], b[:], vec[:, v + k:v + k + 1]).then_inc(sem["group_a"], 1)

            act.wait_ge(sem["emptied_d"], strips_emptied("D", STRIP_IN2 - 1))
            his(0, lambda j: PAIR_IN2, width=IN2_W)
            for t in (1, 3):
                act.activation(junk[:, D:2 * D], proj[:, t, XRES:XRES + D], ACT.Square, accum_out=stat[:, t:t + 1])\
                   .then_inc(sem["squares"], 1)
                act.wait_ge(sem["squares"], 3 + t // 2 + 1)
            normed("x2", VEC["mix"])

            def empty_in2(i, b):
                banks = strip_wait(i, lambda j: STRIP_IN2 + 2 * j + b)
                for t in range(TT):
                    c = at(i, lambda j: (2 * j + b) * IN2_W)
                    ins = act.activation(proj[:, t, bass.ds(c, IN2_W)], banks[t][:, 0:IN2_W], ACT.Copy)
                ins.then_inc(sem["emptied_a"], 1)

            def in2(i, last=False):
                his(i, lambda j: PAIR_IN2 + 8 * j + 4, width=IN2_W)
                empty_in2(i, 0)
                if not last:
                    his(i, lambda j: PAIR_IN2 + 8 * j + 8, width=IN2_W)
                empty_in2(i, 1)
            in2(0)
            with act.Fori(1, 2) as i:
                in2(i)
            in2(2, last=True)

            act.wait_ge(sem["emptied_a"], strips_emptied("A", STRIP_M2 - 1))
            act.activation(gsig[:], proj[:, :, GN2:GN2 + 48], ACT.Tanh, scale=0.5).then_inc(sem["tanh_out"], 1)
            for k in range(2):
                act.wait_ge(sem["tanh_in"], k + 1)
                act.activation(hid[0:62, 1, :], hid[0:62, 1, :], ACT.Tanh, scale=(2 / np.pi) ** 0.5)\
                   .then_inc(sem["tanh_out"], 1)
            for k, name in enumerate(("ckt", "cvt")):
                b = group_wait(name, 0)
                act.mul(hid_t[:, k], b[:, 0:124].rearrange("p (j n) -> p j n", j=2), 0.5).then_inc(sem["group_a"], 1)
            b = group_wait("kct", 0)
            for g in range(2):
                for r in (slice(0, 64), slice(64, 128)):
                    ins = act.activation(kc_t[r, g, 0:NCMP], b[64 * g:64 * g + 64, 0:NCMP], ACT.Copy)
            ins.then_inc(sem["group_a"], 1)
            for g in range(4):
                b = group_wait("pd", g)
                act.activation(d_t[:, g, :], b[:], ACT.Copy).then_inc(sem["group_a"], 1)
            for g in range(4):
                b = group_wait("py", g)
                act.mul(proj[:, g, U2:U2 + S], b[:], vec[:, VEC["pool"] + g:VEC["pool"] + g + 1]).then_inc(sem["group_a"], 1)
            his(0, lambda j: PAIR_M2)
            for g in range(2):
                for k in range(4):
                    b = group_wait(f"n{g}", k)
                    act.activation(q_t[:, k, :], b[:], ACT.Copy).then_inc(sem["group_a"], 1)
                for k in range(2):
                    b = group_wait(f"n{g}", 4 + k)
                    act.activation(kd_t[0:64, k, :], b[64 * g:64 * g + 64, :], ACT.Copy)
                    act.activation(kd_t[64:128, k, :], b[64 * g:64 * g + 64, :], ACT.Copy).then_inc(sem["group_a"], 1)
                attention(f"n{g}")
            act.wait_ge(sem["o_emptied"], len(PASSES))
            yn = proj[:, :, Q2:Q2 + D]
            for half_ in range(2):
                ins = act.activation(yn_hi[:, 4 * half_:4 * half_ + 4, :], yn[:, :, S * half_:S * half_ + S], ACT.Copy)
            ins.then_inc(sem["yn_hi"], 1)

            act.wait_ge(sem["yn_lo"], 1)
            act.activation(projr[:, :, YS2:YS2 + S], proj[:, :, U2:U2 + S], ACT.Copy).then_inc(sem["ys_hi"], 1)
            his(0, lambda j: PAIR_M2 + 4)

            def empty_gate2(b, k):
                banks = strip_wait(0, lambda j: STRIP_M2 + 4 * k + b)
                if b == 0 and k == 1:
                    act.wait_ge(sem["gated"], 8)
                for m in range(4):
                    mt = 4 * b + m
                    ins = act.activation(proj[:, mt // 2, GATED2 + S * (mt % 2):GATED2 + S * (mt % 2) + S],
                                         banks[m][:], ACT.Tanh, scale=0.5)
                ins.then_inc(sem["emptied_a"], 1)
            empty_gate2(0, 0)
            his(0, lambda j: PAIR_M2 + 8)
            empty_gate2(1, 0)
            his(0, lambda j: PAIR_M2 + 12)
            his(0, lambda j: PAIR_M2 + 16)
            empty_gate2(0, 1)
            his(0, lambda j: PAIR_M2 + 20)
            empty_gate2(1, 1)
            his(0, lambda j: PAIR_M2 + 24)
            his(0, lambda j: PAIR_OUT2)
            act.wait_ge(sem["pair_used"], strip_end(STRIP_OUT2 - 3))
            for t in range(TT):
                act.wait_ge(sem["merged_in"], 2 + t // 2 + 1)
                act.mul(xt_hi[:, 2 * t:2 * t + 2, :], proj[:, t, MERGED2:MERGED2 + D].rearrange("p (a n) -> p a n", a=2),
                        0.5).then_inc(sem["mhi"], 1)
            his(0, lambda j: PAIR_OUT2 + 4)
            act.wait_ge(sem["emptied_d"], strips_emptied("D", STRIP_FF - 1))
            his(0, lambda j: PAIR_FF)
            for t in (1, 3):
                act.activation(proj[:, t, D:2 * D], proj[:, t, XRES:XRES + D],
                               ACT.Square, accum_out=stat[:, t:t + 1]).then_inc(sem["squares"], 1)
                act.wait_ge(sem["squares"], 5 + t // 2 + 1)
            normed("x3", VEC["mlp"])

            relu = proj[:, :, D:D + S]
            square = proj[:, :, D + S:D + 2 * S]

            def ff_act(i, parity, s, p, f):
                his(i, p)
                empty_up(i, parity, s, f)

            def empty_up(i, parity, s, f):
                banks = strip_wait(i, s)
                wait(act, sem["sq_out"], at(i, lambda j: f(j)))
                for m in range(4):
                    ins = act.activation(relu[:, m, :], banks[m][:], ACT.Relu)
                ins.then_inc(sem["emptied_a"], 1)
                if not (isinstance(i, int) and f(i) < 2):
                    act.wait_ge(sem["pair_used"], at(i, lambda j: PAIR_FF + 12 + 8 * (f(j) - 2)))
                act.wait_ge(sem["sq_out"], at(i, lambda j: f(j) + 1))
                act.activation(ys[parity][0][:], square, ACT.Copy).then_inc(sem["h_hi"], 1)

            his(0, lambda j: PAIR_FF + 4)
            empty_up(0, 0, lambda j: STRIP_FF, lambda j: 0)

            def ff_step(i, parity, t):
                his(i, lambda j: PAIR_FF + 8 + 8 * t(j))
                empty_up(i, 1 - parity, lambda j: STRIP_FF + 1 + 3 * t(j), lambda j: t(j) + 1)
                his(i, lambda j: PAIR_FF + 12 + 8 * t(j))
            ff_step(0, 0, lambda j: 0)
            with act.Fori(1, 4) as i:
                ff_step(i, 1, lambda j: 2 * j - 1)
                ff_step(i, 0, lambda j: 2 * j)
            act.wait_ge(sem["emptied_d"], strips_emptied("D", len(STRIPS) - 1))
            for t in (1, 3):
                act.activation(proj[:, t, D:2 * D], proj[:, t, XRES:XRES + D],
                               ACT.Square, accum_out=stat[:, t:t + 1]).then_inc(sem["squares"], 1)
                act.wait_ge(sem["squares"], 7 + t // 2 + 1)

        @block.vector
        def _(dve):
            steps = [0]

            def step(ins):
                steps[0] += 1
                ins.then_inc(sem["dve_step"], 1)
                dve.wait_ge(sem["dve_step"], steps[0])

            def group_wait(name, n):
                dve.wait_ge(sem["group_done"], GROUPS[name] + n + 1)
                return bank[6 + (GROUPS[name] + n) % 2]

            def strip_wait(i, s):
                dve.wait_ge(sem["pair_used"], at(i, lambda j: strip_end(s(j))))
                sx = s(i if isinstance(i, int) else 1)
                return bank[4 * (sx % 2):4 * (sx % 2) + 4]

            powers = [0]

            def inv_rms(n, width, first=0):
                dve.tensor_scalar(stat[:, 0:n], stat[:, first:first + n], 1.0 / width, EPS, ALU.mult, ALU.add)\
                   .then_inc(sem["stat_ready"], 1)
                powers[0] += 1
                dve.wait_ge(sem["pow_done"], powers[0])

            def head_norm(v, h, d, gain):
                nt = v.shape[1]
                s = junk[:, 0:nt * h * d].rearrange("p (t h d) -> p t h d", t=nt, h=h)
                step(dve.tensor_tensor(s, v, v, ALU.mult))
                step(dve.tensor_reduce(stat[:, 0:nt * h].rearrange("p (t h) -> p t h", t=nt), s, AX.X, ALU.add))
                inv_rms(nt * h, d)
                r = rstd[:, 0:nt * h].rearrange("p (t h) -> p t h", t=nt).unsqueeze(3).to_broadcast([P, nt, h, d])
                step(dve.tensor_tensor(v, v, r, ALU.mult))
                step(dve.tensor_tensor(v, v, gain[:].unsqueeze(1).unsqueeze(1).to_broadcast([P, nt, h, d]), ALU.mult))

            def rotate(a, b, cos, sin, t1, t2):
                dve.tensor_tensor(t1[0], a, cos, ALU.mult)
                dve.tensor_tensor(t1[1], b, sin, ALU.mult)
                dve.tensor_tensor(t2[0], b, cos, ALU.mult)
                step(dve.tensor_tensor(t2[1], a, sin, ALU.mult))
                dve.tensor_tensor(a, t1[0], t1[1], ALU.subtract)
                return dve.tensor_tensor(b, t2[0], t2[1], ALU.add)

            def rotate_heads(c, h, d, r0, n, cos, sin, scratch):
                v = proj[:, :, c:c + h * d].rearrange("p t (h d) -> p t h d", h=h)
                a, b = v[:, :, :, r0:r0 + n], v[:, :, :, r0 + n:r0 + 2 * n]
                k = [scratch[j] .rearrange("p (t h n) -> p t h n", t=TT, h=h) for j in range(4)]
                cb, sb_ = (z.unsqueeze(2).to_broadcast([P, TT, h, n]) for z in (cos, sin))
                return rotate(a, b, cb, sb_, k[0:2], k[2:4])

            def rot_scratch(n):
                return [junk[:, n * j:n * j + n] for j in range(4)]

            dve.wait_ge(sem["mem_in"], 16)
            step(dve.tensor_tensor_reduce(junk[:, 0:D], proj[:, 0, 2792:2792 + D], proj[:, 0, 2792:2792 + D],
                                          1.0, 0.0, ALU.mult, ALU.add, stat[:, 0:1]))
            dve.wait_ge(sem["squares"], 1)
            inv_rms(2, D)
            for t in range(2):
                v = proj[:, t, 2792:2792 + D]
                dve.tensor_scalar(v, v, rstd[:, t:t + 1], None, ALU.mult).then_inc(sem["xs_ready"], 1)
            dve.wait_ge(sem["x_in"], 16)
            for t in (0, 2):
                step(dve.tensor_tensor_reduce(junk[:, 0:D], proj[:, t, XRES:XRES + D], proj[:, t, XRES:XRES + D],
                                              1.0, 0.0, ALU.mult, ALU.add, stat[:, 4 + t:5 + t]))
            dve.wait_ge(sem["squares"], 3)
            dve.wait_ge(sem["xs_ready"], 2)
            inv_rms(4, D, 4)
            for t in range(TT):
                v = proj[:, t, XRES:XRES + D]
                dve.tensor_scalar(v, v, rstd[:, t:t + 1], None, ALU.mult).then_inc(sem["xs_ready"], 1)
            dve.wait_ge(sem["group_a"], 1)
            for k in range(4):
                b = group_wait("mem", k)
                dve.wait_ge(sem["group_a"], groups_emptied("A", GROUPS["mem"] + k))
                for j in range(2):
                    kt = 2 * k + j
                    ins = dve.scalar_tensor_tensor(mt_lo[:, kt, :], b[:, 256 * j:256 * j + 256], vec[:, 8 + kt:9 + kt],
                                                   mt_hi[:, kt, :].bitcast(F32), ALU.mult, ALU.subtract)
                ins.then_inc(sem["group_d"], 1)
            for k in range(KT):
                b = group_wait("x", k)
                dve.wait_ge(sem["group_a"], groups_emptied("A", GROUPS["x"] + k))
                dve.scalar_tensor_tensor(xt_lo[:, k, :], b[:], vec[:, k:k + 1], xt_hi[:, k, :].bitcast(F32),
                                         ALU.mult, ALU.subtract).then_inc(sem["group_d"], 1)

            dve.wait_ge(sem["pos_in"], 16)
            dve.wait_ge(sem["cst_in"], 16)
            step(dve.tensor_copy(pos_f[:], pos_i[:]))
            step(dve.tensor_tensor(ang[:, 0], pos_f[:].unsqueeze(2).to_broadcast([P, TT, 24]),
                                   col["inv"].unsqueeze(1).to_broadcast([P, TT, 24]), ALU.mult))
            step(dve.tensor_scalar(ang[:, 2], ang[:, 0], 1.0 / TWO_PI, ROUND, ALU.mult, ALU.add))
            step(dve.tensor_scalar(ang[:, 2], ang[:, 2], ROUND, None, ALU.subtract))
            c1 = 6.28125
            c2 = float(np.round((TWO_PI - c1) * 2 ** 20) / 2 ** 20)
            c3 = TWO_PI - c1 - c2
            for c, src in ((c1, 0), (c2, 3), (c3, 3)):
                step(dve.scalar_tensor_tensor(ang[:, 3], ang[:, 2], -float(c), ang[:, src], ALU.mult, ALU.add))
            dve.tensor_scalar(ang[:, 1], ang[:, 3], PI_LOW, -PI_LOW, ALU.min, ALU.max).then_inc(sem["sin_in"], 1)
            dve.wait_ge(sem["sin_out"], 2)
            step(dve.tensor_tensor(cos1[:], cos1[:], cos1[:], ALU.mult))
            step(dve.tensor_scalar(cos1[:], cos1[:], -2.0, 1.0, ALU.mult, ALU.add))
            dve.wait_ge(sem["row_in"], 16 * 6)
            cosa, sina = cos1[:, :, 0:8], sin1[:, :, 0:8]
            cosb, sinb = cos1[:, :, 8:24], sin1[:, :, 8:24]
            dve.wait_ge(sem["emptied_a"], STRIP_MEM + 1)
            head_norm(kvm[:, :, 0:512].rearrange("p t (h d) -> p t h d", h=4), 4, P, rows["km"][0])

            def columns_in(c):
                dve.wait_ge(sem["emptied_a"], STRIP_IN1 + -(-c // IN1_W))

            def heads(c, h, d):
                return proj[:, :, c:c + h * d].rearrange("p t (h d) -> p t h d", h=h)

            columns_in(KA)
            head_norm(heads(QA, 8, 64), 8, 64, rows["qa"][0])
            columns_in(VA)
            head_norm(heads(KA, 8, 64), 8, 64, rows["ka"][0])
            step(rotate_heads(QA, 8, 64, 0, 8, cosa, sina, rot_scratch(256)))
            step(rotate_heads(KA, 8, 64, 0, 8, cosa, sina, rot_scratch(256)))
            columns_in(ZA)
            step(rotate_heads(QI, 8, 64, 0, 8, cosa, sina, rot_scratch(256)))
            step(rotate_heads(KI, 1, 64, 0, 8, cosa, sina, rot_scratch(32)))
            step(dve.tensor_scalar(wi8[:], proj[:, :, WI:WI + 8], HEADS ** -0.5, None, ALU.mult))
            dve.sem_inc(sem["ready_for_t"], 1)

            index = {1: allow[:, 0:256], 2: allow[:, 256:640], 3: allow[:, 640:1152]}
            for n, (i, h) in enumerate((i, h) for i in range(1, TT) for h in range(HEADS)):
                dve.wait_ge(sem["ix_relu"], n + 1)
                if h:
                    dve.wait_ge(sem["ix_acc"], n)
                w = (i + 1) * P
                dve.scalar_tensor_tensor(index[i], sc[:, n % 2, 0:w], wi8[:, i, h:h + 1],
                                         causal_mask(i) if h == 0 else index[i], ALU.mult, ALU.add)\
                   .then_inc(sem["ix_acc"], 1)
            dve.wait_ge(sem["ix_acc"], 24)
            for r in range(TOPK // 8):
                for i in range(1, TT):
                    step(dve.max(m8[:], index[i]))
                    step(dve.match_replace(index[i], m8[:], index[i], TAKEN))
            for i in range(1, TT):
                step(dve.tensor_scalar(index[i], index[i], 0.5 * TAKEN, NEG, ALU.is_gt, ALU.mult))
                step(dve.tensor_tensor(index[i], index[i], causal_mask(i), ALU.add))

            def silu(n):
                z = proj[:, :, (ZA, ZB, ZM)[n]:(ZA, ZB, ZM)[n] + S]
                dve.wait_ge(sem["z_tanh"], n + 1)
                dve.scalar_tensor_tensor(z, z_tanh[n][:] if n < 2 else z_tanh[n], 1.0, z, ALU.add, ALU.mult)\
                   .then_inc(sem["z_ready"], 1)

            silu(0)
            silu(1)
            columns_in(KR)
            for n, (c, w) in enumerate(((CQ, 384), (CKV, 256))):
                for t in range(TT):
                    v = proj[:, t, c:c + w]
                    step(dve.tensor_tensor_reduce(junk[:, 0:w], v, v, 1.0, 0.0, ALU.mult, ALU.add,
                                                  stat[:, 4 * n + t:4 * n + t + 1]))
            step(dve.tensor_scalar(stat[:, 0:4], stat[:, 0:4], 256.0 / 384.0, None, ALU.mult))
            inv_rms(8, 256)
            for n, (c, w) in enumerate(((CQ, 384), (CKV, 256))):
                v = proj[:, :, c:c + w]
                step(dve.tensor_tensor(v, v, rstd[:, 4 * n:4 * n + 4].unsqueeze(2).to_broadcast([P, TT, w]), ALU.mult))
            kr = proj[:, :, KR:KR + 32]
            s_ = junk[:, 0:P].rearrange("p (t n) -> p t n", t=TT)
            step(dve.tensor_tensor(s_, kr, kr, ALU.mult))
            step(dve.tensor_reduce(kr_sq[:], s_, AX.X, ALU.add))
            step(dve.tensor_tensor(kr, kr, rows["kb"][0][:, 64:96].unsqueeze(1).to_broadcast([P, TT, 32]), ALU.mult))
            step(rotate_heads(KR, 1, 32, 0, 16, cosb, sinb, rot_scratch(64)))
            g1, g2 = (rows["qb"][0][:, c:c + 16].unsqueeze(1).to_broadcast([P, TT, 16]) for c in (64, 80))
            for k, (z, g) in enumerate(((cosb, g1), (sinb, g2), (cosb, g2), (sinb, g1))):
                step(dve.tensor_tensor(gained[:, k], z, g, ALU.mult))
            columns_in(ZM)
            head_norm(heads(QM, 4, P), 4, P, rows["qm"][0])
            silu(2)

            def attention(stage):
                u0, u1 = STAGE_UNITS[stage]
                for s in range(u0, u1 + LAG_PV + 1):
                    u = s - LAG_COPY
                    if u0 <= u < u1 and copier(u) == "D":
                        w = UNITS[u]
                        dve.wait_ge(sem["probs_t"], u + 1)
                        if u >= 2:
                            dve.wait_ge(sem["applied"], u - 1)
                        n, r = (w["n"], P) if w["n"] >= P else (P, w["n"])
                        dve.tensor_copy(prob_t[0:r, u % 2, 0:n], bank[2 + u % 2][0:r, 0:n]).then_inc(sem["copied_d"], 1)
                    u = s
                    if u < u1:
                        w = UNITS[u]
                        dve.wait_ge(sem["scores"], u + 1)
                        if u >= SC:
                            dve.wait_ge(sem["probs_t"], u - SC + 1)
                        dve.tensor_tensor_reduce(sc[:, u % SC, 0:w["n"]], bank[u % 2][:, 0:w["n"]], w["mask"],
                                                 -w["scale"], BIG, ALU.add, ALU.min, negmax[:, u % SC:u % SC + 1])\
                           .then_inc(sem["masked"], 1)
                    u = s - 1
                    if u0 <= u < u1:
                        dve.wait_ge(sem["exps"], u + 1)
                        dve.reciprocal(rsum[:, u % SC:u % SC + 1], sums[:, u % SC:u % SC + 1]).then_inc(sem["rsums"], 1)
                    u = s - LAG_PV
                    if u0 <= u < u1 and UNITS[u]["last"]:
                        empty(UNITS[u]["pas"])

            def empty(q):
                w = PASSES[q]
                dve.wait_ge(sem["applied"], w["last"] + 1)
                o = bank[4 + q % 2][:]
                if w["z"] is None:
                    dve.tensor_copy(w["y"], o).then_inc(sem["o_emptied"], 1)
                else:
                    dve.tensor_tensor(w["y"], o, w["z"], ALU.mult).then_inc(sem["o_emptied"], 1)

            attention("a")
            dve.sem_inc(sem["ready_for_t"], 1)
            for name, parts, v, n in (("cq", (cq_hi, cq_lo), "cq", 3), ("ckv", (ckv_hi, ckv_lo), "ckv", 2)):
                for k in range(n):
                    b = group_wait(name, k)
                    dve.wait_ge(sem["group_a"], groups_emptied("A", GROUPS[name] + k))
                    dve.scalar_tensor_tensor(parts[1][:, k, :], b[:], vec[:, VEC[v] + k:VEC[v] + k + 1],
                                             parts[0][:, k, :].bitcast(F32), ALU.mult, ALU.subtract)\
                       .then_inc(sem["group_d"], 1)
            dve.wait_ge(sem["b_squares"], 1)
            step(dve.tensor_reduce(stat[:, 0:32].rearrange("p (t h) -> p t h", t=TT),
                                   sq_q[:].rearrange("p t (h d) -> p t h d", h=8), AX.X, ALU.add))
            dve.wait_ge(sem["b_squares"], 2)
            k_stat = stat[:, 32:64].rearrange("p (t h) -> p t h", t=TT)
            step(dve.tensor_reduce(k_stat, sq_k[:].rearrange("p t (h d) -> p t h d", h=8), AX.X, ALU.add))
            step(dve.tensor_tensor(k_stat, k_stat, kr_sq[:].unsqueeze(2).to_broadcast([P, TT, 8]), ALU.add))
            inv_rms(64, 96)
            rq, rk = (rstd[:, 32 * k:32 * k + 32].rearrange("p (t h) -> p t h", t=TT).unsqueeze(3) for k in range(2))
            qb, kb = heads(QB, 8, 96), heads(KB, 8, 96)
            step(dve.tensor_tensor(qb, qb, rq.to_broadcast([P, TT, 8, 96]), ALU.mult))
            dve.wait_ge(sem["y_moved"], 1)
            dve.tensor_tensor(kb[:, :, :, 0:64], heads(KVB, 8, P)[:, :, :, 0:64], rk.to_broadcast([P, TT, 8, 64]), ALU.mult)
            dve.tensor_tensor(kb[:, :, :, 64:96], proj[:, :, KR:KR + 32].unsqueeze(2).to_broadcast([P, TT, 8, 32]),
                              rk.to_broadcast([P, TT, 8, 32]), ALU.mult)
            a, b = qb[:, :, :, 64:80], qb[:, :, :, 80:96]
            g = [gained[:, k].unsqueeze(2).to_broadcast([P, TT, 8, 16]) for k in range(4)]
            t = [z.rearrange("p (t h n) -> p t h n", t=TT, h=8) for z in rot_scratch(512)]
            dve.tensor_tensor(t[0], a, g[0], ALU.mult)
            dve.tensor_tensor(t[1], b, g[1], ALU.mult)
            dve.tensor_tensor(t[2], b, g[2], ALU.mult)
            step(dve.tensor_tensor(t[3], a, g[3], ALU.mult))
            dve.tensor_tensor(a, t[0], t[1], ALU.subtract)
            step(dve.tensor_tensor(b, t[2], t[3], ALU.add))
            dve.sem_inc(sem["ready_for_t"], 1)
            attention("b0")
            attention("b1")
            attention("m")

            def cols(c, m):
                return proj[:, m // 2, c + S * (m % 2):c + S * (m % 2) + S]

            def weigh(strip, first, gated, merged):
                b = strip % 2
                banks = strip_wait(0, lambda j: strip)
                dve.wait_ge(sem["emptied_a"], strips_emptied("A", strip - 2))
                for m in range(4):
                    g = cols(gated, 4 * b + m)
                    o = cols(merged, 4 * b + m) if first else g
                    ins = dve.scalar_tensor_tensor(o, g, 1.0, banks[m][:], ALU.add, ALU.mult)
                ins.then_inc(sem["emptied_d"], 1)
                dve.wait_ge(sem["emptied_d"], strips_emptied("D", strip))
                if not first:
                    for m in range(4):
                        o = cols(merged, 4 * b + m)
                        ins = dve.tensor_tensor(o, o, cols(gated, 4 * b + m), ALU.add)
                    step(ins)
                dve.sem_inc(sem["gated"], 1)

            def merged_lo(c, n, b):
                dve.sem_inc(sem["merged_in"], 1)
                for t in (2 * b, 2 * b + 1):
                    dve.wait_ge(sem["mhi"], 4 * n + t + 1)
                    dve.scalar_tensor_tensor(
                        xt_lo[:, 2 * t:2 * t + 2, :], proj[:, t, c:c + D].rearrange("p (a n) -> p a n", a=2), 0.5,
                        xt_hi[:, 2 * t:2 * t + 2, :].bitcast(F32), ALU.mult, ALU.subtract).then_inc(sem["mlo"], 1)

            def add_strip(i, s, half_of):
                banks = strip_wait(i, s)
                for t in range(TT):
                    v = proj[:, t, XRES + S * half_of:XRES + S * half_of + S]
                    ins = dve.tensor_tensor(v, v, banks[t][:], ALU.add)
                ins.then_inc(sem["emptied_d"], 1)

            for n, c in enumerate((YTA, YTB, YTM)):
                dve.wait_ge(sem["ys_hi"], n + 1)
                dve.tensor_tensor(ys[n % 2][1][:], proj[:, :, c:c + S], ys[n % 2][0][:].bitcast(F32), ALU.subtract)\
                   .then_inc(sem["ys_lo"], 1)
                for b in range(2):
                    weigh(STRIP_MERGE + 4 * n + 2 + b, n == 0, GATED, MERGED)
                    if n == 2:
                        merged_lo(MERGED, 0, b)
            dve.wait_ge(sem["xres_in"], 16)
            for b in range(2):
                add_strip(0, lambda j: STRIP_OUT1 + b, b)

            def norm_x(n, strips, scratch, squares):
                dve.wait_ge(sem["emptied_d"], strips_emptied("D", strips - 1))
                for t in (0, 2):
                    v = proj[:, t, XRES:XRES + D]
                    step(dve.tensor_tensor_reduce(scratch(t), v, v, 1.0, 0.0, ALU.mult, ALU.add, stat[:, t:t + 1]))
                dve.wait_ge(sem["squares"], squares)
                inv_rms(4, D)

            def norm_to_xt(name, v):
                for t in range(TT):
                    dve.tensor_scalar(proj[:, t, 0:D], proj[:, t, XRES:XRES + D], rstd[:, t:t + 1], None, ALU.mult)\
                       .then_inc(sem["xs_ready"], 1)
                for k in range(KT):
                    b = group_wait(name, k)
                    dve.wait_ge(sem["group_a"], groups_emptied("A", GROUPS[name] + k))
                    dve.scalar_tensor_tensor(xt_lo[:, k, :], b[:], vec[:, v + k:v + k + 1], xt_hi[:, k, :].bitcast(F32),
                                             ALU.mult, ALU.subtract).then_inc(sem["group_d"], 1)

            norm_x(0, STRIP_IN2, lambda t: junk[:, 0:D], 5)
            norm_to_xt("x2", VEC["mix"])

            def columns2_in(c):
                dve.wait_ge(sem["emptied_a"], strips_emptied("A", STRIP_IN2 - 1) + -(-c // IN2_W))

            columns2_in(KC2)
            for t in range(TT):
                v = proj[:, t, Q2:Q2 + D].rearrange("p (h d) -> p h d", h=16)
                c, s_ = (col[k][:, 32 * t:32 * t + 32].unsqueeze(1).to_broadcast([P, 16, 32]) for k in ("cos2", "sin2"))
                k = [rot_q[:, j, :].rearrange("p (h n) -> p h n", h=16) for j in range(4)]
                step(rotate(v[:, :, 0:32], v[:, :, 32:64], c, s_, k[0:2], k[2:4]))
            columns2_in(GATES2)
            cos2, sin2 = (col[k].rearrange("p (t n) -> p t n", t=TT) for k in ("cos2", "sin2"))
            for c in (KS2, KW2):
                step(rotate_heads(c, 2, 64, 0, 32, cos2, sin2, [rot_q[:, j, 0:256] for j in range(4)]))
            dve.wait_ge(sem["tanh_out"], 1)
            step(dve.tensor_scalar(gsig[:], gsig[:], 1.0, 0.5, ALU.add, ALU.mult))
            step(dve.tensor_tensor(gsig[:, :, 0:48:3], gsig[:, :, 0:48:3],
                                   col["anyc"].unsqueeze(2).to_broadcast([P, TT, 16]), ALU.mult))
            dve.sem_inc(sem["ready_for_t"], 1)

            for k, (name, pe_col) in enumerate((("ck", VEC["pek"]), ("cv", VEC["pev"]))):
                b = group_wait(name, 0)
                for par in range(2):
                    for g in range(2):
                        r = slice(64 * par, 64 * par + 64)
                        src = b[64 * g:64 * g + 64, :].rearrange("p (n l two) -> p two l n", l=8, two=2)[:, par]
                        lo = src[:, :, 0:NCMP], src[:, :, 1:NCMP + 1]
                        for k2 in range(2):
                            c = pe_col + 8 * k2
                            ins = dve.tensor_tensor(flat[r, 8 * k2:8 * k2 + 8, g, :], lo[k2],
                                                    vec[r, c:c + 8].unsqueeze(2).to_broadcast([64, 8, NCMP]), ALU.add)
                ins.then_inc(sem["group_d"], 1)
                b = group_wait(name + "h", 0)
                dve.tensor_copy(hid[0:62, 0, :], b[0:62, 0:256]).then_inc(sem["group_d"], 1)
                dve.wait_ge(sem["group_d"], groups_emptied("D", GROUPS[name + "h"]))
                h, s_ = hid[0:62, 0, :], hid[0:62, 1, :]
                step(dve.tensor_tensor(s_, h, h, ALU.mult))
                step(dve.tensor_scalar(s_, s_, 0.044715, 1.0, ALU.mult, ALU.add))
                dve.tensor_tensor(s_, s_, h, ALU.mult).then_inc(sem["tanh_in"], 1)
                dve.wait_ge(sem["tanh_out"], k + 2)
                dve.scalar_tensor_tensor(hid[0:62, 2 + k, :], s_, 1.0, h, ALU.add, ALU.mult).then_inc(sem["hid_in"], 1)
                dve.wait_ge(sem["hid_in"], k + 1)
            for k, name in enumerate(("kcmp", "vcmp")):
                b = group_wait(name, 0)
                dve.tensor_copy(kcv[0:NCMP, k], b[0:NCMP, 0:128].rearrange("p (g d) -> p g d", g=2)).then_inc(sem["group_d"], 1)
                dve.wait_ge(sem["group_d"], groups_emptied("D", GROUPS[name]))
            c, s_ = (col[k][0:NCMP, :].unsqueeze(1).to_broadcast([NCMP, 2, 32]) for k in ("cosc", "sinc"))
            k = [rot_c[0:NCMP, j, :].rearrange("p (g n) -> p g n", g=2) for j in range(4)]
            step(rotate(kcv[0:NCMP, 0, :, 0:32], kcv[0:NCMP, 0, :, 32:64], c, s_, k[0:2], k[2:4]))
            dve.sem_inc(sem["ready_for_t"], 1)
            attention("n0")
            attention("n1")
            dve.wait_ge(sem["yn_hi"], 1)
            yn = proj[:, :, Q2:Q2 + D]
            for half_ in range(2):
                ins = dve.tensor_tensor(yn_lo[:, 4 * half_:4 * half_ + 4, :], yn[:, :, S * half_:S * half_ + S],
                                        yn_hi[:, 4 * half_:4 * half_ + 4, :].bitcast(F32), ALU.subtract)
            ins.then_inc(sem["yn_lo"], 1)

            dve.wait_ge(sem["ys_hi"], 4)
            dve.tensor_tensor(projr[:, :, YS2 + S:YS2 + 2 * S], proj[:, :, U2:U2 + S],
                              projr[:, :, YS2:YS2 + S].bitcast(F32), ALU.subtract).then_inc(sem["ys_lo"], 1)
            for n in range(2):
                for b in range(2):
                    weigh(STRIP_M2 + 4 * n + 2 + b, n == 0, GATED2, MERGED2)
                    if n == 1:
                        merged_lo(MERGED2, 1, b)
            for b in range(2):
                add_strip(0, lambda j: STRIP_OUT2 + b, b)
            norm_x(1, STRIP_FF, lambda t: proj[:, t, D:2 * D], 7)
            norm_to_xt("x3", VEC["mlp"])

            relu = proj[:, :, D:D + S]
            square = proj[:, :, D + S:D + 2 * S]

            def hidden(i, parity, f):
                dve.wait_ge(sem["emptied_a"], at(i, lambda j: strips_emptied("A", STRIP_FF - 1) + f(j) + 1))
                wait(dve, sem["h_hi"], at(i, f))
                wait(dve, sem["h_lo"], at(i, f))
                dve.tensor_tensor(square, relu, relu, ALU.mult).then_inc(sem["sq_out"], 1)
                dve.wait_ge(sem["h_hi"], at(i, lambda j: f(j) + 1))
                dve.tensor_tensor(ys[parity][1][:], square, ys[parity][0][:].bitcast(F32), ALU.subtract)\
                   .then_inc(sem["h_lo"], 1)

            def ff_step(i, parity, t):
                hidden(i, 1 - parity, lambda j: t(j) + 1)
                for b in range(2):
                    add_strip(i, lambda j: STRIP_FF + 2 + b + 3 * t(j), b)
            hidden(0, 0, lambda j: 0)
            ff_step(0, 0, lambda j: 0)
            with dve.Fori(1, 4) as i:
                ff_step(i, 1, lambda j: 2 * j - 1)
                ff_step(i, 0, lambda j: 2 * j)
            for b in range(2):
                add_strip(0, lambda j: STRIP_FF + 22 + b, b)
            norm_x(2, len(STRIPS), lambda t: proj[:, t, D:2 * D], 9)
            dve.wait_ge(sem["fin_in"], 16)
            for t in range(TT):
                dve.scalar_tensor_tensor(proj[:, t, 0:D], proj[:, t, XRES:XRES + D], rstd[:, t:t + 1], gfin[:],
                                         ALU.mult, ALU.mult).then_inc(sem["x_out"], 1)


_INS = ["x", "mem", "positions", "g_norm", "w_in", "g_qn_a", "g_kn_a", "g_cq", "g_ckv", "w_uq", "w_ukv", "g_qn_b",
        "g_kn_b", "g_mem", "w_mem_kv", "g_qn_m", "g_kn_m", "w_branch", "w_out", "norm_mix_2", "w_in_2", "w_pool_2",
        "pool_scale_2", "pe_k_2", "pe_v_2", "w_ck1_2", "w_ck2_2", "w_cv1_2", "w_cv2_2", "w_proj_pool_2",
        "w_proj_nsa_2", "w_out_2", "norm_mlp_2", "w_ff1_2", "w_ff2_2", "norm_final_2"]


def kernel(**inputs):
    import concourse.bacc as bacc
    from concourse.bass_utils import run_bass_kernel_spmd

    nc = bacc.Bacc("TRN2", target_bir_lowering=False, num_devices=1)
    arrays, args = {}, {}
    for name in _INS:
        a = np.ascontiguousarray(inputs[name])
        arrays[f"in_{name}"] = a
        args[name] = nc.dram_tensor(f"in_{name}", a.shape, mybir.dt.from_np(a.dtype), kind="ExternalInput").ap()
    out = nc.dram_tensor("out_0", (1, S, D), F32, kind="ExternalOutput").ap()
    two_block_kernel(nc, out=out, **args)
    r = run_bass_kernel_spmd(nc, [arrays], core_ids=[0])
    return r.results[0]["out_0"]
```

```python
from contextlib import ExitStack

import numpy as np

import concourse.bass as bass
from concourse import mybir

ALU = mybir.AluOpType
ACT = mybir.ActivationFunctionType
AX = mybir.AxisListType
F32 = mybir.dt.float32
F32R = mybir.dt.float32r
I32 = mybir.dt.int32

P = 128
S = 512
TT = S // P
D = 1024
KT = D // P
NEG = -1e30
TAKEN = -3e38
BIG = 3e38
EPS = 1e-6
TOPK = 128
TWO_PI = 2 * np.pi
ROUND = 1.5 * 2.0 ** 23
PI_LOW = 3.1415925

QA, KA, VA, QI, KI, WI, ZA, CQ, CKV, KR, ZB, QM, ZM, GATES = (
    0, 512, 1024, 1536, 2048, 2112, 2120, 2632, 3016, 3272, 3304, 3816, 4328, 4840)
IN1_W = GATES // 10
KVB, QB, KB, YTA, YTB, YTM = 0, 1024, 1792, 2760, ZB, ZM
GATED, MERGED, XRES = 512, 1536, 3816
U2, Q2, KC2, VC2, KS2, VS2, KW2, VW2, GN2, GATES2 = (
    0, 512, 1536, 1664, 1792, 1920, 2048, 2176, 2304, 2352)
IN2_W = GATES2 // 6
W1C = 2352
POOLC, WPOOLC = 3376, 3648
YS2, GATED2, MERGED2 = 512, 1536, 2560
NCMP = 31
HEADS = 8
WINDOWS = (2, 4, 8, 16)
SC = 4
LAG_T, LAG_PV, LAG_COPY = 4, 6, 4
SCORE_BANKS = (0,1,6,7)

PAIR_MEM, PAIR_IN1, PAIR_UQ, PAIR_UKV, PAIR_MERGE, PAIR_OUT1, PAIR_IN2, PAIR_M2, PAIR_OUT2, PAIR_FF = (
    0, 8, 48, 52, 54, 90, 98, 122, 150, 158)
RING = 4

STRIP_MEM, STRIP_IN1, STRIP_UQ, STRIP_UKV, STRIP_MERGE, STRIP_OUT1, STRIP_IN2, STRIP_M2, STRIP_OUT2, STRIP_FF = (
    0, 2, 12, 14, 16, 28, 30, 36, 44, 46)
STRIPS = ("AA" + "A" * 10 + "AA" + "AA" + "AADD" * 3 + "DD" + "A" * 6 + "AADDAADD" + "DD"
          + "A" + "ADD" * 7 + "DD")

PAIRS_OF = [4] * 12 + [2, 2, 1, 1] + [4, 4, 2, 2] * 3 + [4] * 8 + [4, 4, 2, 2, 4, 4, 4, 4] + [4, 4] + [4] + [4, 2, 2] * 7 + [2, 2]

GROUPS = {}
GROUP_OF = []
for _name, _n, _who in (
        ("vec", 1, "A"), ("mem", 4, "AD"), ("x", 8, "AD"), ("iq", 4, "AD"), ("ik", 1, "AD"),
        ("aq", 4, "A"), ("ak", 4, "A"), ("cq", 3, "AD"), ("ckv", 2, "AD"),
        ("b0", 8, ("A", "D")), ("b1", 8, ("A", "D")), ("mq", 4, "A"), ("mk", 2, "A"),
        ("x2", 8, "AD"), ("ck", 1, "D"), ("cv", 1, "D"), ("pd", 4, "A"), ("py", 4, "A"),
        ("ckh", 1, "D"), ("cvh", 1, "D"), ("ckt", 1, "A"), ("cvt", 1, "A"),
        ("kcmp", 1, "D"), ("vcmp", 1, "D"), ("kct", 1, "A"),
        ("n0", 6, "AD"), ("n1", 6, "AD"), ("x3", 8, "AD")):
    GROUPS[_name] = len(GROUP_OF)
    GROUP_OF += [_who] * _n if isinstance(_who, str) else list(_who) * (_n // 2)


def groups_emptied(who, through):
    return sum(who in g for g in GROUP_OF[:through + 1])


def strip_end(s):
    return sum(PAIRS_OF[:s + 1])


def strips_emptied(who, through):
    return sum(who == g for g in STRIPS[:through + 1])


def at(i, count):
    if isinstance(i, int):
        return count(i)
    step = count(2) - count(1)
    return i * step + (count(1) - step)


def wait(eng, sem, value):
    if not isinstance(value, int) or value > 0:
        eng.wait_ge(sem, value)


def constants():
    p = np.arange(P)
    out = {"ident": np.eye(P)}
    causal = np.zeros((P, S))
    causal[:, S - P:] = np.where(p[None, :] <= p[:, None], 0.0, NEG)
    out["causal"] = causal
    pos = (np.arange(TT)[None, :] * P + p[:, None]).astype(np.float64)
    inv2 = 10000.0 ** (-np.arange(0, 64, 2) / 64)
    ang = (pos[:, :, None].astype(np.float32) * inv2.astype(np.float32)).astype(np.float64)
    out["cos2"], out["sin2"] = np.cos(ang).reshape(P, -1), np.sin(ang).reshape(P, -1)
    end = p * 16 + 31
    angc = (end[:, None].astype(np.float32) * inv2.astype(np.float32)).astype(np.float64)
    out["cosc"], out["sinc"] = np.cos(angc), np.sin(angc)
    end = np.arange(NCMP) * 16 + 31
    out["cmask"] = np.where(end[None, None, :] <= pos[:, :, None], 0.0, NEG).reshape(P, -1)
    out["anyc"] = (pos >= 31).astype(np.float64)
    inva = 500000.0 ** (-np.arange(0, 16, 2) / 16)
    invb = 500000.0 ** (-np.arange(0, 32, 2) / 32)
    out["inv"] = np.tile(np.concatenate([inva, invb])[None], (P, 1))
    first, rest, halo = (np.zeros((P, 4, n)) for n in (P, P, 16))
    for g, w in enumerate(WINDOWS):
        for t in range(P):
            lo = max(0, t - w + 1)
            first[lo:t + 1, g, t] += 1.0 / min(t + 1, w)
            rest[lo:t + 1, g, t] += 1.0 / w
            first[t, g, t] -= 1.0
            rest[t, g, t] -= 1.0
            if t < w - 1:
                halo[P + t - w + 1:, g, t] = 1.0 / w
    out["pool0"], out["pool1"], out["poolh"] = (a.reshape(P, -1) for a in (first, rest, halo))
    return {k: v.astype(np.float32) for k, v in out.items()}


POOLS = ("pool0", "pool1", "poolh")


def two_block_kernel(
        nc, x, mem, positions, g_norm, w_in, g_qn_a, g_kn_a, g_cq, g_ckv, w_uq, w_ukv, g_qn_b, g_kn_b,
        g_mem, w_mem_kv, g_qn_m, g_kn_m, w_branch, w_out, norm_mix_2, w_in_2, w_pool_2,
        pool_scale_2, pe_k_2, pe_v_2, w_ck1_2, w_ck2_2, w_cv1_2, w_cv2_2, w_proj_pool_2,
        w_proj_nsa_2, w_out_2, norm_mlp_2, w_ff1_2, w_ff2_2, norm_final_2, out):
    with ExitStack() as ctx:
        SIZE = 53100
        arena = ctx.enter_context(nc.sbuf_tensor("arena", [P, SIZE], F32))
        base = nc.sbuf_base - SIZE * 4
        top = [0]

        def place(name, shape, dt=F32, where=None):
            n = int(np.prod(shape[1:]))
            if where is None:
                where = top[0]
                top[0] += -(-n // 8) * 8
                assert top[0] <= SIZE, (name, top[0])
            return nc.alloc_sbuf_tensor_at(name, shape, dt, offset=base + 4 * where)

        proj = place("proj", [P, TT, GATES])
        projr = place("projr", [P, TT, GATES], F32R, where=0)
        xt_hi = place("xt_hi", [P, KT, S], F32R)
        xt_lo = place("xt_lo", [P, KT, S], F32R)
        raw = place("raw", [P, RING, 2, S])
        w_hi = place("w_hi", [P, RING, 2, S], F32R)
        w_lo = place("w_lo", [P, RING, 2, S], F32R)
        E = top[0]
        top[0] += 9216
        mt_hi = place("mt_hi", [P, KT, 256], F32R, where=E)
        mt_lo = place("mt_lo", [P, KT, 256], F32R, where=E + 2048)
        kvm = place("kvm", [P, 2, D], where=E + 4096)
        q_parts = place("q_parts", [P, HEADS, S], F32R, where=E)
        ix_k = place("ix_k", [P, 2, S], F32R, where=E + 6144)
        k_parts = place("k_parts", [P, 2, 2, S], F32R, where=E + 4096)
        q_t = place("q_t", [P, 4, S], where=E)
        k_t = place("k_t", [P, 4, S], where=E + 2048)
        z_tanh = [place(f"z_tanh{b}", [P, TT, S], where=E + 2048 * b) for b in range(2)]
        z_tanh.append(proj[:, :, QI:QI + S])
        cq_hi = place("cq_hi", [P, 3, S], F32R, where=E)
        cq_lo = place("cq_lo", [P, 3, S], F32R, where=E + 1536)
        ckv_hi = place("ckv_hi", [P, 2, S], F32R, where=E + 6144)
        ckv_lo = place("ckv_lo", [P, 2, S], F32R, where=E + 7168)
        junk = place("junk", [P, 3072], where=E + 6144)
        sq_q = place("sq_q", [P, TT, 768], where=E)
        rot_b = place("rot_b", [P, 4, S], where=E)
        sq_k = place("sq_k", [P, TT, S], where=E + 6144)
        prob_t = place("prob_t", [P, 2, S], where=E + 6144)
        sc = place("sc", [P, SC, S], where=E + 7168)
        ys = [[place(f"ys_{part}{b}", [P, 4, S], F32R, where=E + 4096 * b + 2048 * k)
               for k, part in enumerate(("hi", "lo"))] for b in range(2)]
        w1v = place("w1v", [P, 16, 256], where=E)
        rot_q = place("rot_q", [P, 4, 512], where=E + 4096)
        rot_k = place("rot_k", [P, 4, 256], where=E + 5120)
        flat = [place("flat_k", [P, 16, 2, NCMP], where=E + 8192), place("flat_v", [P, 16, 2, NCMP], where=E + 4096)]
        hid = place("hid", [64, 4, 256], where=E + 5120)
        d_t = place("d_t", [P, 4, S], where=E + 6144)
        yn_hi = place("yn_hi", [P, KT, S], F32R, where=E)
        yn_lo = place("yn_lo", [P, KT, S], F32R, where=E + 4096)
        gfin = place("gfin", [P, D], where=E + 8192)

        consts = constants()
        cw = sum(v.shape[1] for k, v in consts.items() if k not in POOLS)
        cst = place("cst", [P, cw])
        col, o = {}, 0
        for k, v in consts.items():
            if k not in POOLS:
                col[k] = cst[:, o:o + v.shape[1]]
                o += v.shape[1]
        ident = col["ident"]
        causal = col["causal"]
        cst_d = nc.inline_tensor(np.concatenate([v for k, v in consts.items() if k not in POOLS], 1), "cst_d").ap()
        pool_d = nc.inline_tensor(np.concatenate([consts[k].reshape(P, 4, -1) for k in POOLS], 2), "pool_d").ap()

        vec_rows = place("vec_rows", [73, P], where=E + 8192)
        vec = place("vec", [P, 73])
        rows = {}
        for name, src, n in (("qa", g_qn_a, 64), ("ka", g_kn_a, 64), ("qb", g_qn_b, 96), ("kb", g_kn_b, 96),
                             ("qm", g_qn_m, P), ("km", g_kn_m, P)):
            rows[name] = (place("row_" + name, [P, n]), src)
        A = top[0]
        allow = place("allow", [P, 1280 - P])
        kcv = place("kcv", [32, 2, 2, 64], where=A)
        kc_t = place("kc_t", [P, 2, 32], where=A + 256)
        wc2 = place("wc2", [P, 2, 2, 64], where=A + 320)
        hid_t = place("hid_t", [P, 2, 2, 62], where=A + 576)
        rot_c = place("rot_c", [32, 4, 64], where=A + 832)
        pos_i = place("pos_i", [P, TT], I32)
        pos_f = place("pos_f", [P, TT])
        gained = place("gained", [P, 4, TT, 16], where=top[0])
        ang = place("ang", [P, 4, TT, 24])
        cos1 = place("cos1", [P, TT, 24])
        sin1 = place("sin1", [P, TT, 24])
        stat = place("stat", [P, 64])
        kr_sq = place("kr_sq", [P, TT])
        nope_gain = place("nope_gain", [P, 2])
        rstd = place("rstd", [P, 64])
        half = place("half", [P, 64])
        m8 = place("m8", [P, 8])
        wi8 = place("wi8", [P, TT, HEADS])
        negmax = place("negmax", [P, 4])
        sums = place("sums", [P, SC])
        rsum = place("rsum", [P, SC])
        gsig = place("gsig", [P, TT, 48])

        bank = [ctx.enter_context(nc.psum_tensor(f"bank{i}", [P, 512], F32)) for i in range(8)]

        VEC = dict(norm=0, mem=8, mix=16, mlp=24, pool=32, cq=36, ckv=39, pek=41, pev=57)

        names = (
            "x_in", "mem_in", "cst_in", "vec_in", "pos_in", "row_in", "xres_in", "w1_in", "wc2_in", "w1v_in",
            "pool_in", "wpool_in", "fin_in", "stored",
            "hi_made", "lo_made", "pair_used", "emptied_a", "emptied_d",
            "group_done", "group_a", "group_d",
            "squares", "b_squares", "b_mean", "b_root", "x_added", "gain_in", "xs_ready", "stat_ready", "pow_done", "dve_step", "sin_in", "sin_out", "half_set",
            "ready_for_t", "ix_scores", "ix_relu", "ix_acc", "z_ready", "z_tanh",
            "zt_done", "zt_emptied",
            "scores", "masked", "exps", "rsums", "normed", "probs_t", "copied_a", "copied_d", "applied", "o_emptied",
            "y_moved", "yn_hi", "yn_lo", "ys_hi", "ys_lo", "gated", "merged_in", "mhi", "mlo", 
            "tanh_in", "tanh_out", "flats", "hid_in", "sq_out", "h_hi", "h_lo",
            "x_out")
        sem = {n: ctx.enter_context(nc.semaphore(n)) for n in names}
        landed = [ctx.enter_context(nc.semaphore(f"landed{i}")) for i in range(RING)]

        UNITS, PASSES = [], []
        STAGE_UNITS, STAGE_PASSES = {}, {}

        def add_pass(stage, units, **empty):
            STAGE_UNITS.setdefault(stage, [len(UNITS), 0])
            STAGE_PASSES.setdefault(stage, [len(PASSES), 0])
            for j, u in enumerate(units):
                UNITS.append(dict(dict(start=True, stop=True, gate=None, k_lo=None), **u,
                                  pas=len(PASSES), first=j == 0, last=j == len(units) - 1))
            PASSES.append(dict(last=len(UNITS) - 1, **empty))
            STAGE_UNITS[stage][1] = len(UNITS)
            STAGE_PASSES[stage][1] = len(PASSES)

        def causal_mask(i):
            return causal[:, (TT - 1 - i) * P:S]

        def allow_mask(i):
            o = 0 if i == 1 else 256 if i == 2 else 640
            return causal_mask(0) if i == 0 else allow[:, o:o + (i + 1) * P]

        def half_rows(h):
            return slice(64 * (h % 2), 64 * (h % 2) + 64)

        def unit(h, i, width=64, **rest):
            return dict(rows=half_rows(h) if width == 64 else slice(0, P), cols=slice(i * P, (i + 1) * P), **rest)

        for pair in range(HEADS // 2):
            add_pass("a", [unit(h, i, q=q_t[half_rows(h), pair, i * P:(i + 1) * P],
                                k=k_t[half_rows(h), pair, 0:(i + 1) * P], mask=allow_mask(i), n=(i + 1) * P,
                                v=[proj[:, t, VA + 64 * h:VA + 64 * h + 64] for t in range(i + 1)], scale=64 ** -0.5)
                           for i in range(TT) for h in (2 * pair, 2 * pair + 1)],
                     z=proj[:, pair, ZA:ZA + S], y=proj[:, pair, ZA:ZA + S])
        for pair in range(HEADS // 2):
            add_pass(f"b{pair // 2}", [
                unit(h, i, q=q_t[0:96, h % 4, i * P:(i + 1) * P], k=k_t[0:96, h % 4, 0:(i + 1) * P],
                     mask=causal_mask(i), n=(i + 1) * P, scale=96 ** -0.5,
                     v=[proj[:, t, KVB + 128 * h + 64:KVB + 128 * h + 128] for t in range(i + 1)])
                for i in range(TT) for h in (2 * pair, 2 * pair + 1)],
                     z=proj[:, pair, ZB:ZB + S], y=proj[:, pair, ZB:ZB + S])
        for h in range(4):
            add_pass("m", [unit(h, i, width=P, q=q_t[:, h, i * P:(i + 1) * P], k=k_t[:, h, 0:256],
                                mask=causal[:, 0:256], n=256, scale=P ** -0.5,
                                v=[kvm[:, t, 512 + P * h:512 + P * h + P] for t in range(2)]) for i in range(TT)],
                     z=proj[:, h, ZM:ZM + S], y=proj[:, h, ZM:ZM + S])

        def nsa_unit(g, pair, i, kind, odd):
            h = 2 * pair + odd
            u = dict(q=q_parts[:, h, i * P:(i + 1) * P], scale=64 ** -0.5, start=kind == 0, stop=kind == 2,
                     gate=gsig[:, i, 24 * g + 3 * h + kind:24 * g + 3 * h + kind + 1])
            if kind == 0:
                u.update(q=u["q"].bitcast(F32), k=kc_t[:, g, 0:NCMP], n=NCMP, mask=col["cmask"][:, NCMP * i:NCMP * (i + 1)],
                         v=[kcv[0:NCMP, 1, g, :]])
            else:
                vc = (VS2, VW2)[kind - 1] + 64 * g
                u.update(k=k_parts[:, kind - 1, 0, 0:max(i + 1, 2) * P], k_lo=k_parts[:, kind - 1, 1, 0:max(i + 1, 2) * P], n=(i + 1) * P, mask=causal_mask(i),
                         v=[proj[:, t, vc:vc + 64] for t in range(i + 1)])
            return unit(h, i, **u)

        for g in range(2):
            for pair in range(HEADS // 2):
                add_pass(f"n{g}", [nsa_unit(g, pair, i, kind, odd)
                                   for i in range(TT) for kind in range(3) for odd in range(2)],
                         z=None, y=proj[:, pair, Q2 + S * g:Q2 + S * g + S])

        def copier(u):
            return "D" if u % 2 == 0 else "A"

        def copies(who, through):
            return sum(copier(u) == who for u in range(through + 1))

        def wait_copied(eng, u):
            if u >= 0:
                eng.wait_ge(sem["copied_d" if copier(u) == "D" else "copied_a"], copies(copier(u), u))

        block = ctx.enter_context(nc.Block())

        def pairs_of(w, c0, n):
            return w.rearrange("(q two p) c -> q p two c", two=2, p=P)

        @block.sync
        def _(sp):
            sp.dma_start(proj[:, 0:2, 2792:2792 + D], mem[0].rearrange("(t p) d -> p t d", p=P)).then_inc(sem["mem_in"], 16)
            sp.dma_start(cst[:], cst_d).then_inc(sem["cst_in"], 16)

            def load(p, slot, src, halves, width):
                if not isinstance(p, int) or p >= RING:
                    sp.wait_ge(sem["hi_made"], p - (RING - 1))
                    sp.wait_ge(sem["lo_made"], p - (RING - 1))
                sp.dma_start(raw[:, slot, 0:halves, 0:width], src).then_inc(landed[slot], 16)

            def stream(p0, w, col0, width, strips, looped=True):
                v = pairs_of(w, 0, 0)
                for q in range(4):
                    load(p0 + q, (p0 + q) % RING, v[q][:, :, col0:col0 + width], 2, width)
                if strips > 1:
                    with sp.Fori(1, strips) as i:
                        for q in range(4):
                            load(i * 4 + (p0 + q), (p0 + q) % RING,
                                 v[q][:, :, bass.ds(i * width + col0, width)], 2, width)

            mem_w = pairs_of(w_mem_kv[0], 0, 0)
            sp.wait_ge(sem["vec_in"], 16 * 9)
            for q in range(4):
                load(PAIR_MEM + q, q, mem_w[q][:, :, 0:S], 2, S)
            sp.dma_start(proj[:, 0:TT, XRES:XRES + D], x[0].rearrange("(t p) d -> p t d", p=P)).then_inc(sem["x_in"], 16)
            for q in range(4):
                load(PAIR_MEM + 4 + q, q, mem_w[q][:, :, S:2 * S], 2, S)
            stream(PAIR_IN1, w_in[0], 0, IN1_W, 10)
            for s in range(2):
                for q, halves in enumerate((2, 1)):
                    p = PAIR_UQ + 2 * s + q
                    src = w_uq[0, 256 * q:256 * q + 128 * halves, 384 * s:384 * s + 384]
                    load(p, p % RING, src.rearrange("(two p) c -> p two c", p=P), halves, 384)
            for s in range(2):
                p = PAIR_UKV + s
                load(p, p % RING, w_ukv[0, :, S * s:S * s + S].rearrange("(two p) c -> p two c", p=P), 2, S)

            def merge_weights(n):
                for s in range(2):
                    for q in range(4):
                        p = n * 12 + (PAIR_MERGE + 4 * s + q)
                        load(p, (PAIR_MERGE + q) % RING,
                             pairs_of(w_in[0], 0, 0)[q][:, :, bass.ds(n * D + (GATES + S * s), S)], 2, S)
                for s in range(2):
                    for q in range(2):
                        p = n * 12 + (PAIR_MERGE + 8 + 2 * s + q)
                        src = w_branch[0].rearrange("n (q two p) c -> (n q) p two c", two=2, p=P)
                        load(p, (PAIR_MERGE + 2 * s + q) % RING, src[n * 2 + q][:, :, S * s:S * s + S], 2, S)

            merge_weights(0)
            with sp.Fori(1, 3) as n:
                merge_weights(n)
            stream(PAIR_OUT1, w_out[0], 0, S, 2)
            sp.wait_ge(sem["pair_used"], strip_end(STRIP_OUT1 - 1))
            sp.dma_start(proj[:, 0:TT, XRES:XRES + D], x[0].rearrange("(t p) d -> p t d", p=P)).then_inc(sem["xres_in"], 16)
            stream(PAIR_IN2, w_in_2[0], 0, IN2_W, 3)
            sp.wait_ge(sem["pair_used"], strip_end(STRIP_OUT1 + 2 - 1))
            for t in range(TT):
                sp.dma_start(proj[:, t, W1C:W1C + D].rearrange("p (l c) -> p l c", l=4),
                             w_ck1_2[0, S * t:S * t + S, :].rearrange("(l p) c -> p l c", p=P)).then_inc(sem["w1_in"], 16)
            sp.dma_start(w1v[:], w_cv1_2[0].rearrange("(l p) c -> p l c", p=P)).then_inc(sem["w1v_in"], 16)
            for k, w in enumerate((w_ck2_2, w_cv2_2)):
                sp.dma_start(wc2[:, k], w[0].rearrange("(j p) c -> p j c", p=P)).then_inc(sem["wc2_in"], 16)
            sp.dma_start(proj[:, 0:4, POOLC:POOLC + 272], pool_d).then_inc(sem["pool_in"], 16)
            sp.dma_start(proj[:, 0:4, WPOOLC:WPOOLC + P], w_pool_2[0].rearrange("g c d -> c g d")).then_inc(sem["wpool_in"], 16)
            stream(PAIR_IN2 + 12, w_in_2[0], 3 * IN2_W, IN2_W, 3)
            stream(PAIR_M2, w_in_2[0], GATES2, S, 2)
            sp.wait_ge(sem["applied"], len(UNITS))
            sp.dma_start(gfin[:], norm_final_2.rearrange("(o d) -> o d", o=1).to_broadcast([P, D])).then_inc(sem["fin_in"], 16)
            for s in range(2):
                for q in range(2):
                    p = PAIR_M2 + 8 + 2 * s + q
                    load(p, p % RING, pairs_of(w_proj_pool_2[0], 0, 0)[q][:, :, S * s:S * s + S], 2, S)
            stream(PAIR_M2 + 12, w_in_2[0], GATES2 + D, S, 2)
            stream(PAIR_M2 + 20, w_proj_nsa_2[0], 0, S, 2)
            stream(PAIR_OUT2, w_out_2[0], 0, S, 2)

            def ff1_weights(f, p0):
                for q in range(4):
                    load(p0 + q, (PAIR_FF + q) % RING, pairs_of(w_ff1_2[0], 0, 0)[q][:, :, bass.ds(f * S, S)], 2, S)

            def ff2_weights(f, p0):
                for s in range(2):
                    for q in range(2):
                        src = pairs_of(w_ff2_2[0], 0, 0)[f * 2 + q]
                        load(p0 + 2 * s + q, (PAIR_FF + 2 * s + q) % RING, src[:, :, S * s:S * s + S], 2, S)

            ff1_weights(0, PAIR_FF)
            with sp.Fori(1, 8) as f:
                ff1_weights(f, f * 8 + (PAIR_FF - 4))
                ff2_weights(f - 1, f * 8 + PAIR_FF)
            ff2_weights(7, PAIR_FF + 60)
            for t in range(TT):
                sp.wait_ge(sem["x_out"], t + 1)
                sp.dma_start(out[0, t * P:(t + 1) * P, :], proj[:, t, 0:D]).then_inc(sem["stored"], 16)
            sp.wait_ge(sem["stored"], 16 * TT)

        @block.gpsimd
        def _(pool):
            pool.memset(nope_gain[64:96, :], 1.0).then_inc(sem["half_set"], 1)
            pool.wait_ge(sem["half_set"], 1)
            pool.memset(half[:], -0.5).then_inc(sem["half_set"], 1)
            pool.wait_ge(sem["half_set"], 2)
            pows = [0]

            def inv_sqrt(n):
                pool.wait_ge(sem["stat_ready"], pows[0] + 1)
                pool.tensor_tensor(rstd[:, 0:n], stat[:, 0:n], half[:, 0:n], ALU.pow).then_inc(sem["pow_done"], 1)
                pows[0] += 1

            def split(p, slot, halves, width):
                pool.wait_ge(sem["hi_made"], p + 1)
                if not isinstance(p, int) or p >= RING:
                    pool.wait_ge(sem["pair_used"], p - (RING - 1))
                pool.tensor_tensor(w_lo[:, slot, 0:halves, 0:width], raw[:, slot, 0:halves, 0:width],
                                   w_hi[:, slot, 0:halves, 0:width].bitcast(F32), ALU.subtract).then_inc(sem["lo_made"], 1)

            def split_run(p0, p1, width):
                if p0 == 0:
                    for q in range(RING):
                        split(q, q, 2, width)
                    p0 = RING
                if p0 == p1:
                    return
                with pool.Fori(0, (p1 - p0) // RING) as i:
                    for q in range(RING):
                        split(i * RING + (p0 + q), (p0 + q) % RING, 2, width)

            def attention(stage):
                for u in range(*STAGE_UNITS[stage]):
                    w = UNITS[u]
                    v = sc[:, u % SC, 0:w["n"]]
                    pool.wait_ge(sem["rsums"], u + 1)
                    gate = 1.0 if w["gate"] is None else w["gate"]
                    pool.tensor_scalar(v, v, rsum[:, u % SC:u % SC + 1], gate, ALU.mult, ALU.mult)\
                        .then_inc(sem["normed"], 1)

            inv_sqrt(2)
            split_run(PAIR_MEM, PAIR_MEM + 4, S)
            inv_sqrt(4)
            split_run(PAIR_MEM + 4, PAIR_IN1, S)
            split_run(PAIR_IN1, PAIR_IN1 + 4, IN1_W)
            inv_sqrt(8)
            split_run(PAIR_IN1 + 4, PAIR_IN1 + 16, IN1_W)
            inv_sqrt(32)
            split_run(PAIR_IN1 + 16, PAIR_IN1 + 20, IN1_W)
            inv_sqrt(32)
            split_run(PAIR_IN1 + 20, PAIR_UQ, IN1_W)
            inv_sqrt(8)
            inv_sqrt(16)
            for p in range(PAIR_UQ, PAIR_UKV):
                split(p, p % RING, 2 - p % 2, 384)
            attention("a")
            for p in range(PAIR_UKV, PAIR_MERGE):
                split(p, p % RING, 2, S)
            split_run(PAIR_MERGE, PAIR_MERGE + 4, S)
            attention("b0")
            attention("b1")
            attention("m")
            split_run(PAIR_MERGE + 4, PAIR_IN2, S)
            inv_sqrt(4)
            split_run(PAIR_IN2, PAIR_M2, IN2_W)
            split_run(PAIR_M2, PAIR_M2 + 4, S)
            attention("n0")
            attention("n1")
            split_run(PAIR_M2 + 4, PAIR_FF, S)
            inv_sqrt(4)
            split_run(PAIR_FF, PAIR_FF + 64, S)
            inv_sqrt(4)

        @block.tensor
        def _(pe):
            def group(name, n, work):
                t = GROUPS[name] + n
                if t >= 2:
                    for who, s in (("A", "group_a"), ("D", "group_d")):
                        if who in GROUP_OF[t - 2]:
                            pe.wait_ge(sem[s], groups_emptied(who, t - 2))
                work(bank[6 + t % 2]).then_inc(sem["group_done"], 1)

            def enter_banks(strips):
                for who, s in (("A", "emptied_a"), ("D", "emptied_d")):
                    wait(pe, sem[s], strips_emptied(who, strips - 1))

            def enter_strips(name, passes):
                t = GROUPS[name] - 1
                pe.wait_ge(sem["group_a"], groups_emptied("A", t))
                pe.wait_ge(sem["group_d"], groups_emptied("D", t))
                wait(pe, sem["o_emptied"], passes)

            def transposes(pieces):
                def work(b):
                    o = 0
                    for src, k, m in pieces:
                        ins = pe.transpose(b[0:m, o:o + k], src, ident[0:k, 0:k])
                        o += k
                    return ins
                return work

            def columns(c, n=P):
                return transposes([(proj[:, t, c:c + n], P, n) for t in range(TT)])

            def wait_pair(p):
                pe.wait_ge(sem["hi_made"], p + 1)
                pe.wait_ge(sem["lo_made"], p + 1)

            def free_banks(i, strip):
                s0 = strip(i if isinstance(i, int) else 1) - 2
                if s0 >= 0:
                    who = STRIPS[s0]
                    pe.wait_ge(sem["emptied_a" if who == "A" else "emptied_d"],
                               at(i, lambda j: strips_emptied(who, strip(j) - 2)))

            def strip_products(s, p0, tiles, halves, kt0, x_parts, width, feature_major, first=True, last=True,
                               tok=TT, before=None):
                x_hi, x_lo = x_parts
                for q in range(tiles):
                    p = p0[q]
                    wait_pair(p[0])
                    slot = p[1]
                    n_half = halves[q]
                    for kk in range(n_half):
                        kt = kt0 + 2 * q + kk
                        if before is not None:
                            before(kt)
                        st, en = first and q == 0 and kk == 0, last and q == tiles - 1 and kk == n_half - 1
                        wh, wl = w_hi[:, slot, kk, 0:width], w_lo[:, slot, kk, 0:width]
                        for b in range(tok):
                            dst = bank[4 * (s % 2) + b]
                            if feature_major:
                                c = slice(b * P, b * P + P)
                                terms = [(w_hi[:, slot, kk, c], x_hi[:, kt, :]), (w_hi[:, slot, kk, c], x_lo[:, kt, :]),
                                         (w_lo[:, slot, kk, c], x_hi[:, kt, :])]
                                o = dst[:, 0:S]
                            else:
                                c = slice(b * P, b * P + P)
                                terms = [(x_hi[:, kt, c], wh), (x_hi[:, kt, c], wl), (x_lo[:, kt, c], wh)]
                                o = dst[:, 0:width]
                            for j, (lhs, rhs) in enumerate(terms):
                                ins = pe.matmul(o, lhs, rhs, start=st and j == 0, stop=en and j == 2)
                    ins.then_inc(sem["pair_used"], 1)

            def slots(i, p0, n):
                return [(at(i, lambda j, q=q: p0(j) + q), (p0(i if isinstance(i, int) else 1) + q) % RING)
                        for q in range(n)]

            def strip(i, s, p0, n, x_parts, width, feature_major, halves=None, kt0=0, tok=TT,
                      before=None):
                free_banks(i, s)
                sx = s(i if isinstance(i, int) else 1)
                strip_products(sx, slots(i, p0, n), n, halves or [2] * n, kt0, x_parts, width, feature_major, tok=tok,
                               before=before)

            def merged_parts(n):
                def before(kt):
                    if kt % 2 == 0:
                        pe.wait_ge(sem["mhi"], 4 * n + kt // 2 + 1)
                        pe.wait_ge(sem["mlo"], 4 * n + kt // 2 + 1)
                return before

            def normed_parts(name, c, ready):
                def before(kt):
                    for k in ((0, 1) if kt == 0 else (kt + 1,)):
                        if k < KT:
                            pe.wait_ge(sem["xs_ready"], ready(k))
                            group(name, k, columns(c + P * k))
                    for who, s in (("A", "group_a"), ("D", "group_d")):
                        pe.wait_ge(sem[s], groups_emptied(who, GROUPS[name] + kt))
                return before

            pe.wait_ge(sem["cst_in"], 16)
            pe.wait_ge(sem["vec_in"], 16 * 9)
            group("vec", 0, transposes([(vec_rows[:, :], 73, P)]))
            pe.wait_ge(sem["xs_ready"], 2)
            for k in range(4):
                group("mem", k, transposes([(proj[:, t, 2792 + P * (2 * k + j):2792 + P * (2 * k + j) + P], P, P)
                                            for j in range(2) for t in range(2)]))
            pe.wait_ge(sem["group_a"], groups_emptied("A", GROUPS["mem"] + 3))
            pe.wait_ge(sem["group_d"], groups_emptied("D", GROUPS["mem"] + 3))
            for b in range(2):
                strip(0, lambda j: STRIP_MEM + b, lambda j: PAIR_MEM + 4 * b, 4, (mt_hi, mt_lo), S, False, tok=2)

            xt = (xt_hi, xt_lo)

            def in1(i):
                for b in range(2):
                    if isinstance(i, int) and b == 1:
                        enter_strips("iq", 0)
                    strip(i, lambda j: STRIP_IN1 + 2 * j + b, lambda j: PAIR_IN1 + 8 * j + 4 * b, 4, xt, IN1_W, False,
                          before=normed_parts("x", XRES, lambda k: 6) if isinstance(i, int) and b == 0 else None)
            enter_banks(STRIP_IN1)
            in1(0)
            with pe.Fori(1, 3) as i:
                in1(i)

            enter_banks(STRIP_IN1 + 6)
            pe.wait_ge(sem["ready_for_t"], 1)
            for k in range(4):
                group("iq", k, columns(QI + P * k))
            group("ik", 0, transposes([(proj[:, t, KI:KI + 64], P, 64) for t in range(TT)]))
            pe.wait_ge(sem["group_a"], groups_emptied("A", GROUPS["ik"]))
            pe.wait_ge(sem["group_d"], groups_emptied("D", GROUPS["ik"]))
            for n, (i, h) in enumerate((i, h) for i in range(1, TT) for h in range(HEADS)):
                if n >= 2:
                    pe.wait_ge(sem["ix_relu"], n - 1)
                o, q = bank[n % 2][:, 0:(i + 1) * P], q_parts[:, h, i * P:(i + 1) * P]
                pe.matmul(o, q, ix_k[:, 0, 0:(i + 1) * P], start=True, stop=False)
                pe.matmul(o, q, ix_k[:, 1, 0:(i + 1) * P], start=False, stop=True).then_inc(sem["ix_scores"], 1)
            pe.wait_ge(sem["ix_relu"], 24)
            with pe.Fori(3, 5) as i:
                in1(i)
            enter_banks(STRIP_UQ)

            pe.wait_ge(sem["z_ready"], 2)
            for k in range(4):
                group("aq", k, columns(QA + P * k))
            for k in range(4):
                group("ak", k, columns(KA + P * k))

            pe.wait_ge(sem["group_a"], groups_emptied("A", GROUPS["ak"] + 3))
            for n, c in enumerate((ZA, ZB, ZM)):
                wait(pe, sem["zt_emptied"], 4 * (n - 1))
                pe.wait_ge(sem["z_ready"], n + 1)
                for k in range(4):
                    transposes([(proj[:, t, c + P * k:c + P * k + P], P, P) for t in range(TT)])(bank[4 * (n % 2) + k])\
                        .then_inc(sem["zt_done"], 1)

            def attention(stage):
                u0, u1 = STAGE_UNITS[stage]
                for step in range(u0, u1 + LAG_PV):
                    u = step
                    if u < u1:
                        w = UNITS[u]
                        if u >= len(SCORE_BANKS):
                            pe.wait_ge(sem["masked"], u + 1 - len(SCORE_BANKS))
                        o = bank[SCORE_BANKS[u % len(SCORE_BANKS)]][:, 0:w["k"].shape[-1]]
                        ins = pe.matmul(o, w["q"], w["k"], start=True, stop=w["k_lo"] is None)
                        if w["k_lo"] is not None:
                            ins = pe.matmul(o, w["q"], w["k_lo"], start=False, stop=True)
                        ins.then_inc(sem["scores"], 1)
                    u = step - LAG_T
                    if u0 <= u < u1:
                        w = UNITS[u]
                        pe.wait_ge(sem["normed"], u + 1)
                        wait_copied(pe, u - 2)
                        for t in range(-(-w["n"] // P)):
                            n = min(P, w["n"] - t * P)
                            ins = pe.transpose(bank[2 + u % 2][0:n, t * P:(t + 1) * P],
                                               sc[:, u % SC, t * P:t * P + n], ident)
                        ins.then_inc(sem["probs_t"], 1)
                    u = step - LAG_PV
                    if u0 <= u < u1:
                        w = UNITS[u]
                        wait_copied(pe, u)
                        if w["first"] and w["pas"] >= 2:
                            pe.wait_ge(sem["o_emptied"], w["pas"] - 1)
                        nt = len(w["v"])
                        for t in range(nt):
                            n = min(P, w["n"] - t * P)
                            ins = pe.matmul(bank[4 + w["pas"] % 2][w["rows"], w["cols"]], w["v"][t],
                                            prob_t[0:n, u % 2, t * P:(t + 1) * P],
                                            start=w["start"] and t == 0, stop=w["stop"] and t == nt - 1,
                                            skip_group_check=True)
                        ins.then_inc(sem["applied"], 1)

            pe.wait_ge(sem["zt_emptied"], 12)
            attention("a")

            pe.wait_ge(sem["ready_for_t"], 2)
            for k in range(3):
                group("cq", k, columns(CQ + P * k))
            for k in range(2):
                group("ckv", k, columns(CKV + P * k))
            enter_strips("b0", STAGE_PASSES["a"][1])
            for b in range(2):
                strip(0, lambda j: STRIP_UQ + b, lambda j: PAIR_UQ + 2 * b, 2, (cq_hi, cq_lo), 384, False, halves=[2, 1])
            for b in range(2):
                strip(0, lambda j: STRIP_UKV + b, lambda j: PAIR_UKV + b, 1, (ckv_hi, ckv_lo), S, False)
            enter_banks(STRIP_MERGE)
            pe.wait_ge(sem["ready_for_t"], 3)
            for r in range(2):
                for h in range(4):
                    group(f"b{r}", 2 * h, columns(QB + 96 * (4 * r + h), 96))
                    group(f"b{r}", 2 * h + 1, columns(KB + 96 * (4 * r + h), 96))
                pe.wait_ge(sem["group_a"], groups_emptied("A", GROUPS[f"b{r}"] + 7))
                pe.wait_ge(sem["group_d"], groups_emptied("D", GROUPS[f"b{r}"] + 7))
                attention(f"b{r}")
            for k in range(4):
                group("mq", k, columns(QM + P * k))
            for k in range(2):
                group("mk", k, transposes([(kvm[:, t, P * (2 * k + j):P * (2 * k + j) + P], P, P)
                                           for j in range(2) for t in range(2)]))
            pe.wait_ge(sem["group_a"], groups_emptied("A", GROUPS["mk"] + 1))
            attention("m")

            enter_strips("x2", STAGE_PASSES["m"][1])

            def merge(n, buf):
                for b in range(2):
                    strip(n, lambda j: STRIP_MERGE + 4 * j + b, lambda j: PAIR_MERGE + 12 * j + 4 * b, 4, xt, S, True)
                pe.wait_ge(sem["ys_hi"], at(n, lambda j: j + 1))
                pe.wait_ge(sem["ys_lo"], at(n, lambda j: j + 1))
                for b in range(2):
                    strip(n, lambda j: STRIP_MERGE + 4 * j + 2 + b, lambda j: PAIR_MERGE + 12 * j + 8 + 2 * b, 2,
                          buf, S, True)
            for n in range(3):
                merge(n, ys[n % 2])
            for b in range(2):
                strip(0, lambda j: STRIP_OUT1 + b, lambda j: PAIR_OUT1 + 4 * b, 4, xt, S, False,
                      before=merged_parts(0))

            enter_banks(STRIP_IN2)
            def in2(i):
                for b in range(2):
                    if isinstance(i, int) and b == 1:
                        enter_strips("ck", STAGE_PASSES["m"][1])
                    strip(i, lambda j: STRIP_IN2 + 2 * j + b, lambda j: PAIR_IN2 + 8 * j + 4 * b, 4, xt, IN2_W, False,
                          before=normed_parts("x2", 0, lambda k: 10 + k // 4 * 4) if isinstance(i, int) and b == 0 else None)
            in2(0)
            with pe.Fori(1, 3) as i:
                in2(i)

            enter_banks(STRIP_M2)
            for k, name in enumerate(("ck", "cv")):
                group(name, 0, columns((KC2, VC2)[k]))

            pe.wait_ge(sem["pool_in"], 16)
            for g in range(4):
                def means(b):
                    c = slice(U2 + P * g, U2 + P * g + P)
                    for t in range(TT):
                        w = proj[:, g, POOLC + P * (t > 0):POOLC + P * (t > 0) + P]
                        pe.matmul(b[:, t * P:t * P + P], proj[:, t, c], w, start=t == 0, stop=False,
                                  skip_group_check=True)
                    for t in range(1, TT):
                        ins = pe.matmul(b[:, t * P:t * P + 16], proj[:, t - 1, c],
                                        proj[:, g, POOLC + 2 * P:POOLC + 2 * P + 16], start=False, stop=t == TT - 1,
                                        skip_group_check=True)
                    return ins
                group("pd", g, means)
            pe.wait_ge(sem["wpool_in"], 16)
            pe.wait_ge(sem["group_a"], groups_emptied("A", GROUPS["pd"] + 3))
            for g in range(4):
                group("py", g, lambda b: pe.matmul(b[:, 0:S], proj[:, g, WPOOLC:WPOOLC + P], d_t[:, g, :], start=True, stop=True))
            for k, (name, w_in_sem) in enumerate((("ck", "w1_in"), ("cv", "w1v_in"))):
                pe.wait_ge(sem["flats"], k + 1)
                pe.wait_ge(sem[w_in_sem], 16 if k else 64)

                def hidden(b):
                    for lp in range(16):
                        c = W1C + 256 * (lp % 4)
                        ins = pe.matmul(b[0:62, 0:256], flat[k][:, lp].rearrange("p g n -> p (g n)"),
                                        w1v[:, lp, :] if k else proj[:, lp // 4, c:c + 256], start=lp == 0, stop=lp == 15)
                    return ins
                group(name + "h", 0, hidden)
            for k, name in enumerate(("ckt", "cvt")):
                pe.wait_ge(sem["hid_in"], k + 1)
                group(name, 0, transposes([(hid[0:62, 3, j * P:j * P + P] if k else hid[0:62, 2, j * P:j * P + P], 62, P)
                                           for j in range(2)]))
            pe.wait_ge(sem["wc2_in"], 32)
            for k, name in enumerate(("kcmp", "vcmp")):
                pe.wait_ge(sem["group_a"], groups_emptied("A", GROUPS["ckt"] + k))

                def second(b):
                    for g in range(2):
                        for j in range(2):
                            ins = pe.matmul(b[0:NCMP, 64 * g:64 * g + 64], hid_t[:, k, j, NCMP * g:NCMP * g + NCMP],
                                            wc2[:, k, j, :], start=j == 0, stop=j == 1)
                    return ins
                group(name, 0, second)
            pe.wait_ge(sem["ready_for_t"], 5)
            group("kct", 0, transposes([(kcv[0:NCMP, 0].rearrange("p g d -> p (g d)"), NCMP, P)]))


            for g in range(2):
                for k in range(4):
                    group(f"n{g}", k, columns(Q2 + 512 * g + P * k))
                for k, c in enumerate((KS2, KW2)):
                    group(f"n{g}", 4 + k, columns(c))
                pe.wait_ge(sem["group_a"], groups_emptied("A", GROUPS[f"n{g}"] + 5))
                pe.wait_ge(sem["group_d"], groups_emptied("D", GROUPS[f"n{g}"] + 5))
                attention(f"n{g}")

            enter_strips("x3", STAGE_PASSES["n1"][1])
            m2 = PAIR_M2
            pool_parts = (projr[:, :, YS2:YS2 + S], projr[:, :, YS2 + S:YS2 + 2 * S])
            for b in range(2):
                strip(0, lambda j: STRIP_M2 + b, lambda j: m2 + 4 * b, 4, xt, S, True)
            pe.wait_ge(sem["ys_hi"], 4)
            pe.wait_ge(sem["ys_lo"], 4)
            for b in range(2):
                strip(0, lambda j: STRIP_M2 + 2 + b, lambda j: m2 + 8 + 2 * b, 2, pool_parts, S, True)
            for b in range(2):
                strip(0, lambda j: STRIP_M2 + 4 + b, lambda j: m2 + 12 + 4 * b, 4, xt, S, True)
            pe.wait_ge(sem["yn_hi"], 1)
            pe.wait_ge(sem["yn_lo"], 1)
            for b in range(2):
                strip(0, lambda j: STRIP_M2 + 6 + b, lambda j: m2 + 20 + 4 * b, 4, (yn_hi, yn_lo), S, True)
            for b in range(2):
                strip(0, lambda j: STRIP_OUT2 + b, lambda j: PAIR_OUT2 + 4 * b, 4, xt, S, False,
                      before=merged_parts(1))

            enter_banks(STRIP_FF)
            def ff_up(f, s, p, before=None):
                strip(f, s, p, 4, xt, S, True, before=before)

            def ff_down(f, buf, s, p):
                pe.wait_ge(sem["h_hi"], at(f, lambda j: j))
                pe.wait_ge(sem["h_lo"], at(f, lambda j: j))
                for b in range(2):
                    strip(f, lambda j: s(j) + b, lambda j: p(j) + 2 * b, 2, ys[buf], S, False)

            def ff_step(i, parity, t):
                ff_up(i, lambda j: STRIP_FF + 1 + 3 * t(j), lambda j: PAIR_FF + 4 + 8 * t(j))
                pe.wait_ge(sem["h_hi"], at(i, lambda j: t(j) + 1))
                pe.wait_ge(sem["h_lo"], at(i, lambda j: t(j) + 1))
                for b in range(2):
                    strip(i, lambda j: STRIP_FF + 2 + b + 3 * t(j), lambda j: PAIR_FF + 8 + 2 * b + 8 * t(j), 2,
                          ys[parity], S, False)
            ff_up(0, lambda j: STRIP_FF, lambda j: PAIR_FF,
                  before=normed_parts("x3", 0, lambda k: 18 + k // 4 * 4))
            pe.wait_ge(sem["group_a"], groups_emptied("A", GROUPS["x3"] + 7))
            pe.wait_ge(sem["group_d"], groups_emptied("D", GROUPS["x3"] + 7))
            ff_step(0, 0, lambda j: 0)
            with pe.Fori(1, 4) as i:
                ff_step(i, 1, lambda j: 2 * j - 1)
                ff_step(i, 0, lambda j: 2 * j)
            ff_down(8, 1, lambda j: STRIP_FF + 22, lambda j: PAIR_FF + 60)

        @block.scalar
        def _(act):
            r = 0
            for src in (g_norm[0].rearrange("(r c) -> r c", c=P), g_mem[0].rearrange("(r c) -> r c", c=P),
                        norm_mix_2[0].rearrange("(r c) -> r c", c=P), norm_mlp_2[0].rearrange("(r c) -> r c", c=P),
                        pool_scale_2[0].rearrange("(r c) -> r c", c=P), g_cq[0].rearrange("(r c) -> r c", c=P),
                        g_ckv[0].rearrange("(r c) -> r c", c=P), pe_k_2[0].rearrange("(r two) c -> r (two c)", two=2),
                        pe_v_2[0].rearrange("(r two) c -> r (two c)", two=2)):
                act.dma_start(vec_rows[r:r + src.shape[0], :], src).then_inc(sem["vec_in"], 16)
                r += src.shape[0]
            def part_hi(p, slot, halves, width):
                act.wait_ge(landed[slot], p // RING * 16 + 16 if isinstance(p, int) else (p + (RING - slot)) * 4)
                if not isinstance(p, int) or p >= RING:
                    act.wait_ge(sem["pair_used"], p - (RING - 1))
                act.activation(w_hi[:, slot, 0:halves, 0:width], raw[:, slot, 0:halves, 0:width], ACT.Copy)\
                   .then_inc(sem["hi_made"], 1)

            def his(i, p0, n=RING, width=S):
                for q in range(n):
                    slot = (p0(i if isinstance(i, int) else 1) + q) % RING
                    part_hi(at(i, lambda j: p0(j) + q), slot, 2, width)

            def group_wait(name, n):
                act.wait_ge(sem["group_done"], GROUPS[name] + n + 1)
                return bank[6 + (GROUPS[name] + n) % 2]

            def strip_wait(i, s):
                act.wait_ge(sem["pair_used"], at(i, lambda j: strip_end(s(j))))
                sx = s(i if isinstance(i, int) else 1)
                return bank[4 * (sx % 2):4 * (sx % 2) + 4]

            act.wait_ge(sem["mem_in"], 16)
            act.activation(junk[:, D:2 * D], proj[:, 1, 2792:2792 + D], ACT.Square, accum_out=stat[:, 1:2])\
               .then_inc(sem["squares"], 1)
            act.wait_ge(sem["squares"], 1)
            b = group_wait("vec", 0)
            act.activation(vec[:], b[:, 0:73], ACT.Copy).then_inc(sem["group_a"], 1)
            act.wait_ge(sem["group_a"], 1)
            for k in range(4):
                b = group_wait("mem", k)
                act.mul(mt_hi[:, 2 * k, :], b[:, 0:256], vec[:, 8 + 2 * k:9 + 2 * k])
                act.mul(mt_hi[:, 2 * k + 1, :], b[:, 256:512], vec[:, 9 + 2 * k:10 + 2 * k]).then_inc(sem["group_a"], 1)
            his(0, lambda j: PAIR_MEM)
            act.wait_ge(sem["x_in"], 16)
            for t in (1, 3):
                act.activation(junk[:, D:2 * D], proj[:, t, XRES:XRES + D], ACT.Square, accum_out=stat[:, 4 + t:5 + t])\
                   .then_inc(sem["squares"], 1)
                act.wait_ge(sem["squares"], t // 2 + 2)
            act.dma_start(pos_i[:], positions[0].rearrange("(t p) -> p t", p=P), allow_slow_non_contiguous=True)\
               .then_inc(sem["pos_in"], 16)
            for k, src in enumerate((g_qn_b, g_kn_b)):
                act.dma_start(nope_gain[0:64, k:k + 1], src[0, 0:64].rearrange("(p o) -> p o", o=1),
                              allow_slow_non_contiguous=True).then_inc(sem["gain_in"], 16)
            for dst, src in rows.values():
                act.dma_start(dst[:], src.to_broadcast(dst.shape)).then_inc(sem["row_in"], 16)
            his(0, lambda j: PAIR_MEM + 4)
            his(0, lambda j: PAIR_IN1, width=IN1_W)
            for b in range(2):
                banks = strip_wait(0, lambda j: STRIP_MEM + b)
                for t in range(2):
                    ins = act.activation(kvm[:, t, S * b:S * b + S], banks[t][:], ACT.Copy)
                ins.then_inc(sem["emptied_a"], 1)
            for k in range(KT):
                b = group_wait("x", k)
                act.mul(xt_hi[:, k, :], b[:], vec[:, k:k + 1]).then_inc(sem["group_a"], 1)

            def empty_in1(i, b):
                banks = strip_wait(i, lambda j: STRIP_IN1 + 2 * j + b)
                for t in range(TT):
                    c = at(i, lambda j: (2 * j + b) * IN1_W)
                    ins = act.activation(proj[:, t, bass.ds(c, IN1_W)], banks[t][:, 0:IN1_W], ACT.Copy)
                ins.then_inc(sem["emptied_a"], 1)

            def in1(i, last=False):
                his(i, lambda j: PAIR_IN1 + 8 * j + 4, width=IN1_W)
                empty_in1(i, 0)
                if not last:
                    his(i, lambda j: PAIR_IN1 + 8 * j + 8, width=IN1_W)
                empty_in1(i, 1)
            in1(0)
            act.wait_ge(sem["sin_in"], 1)
            act.activation(sin1[:], ang[:, 1], ACT.Sin).then_inc(sem["sin_out"], 1)
            act.activation(cos1[:], ang[:, 1], ACT.Sin, scale=0.5).then_inc(sem["sin_out"], 1)
            with act.Fori(1, 3) as i:
                in1(i)

            def queries_hi(name):
                for k in range(4):
                    b = group_wait(name, k)
                    act.activation(q_parts[0:64, 2 * k, :], b[0:64, :], ACT.Copy)
                    act.activation(q_parts[64:128, 2 * k + 1, :], b[64:128, :], ACT.Copy).then_inc(sem["group_a"], 1)

            def keys_hi(name, k, r, dst):
                b = group_wait(name, k)
                act.activation(dst[0:64, 0], b[r, :], ACT.Copy)
                act.activation(dst[64:128, 0], b[r, :], ACT.Copy).then_inc(sem["group_a"], 1)

            queries_hi("iq")
            keys_hi("ik", 0, half_rows(0), ix_k)
            for n, i in enumerate(i for i in range(1, TT) for h in range(HEADS)):
                act.wait_ge(sem["ix_scores"], n + 1)
                if n >= 2:
                    act.wait_ge(sem["ix_acc"], n - 1)
                act.activation(sc[:, n % 2, 0:(i + 1) * P], bank[n % 2][:, 0:(i + 1) * P], ACT.Relu,
                               scale=64 ** -0.5).then_inc(sem["ix_relu"], 1)
            act.activation(z_tanh[0][:], proj[:, :, ZA:ZA + S], ACT.Tanh, scale=0.5).then_inc(sem["z_tanh"], 1)
            in1(3)
            act.wait_ge(sem["emptied_a"], STRIP_IN1 + 8)
            act.activation(z_tanh[1][:], proj[:, :, ZB:ZB + S], ACT.Tanh, scale=0.5).then_inc(sem["z_tanh"], 1)
            in1(4, last=True)
            act.wait_ge(sem["emptied_a"], STRIP_IN1 + 10)
            act.activation(z_tanh[2], proj[:, :, ZM:ZM + S], ACT.Tanh, scale=0.5).then_inc(sem["z_tanh"], 1)
            for b in range(2):
                for q in range(2):
                    p = PAIR_UQ + 2 * b + q
                    part_hi(p, p % RING, 2 - q, 384)
            for name, dst in (("aq", q_t), ("ak", k_t)):
                for k in range(4):
                    b = group_wait(name, k)
                    act.activation(dst[:, k, :], b[:], ACT.Copy).then_inc(sem["group_a"], 1)

            for n, c in enumerate((ZA, ZB, ZM)):
                act.wait_ge(sem["zt_done"], 4 * n + 4)
                for k in range(4):
                    act.mul(proj[:, k, c:c + S], bank[4 * (n % 2) + k][:], 0.5).then_inc(sem["zt_emptied"], 1)

            def attention(stage):
                u0, u1 = STAGE_UNITS[stage]
                for step in range(u0, u1 + LAG_COPY):
                    u = step - LAG_COPY
                    if u0 <= u < u1 and copier(u) == "A":
                        w = UNITS[u]
                        act.wait_ge(sem["probs_t"], u + 1)
                        if u >= 2:
                            act.wait_ge(sem["applied"], u - 1)
                        n, r = (w["n"], P) if w["n"] >= P else (P, w["n"])
                        act.activation(prob_t[0:r, u % 2, 0:n], bank[2 + u % 2][0:r, 0:n], ACT.Copy)\
                           .then_inc(sem["copied_a"], 1)
                    u = step
                    if u < u1:
                        w = UNITS[u]
                        act.wait_ge(sem["masked"], u + 1)
                        v = sc[:, u % SC, 0:w["n"]]
                        act.activation(v, v, ACT.Exp, scale=-1.0, bias=negmax[:, u % SC:u % SC + 1],
                                       accum_out=sums[:, u % SC:u % SC + 1]).then_inc(sem["exps"], 1)

            attention("a")

            yt = {"ya": proj[:, :, YTA:YTA + S], "yb": proj[:, :, YTB:YTB + S], "ym": proj[:, :, YTM:YTM + S]}

            for k in range(3):
                b = group_wait("cq", k)
                act.mul(cq_hi[:, k, :], b[:], vec[:, VEC["cq"] + k:VEC["cq"] + k + 1]).then_inc(sem["group_a"], 1)
            for k in range(2):
                b = group_wait("ckv", k)
                act.mul(ckv_hi[:, k, :], b[:], vec[:, VEC["ckv"] + k:VEC["ckv"] + k + 1]).then_inc(sem["group_a"], 1)
            act.wait_ge(sem["o_emptied"], STAGE_PASSES["a"][1])
            act.wait_ge(sem["group_d"], groups_emptied("D", GROUPS["ckv"] + 1))
            act.activation(yt["ya"], proj[:, :, ZA:ZA + S], ACT.Copy).then_inc(sem["y_moved"], 1)
            for p in range(PAIR_UKV, PAIR_MERGE):
                part_hi(p, p % RING, 2, S)
            for b in range(2):
                banks = strip_wait(0, lambda j: STRIP_UQ + b)
                for t in range(TT):
                    ins = act.activation(proj[:, t, QB + 384 * b:QB + 384 * b + 384], banks[t][:, 0:384], ACT.Copy)
                ins.then_inc(sem["emptied_a"], 1)
            act.wait_ge(sem["emptied_a"], strips_emptied("A", STRIP_UQ + 1))
            act.activation(sq_q[:], proj[:, :, QB:QB + 768], ACT.Square).then_inc(sem["b_squares"], 1)
            def roots(k):
                act.wait_ge(sem["b_mean"], k + 1)
                act.activation(rstd[:, 0:32], stat[:, 0:32], ACT.Sqrt).then_inc(sem["b_root"], 1)

            for b in range(2):
                if b == 1:
                    roots(0)
                banks = strip_wait(0, lambda j: STRIP_UKV + b)
                for t in range(TT):
                    ins = act.activation(proj[:, t, KVB + S * b:KVB + S * b + S], banks[t][:], ACT.Copy)
                ins.then_inc(sem["emptied_a"], 1)
            act.wait_ge(sem["emptied_a"], strips_emptied("A", STRIP_UKV + 1))
            act.activation(sq_k[:].rearrange("p t (h d) -> p t h d", h=8),
                           proj[:, :, KVB:KVB + D].rearrange("p t (h d) -> p t h d", h=8)[:, :, :, 0:64], ACT.Square)\
               .then_inc(sem["b_squares"], 1)
            roots(1)
            act.preload_act_table(ACT.Exp)
            act.wait_ge(sem["gain_in"], 32)
            act.wait_ge(sem["half_set"], 1)
            his(0, lambda j: PAIR_MERGE)
            for r in range(2):
                for h in range(4):
                    b = group_wait(f"b{r}", 2 * h)
                    act.mul(q_t[0:96, h, :], b[0:96, :], nope_gain[0:96, 0:1]).then_inc(sem["group_a"], 1)
                attention(f"b{r}")
            for k in range(4):
                b = group_wait("mq", k)
                act.activation(q_t[:, k, :], b[:], ACT.Copy).then_inc(sem["group_a"], 1)
            for k in range(2):
                b = group_wait("mk", k)
                act.activation(k_t[:, 2 * k:2 * k + 2, 0:256], b[:].rearrange("p (a n) -> p a n", a=2), ACT.Copy)\
                   .then_inc(sem["group_a"], 1)
            attention("m")

            def merge_act(n):
                for b in range(2):
                    if n or b:
                        his(n, lambda j: PAIR_MERGE + 12 * j + 4 * b)
                    if b == 1:
                        empty_gate(n, 0)
                his(n, lambda j: PAIR_MERGE + 12 * j + 8)
                empty_gate(n, 1)

            def empty_gate(n, b, s0=STRIP_MERGE, per=4, dst=GATED):
                banks = strip_wait(n, lambda j: s0 + per * j + b)
                if b == 0:
                    wait(act, sem["gated"], at(n, lambda j: 2 * j))
                for m in range(4):
                    mt = 4 * b + m
                    ins = act.activation(proj[:, mt // 2, dst + S * (mt % 2):dst + S * (mt % 2) + S],
                                         banks[m][:], ACT.Tanh, scale=0.5)
                ins.then_inc(sem["emptied_a"], 1)

            act.wait_ge(sem["o_emptied"], STAGE_PASSES["m"][1])
            for n, name in enumerate(("ya", "yb", "ym")):
                if n == 2:
                    act.wait_ge(sem["pair_used"], strip_end(STRIP_MERGE + 4 - 1))
                act.activation(ys[n % 2][0][:], yt[name], ACT.Copy).then_inc(sem["ys_hi"], 1)
                merge_act(n)
            his(0, lambda j: PAIR_OUT1)
            act.wait_ge(sem["pair_used"], strip_end(STRIP_OUT1 - 3))
            for t in range(TT):
                act.wait_ge(sem["merged_in"], t // 2 + 1)
                act.mul(xt_hi[:, 2 * t:2 * t + 2, :], proj[:, t, MERGED:MERGED + D].rearrange("p (a n) -> p a n", a=2),
                        0.5).then_inc(sem["mhi"], 1)
            his(0, lambda j: PAIR_OUT1 + 4)

            def squares(n, b, scratch):
                act.wait_ge(sem["squares"], 3 + 8 * n + 4 * b)
                for t in range(TT):
                    act.wait_ge(sem["x_added"], 8 * n + 4 * b + t + 1)
                    act.activation(scratch(t), proj[:, t, XRES + S * b:XRES + S * b + S], ACT.Square,
                                   accum_out=stat[:, 4 * b + t:4 * b + t + 1]).then_inc(sem["squares"], 1)

            def junk_tile(t):
                return junk[:, S * t:S * t + S]

            def relu_tile(t):
                return proj[:, t, D:D + S]

            squares(0, 0, junk_tile)

            def normed(name, v):
                for k in range(KT):
                    b = group_wait(name, k)
                    if k == 0:
                        act.wait_ge(sem["pair_used"], strip_end((STRIP_IN2 if name == "x2" else STRIP_FF) - 1))
                    act.mul(xt_hi[:, k, :], b[:], vec[:, v + k:v + k + 1]).then_inc(sem["group_a"], 1)

            his(0, lambda j: PAIR_IN2, width=IN2_W)
            squares(0, 1, junk_tile)
            normed("x2", VEC["mix"])

            def empty_in2(i, b):
                banks = strip_wait(i, lambda j: STRIP_IN2 + 2 * j + b)
                for t in range(TT):
                    c = at(i, lambda j: (2 * j + b) * IN2_W)
                    ins = act.activation(proj[:, t, bass.ds(c, IN2_W)], banks[t][:, 0:IN2_W], ACT.Copy)
                ins.then_inc(sem["emptied_a"], 1)

            def in2(i, last=False):
                his(i, lambda j: PAIR_IN2 + 8 * j + 4, width=IN2_W)
                empty_in2(i, 0)
                if not last:
                    his(i, lambda j: PAIR_IN2 + 8 * j + 8, width=IN2_W)
                empty_in2(i, 1)
            in2(0)
            with act.Fori(1, 2) as i:
                in2(i)
            in2(2, last=True)

            act.wait_ge(sem["emptied_a"], strips_emptied("A", STRIP_M2 - 1))
            act.activation(gsig[:], proj[:, :, GN2:GN2 + 48], ACT.Tanh, scale=0.5).then_inc(sem["tanh_out"], 1)
            for g in range(4):
                b = group_wait("pd", g)
                act.activation(d_t[:, g, :], b[:], ACT.Copy).then_inc(sem["group_a"], 1)
            for g in range(4):
                b = group_wait("py", g)
                act.mul(proj[:, g, U2:U2 + S], b[:], vec[:, VEC["pool"] + g:VEC["pool"] + g + 1]).then_inc(sem["group_a"], 1)
            for k in range(2):
                act.wait_ge(sem["tanh_in"], k + 1)
                act.activation(hid[0:62, 1, :], hid[0:62, 1, :], ACT.Tanh, scale=(2 / np.pi) ** 0.5)\
                   .then_inc(sem["tanh_out"], 1)
            for k, name in enumerate(("ckt", "cvt")):
                b = group_wait(name, 0)
                act.mul(hid_t[:, k], b[:, 0:124].rearrange("p (j n) -> p j n", j=2), 0.5).then_inc(sem["group_a"], 1)
            b = group_wait("kct", 0)
            for g in range(2):
                for r in (slice(0, 64), slice(64, 128)):
                    ins = act.activation(kc_t[r, g, 0:NCMP], b[64 * g:64 * g + 64, 0:NCMP], ACT.Copy)
            ins.then_inc(sem["group_a"], 1)
            his(0, lambda j: PAIR_M2)
            for g in range(2):
                queries_hi(f"n{g}")
                for k in range(2):
                    keys_hi(f"n{g}", 4 + k, half_rows(g), k_parts[:, k])
                attention(f"n{g}")
            act.wait_ge(sem["o_emptied"], len(PASSES))
            yn = proj[:, :, Q2:Q2 + D]
            for half_ in range(2):
                ins = act.activation(yn_hi[:, 4 * half_:4 * half_ + 4, :], yn[:, :, S * half_:S * half_ + S], ACT.Copy)
            ins.then_inc(sem["yn_hi"], 1)

            act.wait_ge(sem["yn_lo"], 1)
            act.activation(projr[:, :, YS2:YS2 + S], proj[:, :, U2:U2 + S], ACT.Copy).then_inc(sem["ys_hi"], 1)
            his(0, lambda j: PAIR_M2 + 4)

            def empty_gate2(b, k):
                banks = strip_wait(0, lambda j: STRIP_M2 + 4 * k + b)
                if b == 0 and k == 1:
                    act.wait_ge(sem["gated"], 8)
                for m in range(4):
                    mt = 4 * b + m
                    ins = act.activation(proj[:, mt // 2, GATED2 + S * (mt % 2):GATED2 + S * (mt % 2) + S],
                                         banks[m][:], ACT.Tanh, scale=0.5)
                ins.then_inc(sem["emptied_a"], 1)
            empty_gate2(0, 0)
            his(0, lambda j: PAIR_M2 + 8)
            empty_gate2(1, 0)
            his(0, lambda j: PAIR_M2 + 12)
            his(0, lambda j: PAIR_M2 + 16)
            empty_gate2(0, 1)
            his(0, lambda j: PAIR_M2 + 20)
            empty_gate2(1, 1)
            his(0, lambda j: PAIR_M2 + 24)
            his(0, lambda j: PAIR_OUT2)
            act.wait_ge(sem["pair_used"], strip_end(STRIP_OUT2 - 3))
            for t in range(TT):
                act.wait_ge(sem["merged_in"], 2 + t // 2 + 1)
                act.mul(xt_hi[:, 2 * t:2 * t + 2, :], proj[:, t, MERGED2:MERGED2 + D].rearrange("p (a n) -> p a n", a=2),
                        0.5).then_inc(sem["mhi"], 1)
            his(0, lambda j: PAIR_OUT2 + 4)
            squares(1, 0, relu_tile)
            his(0, lambda j: PAIR_FF)
            squares(1, 1, relu_tile)
            normed("x3", VEC["mlp"])

            relu = proj[:, :, D:D + S]
            square = proj[:, :, D + S:D + 2 * S]

            def empty_up(i, parity, s, f):
                banks = strip_wait(i, s)
                wait(act, sem["sq_out"], at(i, lambda j: f(j)))
                for m in range(4):
                    ins = act.activation(relu[:, m, :], banks[m][:], ACT.Relu)
                ins.then_inc(sem["emptied_a"], 1)
                if not (isinstance(i, int) and f(i) < 2):
                    act.wait_ge(sem["pair_used"], at(i, lambda j: PAIR_FF + 12 + 8 * (f(j) - 2)))
                act.wait_ge(sem["sq_out"], at(i, lambda j: f(j) + 1))
                act.activation(ys[parity][0][:], square, ACT.Copy).then_inc(sem["h_hi"], 1)

            his(0, lambda j: PAIR_FF + 4)
            empty_up(0, 0, lambda j: STRIP_FF, lambda j: 0)

            def ff_step(i, parity, t):
                his(i, lambda j: PAIR_FF + 8 + 8 * t(j))
                empty_up(i, 1 - parity, lambda j: STRIP_FF + 1 + 3 * t(j), lambda j: t(j) + 1)
                his(i, lambda j: PAIR_FF + 12 + 8 * t(j))
            ff_step(0, 0, lambda j: 0)
            with act.Fori(1, 4) as i:
                ff_step(i, 1, lambda j: 2 * j - 1)
                ff_step(i, 0, lambda j: 2 * j)
            for b in range(2):
                squares(2, b, relu_tile)

        @block.vector
        def _(dve):
            steps = [0]

            def step(ins):
                steps[0] += 1
                ins.then_inc(sem["dve_step"], 1)
                dve.wait_ge(sem["dve_step"], steps[0])

            def group_wait(name, n):
                dve.wait_ge(sem["group_done"], GROUPS[name] + n + 1)
                return bank[6 + (GROUPS[name] + n) % 2]

            def strip_wait(i, s):
                dve.wait_ge(sem["pair_used"], at(i, lambda j: strip_end(s(j))))
                sx = s(i if isinstance(i, int) else 1)
                return bank[4 * (sx % 2):4 * (sx % 2) + 4]

            powers = [0]

            def inv_rms(n, width, first=0):
                dve.tensor_scalar(stat[:, 0:n], stat[:, first:first + n], 1.0 / width, EPS, ALU.mult, ALU.add)\
                   .then_inc(sem["stat_ready"], 1)
                powers[0] += 1
                dve.wait_ge(sem["pow_done"], powers[0])

            def head_norm(v, h, d, gain):
                nt = v.shape[1]
                s = junk[:, 0:nt * h * d].rearrange("p (t h d) -> p t h d", t=nt, h=h)
                step(dve.tensor_tensor(s, v, v, ALU.mult))
                step(dve.tensor_reduce(stat[:, 0:nt * h].rearrange("p (t h) -> p t h", t=nt), s, AX.X, ALU.add))
                inv_rms(nt * h, d)
                r = rstd[:, 0:nt * h].rearrange("p (t h) -> p t h", t=nt).unsqueeze(3).to_broadcast([P, nt, h, d])
                step(dve.tensor_tensor(v, v, r, ALU.mult))
                step(dve.tensor_tensor(v, v, gain[:].unsqueeze(1).unsqueeze(1).to_broadcast([P, nt, h, d]), ALU.mult))

            def rotate(a, b, cos, sin, t1, t2):
                dve.tensor_tensor(t1[0], a, cos, ALU.mult)
                dve.tensor_tensor(t1[1], b, sin, ALU.mult)
                dve.tensor_tensor(t2[0], b, cos, ALU.mult)
                step(dve.tensor_tensor(t2[1], a, sin, ALU.mult))
                dve.tensor_tensor(a, t1[0], t1[1], ALU.subtract)
                return dve.tensor_tensor(b, t2[0], t2[1], ALU.add)

            def rotate_heads(c, h, d, r0, n, cos, sin, scratch):
                v = proj[:, :, c:c + h * d].rearrange("p t (h d) -> p t h d", h=h)
                a, b = v[:, :, :, r0:r0 + n], v[:, :, :, r0 + n:r0 + 2 * n]
                k = [scratch[j] .rearrange("p (t h n) -> p t h n", t=TT, h=h) for j in range(4)]
                cb, sb_ = (z.unsqueeze(2).to_broadcast([P, TT, h, n]) for z in (cos, sin))
                return rotate(a, b, cb, sb_, k[0:2], k[2:4])

            def rot_scratch(n):
                return [junk[:, n * j:n * j + n] for j in range(4)]

            dve.wait_ge(sem["mem_in"], 16)
            step(dve.tensor_tensor_reduce(junk[:, 0:D], proj[:, 0, 2792:2792 + D], proj[:, 0, 2792:2792 + D],
                                          1.0, 0.0, ALU.mult, ALU.add, stat[:, 0:1]))
            dve.wait_ge(sem["squares"], 1)
            inv_rms(2, D)
            for t in range(2):
                v = proj[:, t, 2792:2792 + D]
                dve.tensor_scalar(v, v, rstd[:, t:t + 1], None, ALU.mult).then_inc(sem["xs_ready"], 1)
            dve.wait_ge(sem["group_a"], 1)
            for k in range(4):
                b = group_wait("mem", k)
                dve.wait_ge(sem["group_a"], groups_emptied("A", GROUPS["mem"] + k))
                for j in range(2):
                    kt = 2 * k + j
                    ins = dve.scalar_tensor_tensor(mt_lo[:, kt, :], b[:, 256 * j:256 * j + 256], vec[:, 8 + kt:9 + kt],
                                                   mt_hi[:, kt, :].bitcast(F32), ALU.mult, ALU.subtract)
                ins.then_inc(sem["group_d"], 1)
            dve.wait_ge(sem["x_in"], 16)
            for t in (0, 2):
                step(dve.tensor_tensor_reduce(junk[:, 0:D], proj[:, t, XRES:XRES + D], proj[:, t, XRES:XRES + D],
                                              1.0, 0.0, ALU.mult, ALU.add, stat[:, 4 + t:5 + t]))
            dve.wait_ge(sem["squares"], 3)
            dve.wait_ge(sem["xs_ready"], 2)
            inv_rms(4, D, 4)
            for t in range(TT):
                v = proj[:, t, XRES:XRES + D]
                dve.tensor_scalar(v, v, rstd[:, t:t + 1], None, ALU.mult).then_inc(sem["xs_ready"], 1)
            for k in range(KT):
                b = group_wait("x", k)
                dve.wait_ge(sem["group_a"], groups_emptied("A", GROUPS["x"] + k))
                dve.scalar_tensor_tensor(xt_lo[:, k, :], b[:], vec[:, k:k + 1], xt_hi[:, k, :].bitcast(F32),
                                         ALU.mult, ALU.subtract).then_inc(sem["group_d"], 1)

            dve.wait_ge(sem["row_in"], 16 * 6)
            cosa, sina = cos1[:, :, 0:8], sin1[:, :, 0:8]
            cosb, sinb = cos1[:, :, 8:24], sin1[:, :, 8:24]
            dve.wait_ge(sem["emptied_a"], STRIP_MEM + 1)
            head_norm(kvm[:, :, 0:512].rearrange("p t (h d) -> p t h d", h=4), 4, P, rows["km"][0])
            dve.wait_ge(sem["pos_in"], 16)
            dve.wait_ge(sem["cst_in"], 16)
            step(dve.tensor_copy(pos_f[:], pos_i[:]))
            step(dve.tensor_tensor(ang[:, 0], pos_f[:].unsqueeze(2).to_broadcast([P, TT, 24]),
                                   col["inv"].unsqueeze(1).to_broadcast([P, TT, 24]), ALU.mult))
            step(dve.tensor_scalar(ang[:, 2], ang[:, 0], 1.0 / TWO_PI, ROUND, ALU.mult, ALU.add))
            step(dve.tensor_scalar(ang[:, 2], ang[:, 2], ROUND, None, ALU.subtract))
            c1 = 6.28125
            c2 = float(np.round((TWO_PI - c1) * 2 ** 20) / 2 ** 20)
            c3 = TWO_PI - c1 - c2
            for c, src in ((c1, 0), (c2, 3), (c3, 3)):
                step(dve.scalar_tensor_tensor(ang[:, 3], ang[:, 2], -float(c), ang[:, src], ALU.mult, ALU.add))
            dve.tensor_scalar(ang[:, 1], ang[:, 3], PI_LOW, -PI_LOW, ALU.min, ALU.max).then_inc(sem["sin_in"], 1)
            dve.wait_ge(sem["sin_out"], 2)
            step(dve.tensor_tensor(cos1[:], cos1[:], cos1[:], ALU.mult))
            step(dve.tensor_scalar(cos1[:], cos1[:], -2.0, 1.0, ALU.mult, ALU.add))

            def columns_in(c):
                dve.wait_ge(sem["emptied_a"], STRIP_IN1 + -(-c // IN1_W))

            def heads(c, h, d):
                return proj[:, :, c:c + h * d].rearrange("p t (h d) -> p t h d", h=h)

            columns_in(KA)
            head_norm(heads(QA, 8, 64), 8, 64, rows["qa"][0])
            columns_in(VA)
            head_norm(heads(KA, 8, 64), 8, 64, rows["ka"][0])
            step(rotate_heads(QA, 8, 64, 0, 8, cosa, sina, rot_scratch(256)))
            step(rotate_heads(KA, 8, 64, 0, 8, cosa, sina, rot_scratch(256)))
            columns_in(ZA)
            step(rotate_heads(QI, 8, 64, 0, 8, cosa, sina, rot_scratch(256)))
            step(rotate_heads(KI, 1, 64, 0, 8, cosa, sina, rot_scratch(32)))
            step(dve.tensor_scalar(wi8[:], proj[:, :, WI:WI + 8], HEADS ** -0.5, None, ALU.mult))
            dve.sem_inc(sem["ready_for_t"], 1)

            def queries_lo(name):
                for k in range(4):
                    b = group_wait(name, k)
                    dve.wait_ge(sem["group_a"], groups_emptied("A", GROUPS[name] + k))
                    for h in (2 * k, 2 * k + 1):
                        r, other = half_rows(h), half_rows(h + 1)
                        ins = dve.tensor_tensor(q_parts[other, h, :], b[r, :], q_parts[r, h, :].bitcast(F32), ALU.subtract)
                    ins.then_inc(sem["group_d"], 1)

            def keys_lo(name, k, r, dst):
                b = group_wait(name, k)
                dve.wait_ge(sem["group_a"], groups_emptied("A", GROUPS[name] + k))
                for half_ in range(2):
                    ins = dve.tensor_tensor(dst[half_rows(half_), 1], b[r, :], dst[r, 0].bitcast(F32), ALU.subtract)
                ins.then_inc(sem["group_d"], 1)

            queries_lo("iq")
            keys_lo("ik", 0, half_rows(0), ix_k)

            index = {1: allow[:, 0:256], 2: allow[:, 256:640], 3: allow[:, 640:1152]}
            for n, (i, h) in enumerate((i, h) for i in range(1, TT) for h in range(HEADS)):
                dve.wait_ge(sem["ix_relu"], n + 1)
                if h:
                    dve.wait_ge(sem["ix_acc"], n)
                w = (i + 1) * P
                dve.scalar_tensor_tensor(index[i], sc[:, n % 2, 0:w], wi8[:, i, h:h + 1],
                                         causal_mask(i) if h == 0 else index[i], ALU.mult, ALU.add)\
                   .then_inc(sem["ix_acc"], 1)
            dve.wait_ge(sem["ix_acc"], 24)
            for r in range(TOPK // 8):
                for i in range(1, TT):
                    step(dve.max(m8[:], index[i]))
                    step(dve.match_replace(index[i], m8[:], index[i], TAKEN))
            for i in range(1, TT):
                step(dve.tensor_scalar(index[i], index[i], 0.5 * TAKEN, NEG, ALU.is_gt, ALU.mult))
                step(dve.tensor_tensor(index[i], index[i], causal_mask(i), ALU.add))

            def silu(n):
                z = proj[:, :, (ZA, ZB, ZM)[n]:(ZA, ZB, ZM)[n] + S]
                dve.wait_ge(sem["z_tanh"], n + 1)
                dve.scalar_tensor_tensor(z, z_tanh[n][:] if n < 2 else z_tanh[n], 1.0, z, ALU.add, ALU.mult)\
                   .then_inc(sem["z_ready"], 1)

            silu(0)
            silu(1)
            columns_in(KR)
            for n, (c, w) in enumerate(((CQ, 384), (CKV, 256))):
                for t in range(TT):
                    v = proj[:, t, c:c + w]
                    step(dve.tensor_tensor_reduce(junk[:, 0:w], v, v, 1.0, 0.0, ALU.mult, ALU.add,
                                                  stat[:, 4 * n + t:4 * n + t + 1]))
            step(dve.tensor_scalar(stat[:, 0:4], stat[:, 0:4], 256.0 / 384.0, None, ALU.mult))
            inv_rms(8, 256)
            for n, (c, w) in enumerate(((CQ, 384), (CKV, 256))):
                v = proj[:, :, c:c + w]
                step(dve.tensor_tensor(v, v, rstd[:, 4 * n:4 * n + 4].unsqueeze(2).to_broadcast([P, TT, w]), ALU.mult))
            kr = proj[:, :, KR:KR + 32]
            s_ = junk[:, 0:P].rearrange("p (t n) -> p t n", t=TT)
            step(dve.tensor_tensor(s_, kr, kr, ALU.mult))
            step(dve.tensor_reduce(kr_sq[:], s_, AX.X, ALU.add))
            step(dve.tensor_tensor(kr, kr, rows["kb"][0][:, 64:96].unsqueeze(1).to_broadcast([P, TT, 32]), ALU.mult))
            step(rotate_heads(KR, 1, 32, 0, 16, cosb, sinb, rot_scratch(64)))
            g1, g2 = (rows["qb"][0][:, c:c + 16].unsqueeze(1).to_broadcast([P, TT, 16]) for c in (64, 80))
            for k, (z, g) in enumerate(((cosb, g1), (sinb, g2), (cosb, g2), (sinb, g1))):
                step(dve.tensor_tensor(gained[:, k], z, g, ALU.mult))
            columns_in(ZM)
            head_norm(heads(QM, 4, P), 4, P, rows["qm"][0])
            silu(2)

            def attention(stage):
                u0, u1 = STAGE_UNITS[stage]
                for s in range(u0, u1 + LAG_PV + 1):
                    u = s
                    if u < u1:
                        w = UNITS[u]
                        dve.wait_ge(sem["scores"], u + 1)
                        if u >= SC:
                            dve.wait_ge(sem["probs_t"], u - SC + 1)
                        dve.tensor_tensor_reduce(sc[:, u % SC, 0:w["n"]], bank[SCORE_BANKS[u % len(SCORE_BANKS)]][:, 0:w["n"]], w["mask"],
                                                 -w["scale"], BIG, ALU.add, ALU.min, negmax[:, u % SC:u % SC + 1])\
                           .then_inc(sem["masked"], 1)
                    u = s - LAG_COPY
                    if u0 <= u < u1 and copier(u) == "D":
                        w = UNITS[u]
                        dve.wait_ge(sem["probs_t"], u + 1)
                        if u >= 2:
                            dve.wait_ge(sem["applied"], u - 1)
                        n, r = (w["n"], P) if w["n"] >= P else (P, w["n"])
                        dve.tensor_copy(prob_t[0:r, u % 2, 0:n], bank[2 + u % 2][0:r, 0:n]).then_inc(sem["copied_d"], 1)
                    u = s - 1
                    if u0 <= u < u1:
                        dve.wait_ge(sem["exps"], u + 1)
                        dve.reciprocal(rsum[:, u % SC:u % SC + 1], sums[:, u % SC:u % SC + 1]).then_inc(sem["rsums"], 1)
                    u = s - LAG_PV
                    if u0 <= u < u1 and UNITS[u]["last"]:
                        empty(UNITS[u]["pas"])

            def empty(q):
                w = PASSES[q]
                dve.wait_ge(sem["applied"], w["last"] + 1)
                o = bank[4 + q % 2][:]
                if w["z"] is None:
                    dve.tensor_copy(w["y"], o).then_inc(sem["o_emptied"], 1)
                else:
                    dve.tensor_tensor(w["y"], o, w["z"], ALU.mult).then_inc(sem["o_emptied"], 1)

            attention("a")
            dve.sem_inc(sem["ready_for_t"], 1)
            for name, parts, v, n in (("cq", (cq_hi, cq_lo), "cq", 3), ("ckv", (ckv_hi, ckv_lo), "ckv", 2)):
                for k in range(n):
                    b = group_wait(name, k)
                    dve.wait_ge(sem["group_a"], groups_emptied("A", GROUPS[name] + k))
                    dve.scalar_tensor_tensor(parts[1][:, k, :], b[:], vec[:, VEC[v] + k:VEC[v] + k + 1],
                                             parts[0][:, k, :].bitcast(F32), ALU.mult, ALU.subtract)\
                       .then_inc(sem["group_d"], 1)
            def over_rms(k):
                dve.tensor_scalar(stat[:, 0:32], stat[:, 0:32], 1.0 / 96, EPS, ALU.mult, ALU.add).then_inc(sem["b_mean"], 1)
                dve.wait_ge(sem["b_root"], k + 1)
                r, m, z = rstd[:, 0:32], stat[:, 0:32], stat[:, 32:64]
                step(dve.reciprocal(r, r))
                step(dve.tensor_tensor(z, r, r, ALU.mult))
                step(dve.tensor_tensor(z, z, m, ALU.mult))
                step(dve.tensor_scalar(z, z, -0.5, 1.5, ALU.mult, ALU.add))
                step(dve.tensor_tensor(r, r, z, ALU.mult))
                return rstd[:, 0:32].rearrange("p (t h) -> p t h", t=TT).unsqueeze(3)

            head_stat = stat[:, 0:32].rearrange("p (t h) -> p t h", t=TT)
            dve.wait_ge(sem["b_squares"], 1)
            step(dve.tensor_reduce(head_stat, sq_q[:].rearrange("p t (h d) -> p t h d", h=8), AX.X, ALU.add))
            qb, kb = heads(QB, 8, 96), heads(KB, 8, 96)
            step(dve.tensor_tensor(qb, qb, over_rms(0).to_broadcast([P, TT, 8, 96]), ALU.mult))
            a, b = qb[:, :, :, 64:80], qb[:, :, :, 80:96]
            g = [gained[:, k].unsqueeze(2).to_broadcast([P, TT, 8, 16]) for k in range(4)]
            t = [rot_b[:, k].rearrange("p (t h n) -> p t h n", t=TT, h=8) for k in range(4)]
            dve.tensor_tensor(t[0], a, g[0], ALU.mult)
            dve.tensor_tensor(t[1], b, g[1], ALU.mult)
            dve.tensor_tensor(t[2], b, g[2], ALU.mult)
            step(dve.tensor_tensor(t[3], a, g[3], ALU.mult))
            dve.tensor_tensor(a, t[0], t[1], ALU.subtract)
            step(dve.tensor_tensor(b, t[2], t[3], ALU.add))
            dve.wait_ge(sem["b_squares"], 2)
            step(dve.tensor_reduce(head_stat, sq_k[:].rearrange("p t (h d) -> p t h d", h=8), AX.X, ALU.add))
            step(dve.tensor_tensor(head_stat, head_stat, kr_sq[:].unsqueeze(2).to_broadcast([P, TT, 8]), ALU.add))
            rk = over_rms(1)
            dve.wait_ge(sem["y_moved"], 1)
            step(dve.tensor_tensor(kb[:, :, :, 0:64], heads(KVB, 8, P)[:, :, :, 0:64], rk.to_broadcast([P, TT, 8, 64]), ALU.mult))
            step(dve.tensor_tensor(kb[:, :, :, 64:96], proj[:, :, KR:KR + 32].unsqueeze(2).to_broadcast([P, TT, 8, 32]),
                                   rk.to_broadcast([P, TT, 8, 32]), ALU.mult))
            dve.sem_inc(sem["ready_for_t"], 1)
            dve.wait_ge(sem["gain_in"], 32)
            dve.wait_ge(sem["half_set"], 1)
            for r in range(2):
                for h in range(4):
                    b = group_wait(f"b{r}", 2 * h + 1)
                    dve.tensor_scalar(k_t[0:96, h, :], b[0:96, :], nope_gain[0:96, 1:2], None, ALU.mult)\
                       .then_inc(sem["group_d"], 1)
                attention(f"b{r}")
            attention("m")

            def cols(c, m):
                return proj[:, m // 2, c + S * (m % 2):c + S * (m % 2) + S]

            def weigh(strip, first, gated, merged):
                b = strip % 2
                banks = strip_wait(0, lambda j: strip)
                dve.wait_ge(sem["emptied_a"], strips_emptied("A", strip - 2))
                for m in range(4):
                    g = cols(gated, 4 * b + m)
                    o = cols(merged, 4 * b + m) if first else g
                    ins = dve.scalar_tensor_tensor(o, g, 1.0, banks[m][:], ALU.add, ALU.mult)
                ins.then_inc(sem["emptied_d"], 1)
                dve.wait_ge(sem["emptied_d"], strips_emptied("D", strip))
                if not first:
                    for m in range(4):
                        o = cols(merged, 4 * b + m)
                        ins = dve.tensor_tensor(o, o, cols(gated, 4 * b + m), ALU.add)
                    step(ins)
                dve.sem_inc(sem["gated"], 1)

            def merged_lo(c, n, b):
                dve.sem_inc(sem["merged_in"], 1)
                for t in (2 * b, 2 * b + 1):
                    dve.wait_ge(sem["mhi"], 4 * n + t + 1)
                    dve.scalar_tensor_tensor(
                        xt_lo[:, 2 * t:2 * t + 2, :], proj[:, t, c:c + D].rearrange("p (a n) -> p a n", a=2), 0.5,
                        xt_hi[:, 2 * t:2 * t + 2, :].bitcast(F32), ALU.mult, ALU.subtract).then_inc(sem["mlo"], 1)

            def add_strip(i, s, half_of):
                banks = strip_wait(i, s)
                for t in range(TT):
                    v = proj[:, t, XRES + S * half_of:XRES + S * half_of + S]
                    ins = dve.tensor_tensor(v, v, banks[t][:], ALU.add)
                ins.then_inc(sem["emptied_d"], 1)

            def residual(n, s):
                for b in range(2):
                    banks = strip_wait(0, lambda j: s + b)
                    for t in range(TT):
                        v = proj[:, t, XRES + S * b:XRES + S * b + S]
                        dve.tensor_tensor(v, v, banks[t][:], ALU.add).then_inc(sem["x_added"], 1)
                    dve.wait_ge(sem["x_added"], 8 * n + 4 * b + 4)
                    dve.sem_inc(sem["emptied_d"], 1)

            for n, c in enumerate((YTA, YTB, YTM)):
                dve.wait_ge(sem["ys_hi"], n + 1)
                dve.tensor_tensor(ys[n % 2][1][:], proj[:, :, c:c + S], ys[n % 2][0][:].bitcast(F32), ALU.subtract)\
                   .then_inc(sem["ys_lo"], 1)
                for b in range(2):
                    weigh(STRIP_MERGE + 4 * n + 2 + b, n == 0, GATED, MERGED)
                    if n == 2:
                        merged_lo(MERGED, 0, b)
            dve.wait_ge(sem["xres_in"], 16)
            residual(0, STRIP_OUT1)

            def norm_x(n):
                dve.wait_ge(sem["squares"], 3 + 8 * n + 8)
                step(dve.tensor_tensor(stat[:, 0:4], stat[:, 0:4], stat[:, 4:8], ALU.add))
                inv_rms(4, D)

            def norm_to_xt(name, v):
                for b in range(2):
                    for t in range(TT):
                        dve.tensor_scalar(proj[:, t, S * b:S * b + S], proj[:, t, XRES + S * b:XRES + S * b + S],
                                          rstd[:, t:t + 1], None, ALU.mult).then_inc(sem["xs_ready"], 1)
                for k in range(KT):
                    b = group_wait(name, k)
                    dve.wait_ge(sem["group_a"], groups_emptied("A", GROUPS[name] + k))
                    dve.scalar_tensor_tensor(xt_lo[:, k, :], b[:], vec[:, v + k:v + k + 1], xt_hi[:, k, :].bitcast(F32),
                                             ALU.mult, ALU.subtract).then_inc(sem["group_d"], 1)

            norm_x(0)
            norm_to_xt("x2", VEC["mix"])

            def columns2_in(c):
                dve.wait_ge(sem["emptied_a"], strips_emptied("A", STRIP_IN2 - 1) + -(-c // IN2_W))

            columns2_in(KC2)
            for t in range(TT):
                v = proj[:, t, Q2:Q2 + D].rearrange("p (h d) -> p h d", h=16)
                c, s_ = (col[k][:, 32 * t:32 * t + 32].unsqueeze(1).to_broadcast([P, 16, 32]) for k in ("cos2", "sin2"))
                k = [rot_q[:, j, :].rearrange("p (h n) -> p h n", h=16) for j in range(4)]
                step(rotate(v[:, :, 0:32], v[:, :, 32:64], c, s_, k[0:2], k[2:4]))
            for k, (name, pe_col) in enumerate((("ck", VEC["pek"]), ("cv", VEC["pev"]))):
                b = group_wait(name, 0)
                for par in range(2):
                    for g in range(2):
                        r = slice(64 * par, 64 * par + 64)
                        src = b[64 * g:64 * g + 64, :].rearrange("p (n l two) -> p two l n", l=8, two=2)[:, par]
                        lo = src[:, :, 0:NCMP], src[:, :, 1:NCMP + 1]
                        for k2 in range(2):
                            c = pe_col + 8 * k2
                            ins = dve.tensor_tensor(flat[k][r, 8 * k2:8 * k2 + 8, g, :], lo[k2],
                                                    vec[r, c:c + 8].unsqueeze(2).to_broadcast([64, 8, NCMP]), ALU.add)
                ins.then_inc(sem["group_d"], 1)
                dve.wait_ge(sem["group_d"], groups_emptied("D", GROUPS[name]))
                dve.sem_inc(sem["flats"], 1)
            columns2_in(GATES2)
            cos2, sin2 = (col[k].rearrange("p (t n) -> p t n", t=TT) for k in ("cos2", "sin2"))
            for c in (KS2, KW2):
                step(rotate_heads(c, 2, 64, 0, 32, cos2, sin2, [rot_k[:, j, :] for j in range(4)]))
            dve.wait_ge(sem["tanh_out"], 1)
            step(dve.tensor_scalar(gsig[:], gsig[:], 1.0, 0.5, ALU.add, ALU.mult))
            step(dve.tensor_tensor(gsig[:, :, 0:48:3], gsig[:, :, 0:48:3],
                                   col["anyc"].unsqueeze(2).to_broadcast([P, TT, 16]), ALU.mult))
            dve.sem_inc(sem["ready_for_t"], 1)

            for k, name in enumerate(("ck", "cv")):
                b = group_wait(name + "h", 0)
                dve.tensor_copy(hid[0:62, 0, :], b[0:62, 0:256]).then_inc(sem["group_d"], 1)
                dve.wait_ge(sem["group_d"], groups_emptied("D", GROUPS[name + "h"]))
                h, s_ = hid[0:62, 0, :], hid[0:62, 1, :]
                step(dve.tensor_tensor(s_, h, h, ALU.mult))
                step(dve.tensor_scalar(s_, s_, 0.044715, 1.0, ALU.mult, ALU.add))
                dve.tensor_tensor(s_, s_, h, ALU.mult).then_inc(sem["tanh_in"], 1)
                dve.wait_ge(sem["tanh_out"], k + 2)
                dve.scalar_tensor_tensor(hid[0:62, 2 + k, :], s_, 1.0, h, ALU.add, ALU.mult).then_inc(sem["hid_in"], 1)
                dve.wait_ge(sem["hid_in"], k + 1)
            for k, name in enumerate(("kcmp", "vcmp")):
                b = group_wait(name, 0)
                dve.tensor_copy(kcv[0:NCMP, k], b[0:NCMP, 0:128].rearrange("p (g d) -> p g d", g=2)).then_inc(sem["group_d"], 1)
                dve.wait_ge(sem["group_d"], groups_emptied("D", GROUPS[name]))
            c, s_ = (col[k][0:NCMP, :].unsqueeze(1).to_broadcast([NCMP, 2, 32]) for k in ("cosc", "sinc"))
            k = [rot_c[0:NCMP, j, :].rearrange("p (g n) -> p g n", g=2) for j in range(4)]
            step(rotate(kcv[0:NCMP, 0, :, 0:32], kcv[0:NCMP, 0, :, 32:64], c, s_, k[0:2], k[2:4]))
            dve.sem_inc(sem["ready_for_t"], 1)
            for g in range(2):
                queries_lo(f"n{g}")
                for k in range(2):
                    keys_lo(f"n{g}", 4 + k, half_rows(g), k_parts[:, k])
                attention(f"n{g}")
            dve.wait_ge(sem["yn_hi"], 1)
            yn = proj[:, :, Q2:Q2 + D]
            for half_ in range(2):
                ins = dve.tensor_tensor(yn_lo[:, 4 * half_:4 * half_ + 4, :], yn[:, :, S * half_:S * half_ + S],
                                        yn_hi[:, 4 * half_:4 * half_ + 4, :].bitcast(F32), ALU.subtract)
            ins.then_inc(sem["yn_lo"], 1)

            dve.wait_ge(sem["ys_hi"], 4)
            dve.tensor_tensor(projr[:, :, YS2 + S:YS2 + 2 * S], proj[:, :, U2:U2 + S],
                              projr[:, :, YS2:YS2 + S].bitcast(F32), ALU.subtract).then_inc(sem["ys_lo"], 1)
            for n in range(2):
                for b in range(2):
                    weigh(STRIP_M2 + 4 * n + 2 + b, n == 0, GATED2, MERGED2)
                    if n == 1:
                        merged_lo(MERGED2, 1, b)
            residual(1, STRIP_OUT2)
            norm_x(1)
            norm_to_xt("x3", VEC["mlp"])

            relu = proj[:, :, D:D + S]
            square = proj[:, :, D + S:D + 2 * S]

            def hidden(i, parity, f):
                dve.wait_ge(sem["emptied_a"], at(i, lambda j: strips_emptied("A", STRIP_FF - 1) + f(j) + 1))
                wait(dve, sem["h_hi"], at(i, f))
                wait(dve, sem["h_lo"], at(i, f))
                dve.tensor_tensor(square, relu, relu, ALU.mult).then_inc(sem["sq_out"], 1)
                dve.wait_ge(sem["h_hi"], at(i, lambda j: f(j) + 1))
                dve.tensor_tensor(ys[parity][1][:], square, ys[parity][0][:].bitcast(F32), ALU.subtract)\
                   .then_inc(sem["h_lo"], 1)

            def ff_step(i, parity, t):
                hidden(i, 1 - parity, lambda j: t(j) + 1)
                for b in range(2):
                    add_strip(i, lambda j: STRIP_FF + 2 + b + 3 * t(j), b)
            hidden(0, 0, lambda j: 0)
            ff_step(0, 0, lambda j: 0)
            with dve.Fori(1, 4) as i:
                ff_step(i, 1, lambda j: 2 * j - 1)
                ff_step(i, 0, lambda j: 2 * j)
            residual(2, STRIP_FF + 22)
            norm_x(2)
            dve.wait_ge(sem["fin_in"], 16)
            for t in range(TT):
                dve.scalar_tensor_tensor(proj[:, t, 0:D], proj[:, t, XRES:XRES + D], rstd[:, t:t + 1], gfin[:],
                                         ALU.mult, ALU.mult).then_inc(sem["x_out"], 1)


_INS = ["x", "mem", "positions", "g_norm", "w_in", "g_qn_a", "g_kn_a", "g_cq", "g_ckv", "w_uq", "w_ukv", "g_qn_b",
        "g_kn_b", "g_mem", "w_mem_kv", "g_qn_m", "g_kn_m", "w_branch", "w_out", "norm_mix_2", "w_in_2", "w_pool_2",
        "pool_scale_2", "pe_k_2", "pe_v_2", "w_ck1_2", "w_ck2_2", "w_cv1_2", "w_cv2_2", "w_proj_pool_2",
        "w_proj_nsa_2", "w_out_2", "norm_mlp_2", "w_ff1_2", "w_ff2_2", "norm_final_2"]


def kernel(**inputs):
    import concourse.bacc as bacc
    from concourse.bass_utils import run_bass_kernel_spmd

    nc = bacc.Bacc("TRN2", target_bir_lowering=False, num_devices=1)
    arrays, args = {}, {}
    for name in _INS:
        a = np.ascontiguousarray(inputs[name])
        arrays[f"in_{name}"] = a
        args[name] = nc.dram_tensor(f"in_{name}", a.shape, mybir.dt.from_np(a.dtype), kind="ExternalInput").ap()
    out = nc.dram_tensor("out_0", (1, S, D), F32, kind="ExternalOutput").ap()
    two_block_kernel(nc, out=out, **args)
    r = run_bass_kernel_spmd(nc, [arrays], core_ids=[0])
    return r.results[0]["out_0"]
```
